# Optimizing a Trainium2 kernel written in Bass

```python
import math
import jax, jax.numpy as jnp
from jax import lax
import numpy as np

D_MODEL = 1024
BATCH = 1
SEQ = 512
DEPTH = 2
DEC_BATCH = 8
DEC_SEQ = 4
PAST_LEN = 256
PAGE_SIZE = 128

N_MIXERS = 2
N_ATTN_LAYERS = (DEPTH + 1) // 2
N_SSD_LAYERS = DEPTH // 2
DILATED_GROUPS = ((128, 1), (512, 4), (2048, 16))
ATTN_Q_HEADS = 16
ATTN_KV_HEADS = 4
HEAD_DIM = 128
ATTN_WIDTH = ATTN_Q_HEADS * HEAD_DIM
ATTN_KV_WIDTH = ATTN_KV_HEADS * HEAD_DIM
ATTN_SPLITS = [ATTN_WIDTH] * 3 + [ATTN_KV_WIDTH] * 3 + [ATTN_KV_WIDTH] * 3 + [ATTN_WIDTH]
ATTN_IN_DIM = sum(ATTN_SPLITS)
ROPE_THETA = 10000.0
SSD_D_INNER = 2 * D_MODEL
SSD_HEAD_DIM = 64
SSD_HEADS = SSD_D_INNER // SSD_HEAD_DIM
SSD_GROUPS = 4
SSD_HEADS_PER_GROUP = SSD_HEADS // SSD_GROUPS
SSD_STATE = 128
SSD_CONV = 4
SSD_CHUNK = 128
SSD_CONV_DIM = SSD_D_INNER + 2 * SSD_GROUPS * SSD_STATE
SSD_SPLITS = [SSD_D_INNER, SSD_CONV_DIM, SSD_HEADS]
SSD_IN_DIM = sum(SSD_SPLITS)
NORM_EPS = 1e-6

kernel_name = "hybrid_dilated_swa_mamba2_decoder_step"

def split_sizes(x, sizes):
    offsets = np.cumsum(sizes)[:-1].tolist()
    return jnp.split(x, offsets, axis=-1)

def rmsnorm(x, w):
    xf = x.astype(jnp.float32)
    y = xf * lax.rsqrt(jnp.mean(xf * xf, axis=-1, keepdims=True) + NORM_EPS)
    return (y * w.astype(jnp.float32)).astype(x.dtype)

def rope(x, pos):
    half = HEAD_DIM // 2
    inv = ROPE_THETA ** (-jnp.arange(half, dtype=jnp.float32) / half)
    ang = pos.astype(jnp.float32)[:, None] * inv[None, :]
    cos = jnp.cos(ang)[None, :, None, :]
    sin = jnp.sin(ang)[None, :, None, :]
    xf = x.astype(jnp.float32)
    x1, x2 = xf[..., :half], xf[..., half:]
    return jnp.concatenate([x1 * cos - x2 * sin, x2 * cos + x1 * sin], axis=-1).astype(x.dtype)

def softmax_with_lse(s):
    m = jnp.max(s, axis=-1, keepdims=True)
    p = jnp.exp(s - m)
    den = jnp.sum(p, axis=-1, keepdims=True)
    return p / den, (m + jnp.log(den))[..., 0]

def to_strided(t, d):
    n, l = t.shape[:2]
    rest = t.shape[2:]
    t = jnp.swapaxes(t.reshape((n, l // d, d) + rest), 1, 2)
    return t.reshape((n * d, l // d) + rest)

def from_strided(t, n, d):
    m = t.shape[1]
    rest = t.shape[2:]
    t = jnp.swapaxes(t.reshape((n, d, m) + rest), 1, 2)
    return t.reshape((n, m * d) + rest)

def banded_attention(q, k, v, blk):
    n, l, hq, hd = q.shape
    hkv = k.shape[2]
    rep = hq // hkv
    pad = (-l) % blk
    lp = l + pad
    nb = lp // blk
    qb = jnp.pad(q, ((0, 0), (0, pad), (0, 0), (0, 0))).reshape(n, nb, blk, hkv, rep, hd)

    def blocks(t):
        tp = jnp.pad(t, ((0, 0), (blk, pad), (0, 0), (0, 0)))
        prev = tp[:, :lp].reshape(n, nb, blk, hkv, hd)
        cur = tp[:, blk:].reshape(n, nb, blk, hkv, hd)
        return jnp.concatenate([prev, cur], axis=2)

    kb, vb = blocks(k), blocks(v)
    qi = jnp.arange(blk)[:, None]
    kj = jnp.arange(2 * blk)[None, :]
    dist = blk + qi - kj
    band = (dist >= 0) & (dist <= blk)
    kpos = jnp.arange(nb)[:, None, None] * blk - blk + kj[None]
    mask = band[None] & (kpos >= 0)
    s = jnp.einsum('nbqgrd,nbkgd->nbgrqk', qb, kb).astype(jnp.float32) * (hd ** -0.5)
    s = jnp.where(mask[None, :, None, None], s, -jnp.inf)
    p, lse = softmax_with_lse(s)
    o = jnp.einsum('nbgrqk,nbkgd->nbqgrd', p, vb.astype(jnp.float32))
    o = o.reshape(n, lp, hq, hd)[:, :l]
    lse = jnp.transpose(lse, (0, 1, 4, 2, 3)).reshape(n, lp, hq)[:, :l]
    return o, lse

def dilated_decode_attention(q, kc, vc, wb, dil, steps):
    n, t, hq, hd = q.shape
    hkv = kc.shape[2]
    rep = hq // hkv
    idx = wb + jnp.arange(t)[:, None] - dil * jnp.arange(steps + 1)[None, :]
    valid = idx >= 0
    idx = jnp.maximum(idx, 0)
    kg = kc[:, idx]
    vg = vc[:, idx]
    qg = q.reshape(n, t, hkv, rep, hd)
    s = jnp.einsum('ntgrd,ntjgd->ntgrj', qg, kg).astype(jnp.float32) * (hd ** -0.5)
    s = jnp.where(valid[None, :, None, None, :], s, -jnp.inf)
    p, lse = softmax_with_lse(s)
    o = jnp.einsum('ntgrj,ntjgd->ntgrd', p, vg.astype(jnp.float32))
    return o.reshape(n, t, hq, hd), lse.reshape(n, t, hq)

def merge_groups(outs, lses):
    w = jax.nn.softmax(jnp.stack(lses, axis=0), axis=0)
    return jnp.sum(w[..., None] * jnp.stack(outs, axis=0), axis=0)

def attn_project(u, w_in, pos):
    n, l, _ = u.shape
    parts = split_sizes(u @ w_in, ATTN_SPLITS)
    qs = [rope(p.reshape(n, l, ATTN_Q_HEADS, HEAD_DIM), pos) for p in parts[0:3]]
    ks = [rope(p.reshape(n, l, ATTN_KV_HEADS, HEAD_DIM), pos) for p in parts[3:6]]
    vs = [p.reshape(n, l, ATTN_KV_HEADS, HEAD_DIM) for p in parts[6:9]]
    return qs, ks, vs, parts[9]

def attn_prompt(u, w_in, w_out):
    n, l, _ = u.shape
    qs, ks, vs, gate = attn_project(u, w_in, jnp.arange(l))
    outs, lses, bufs = [], [], []
    for g, (win, dil) in enumerate(DILATED_GROUPS):
        o, lse = banded_attention(to_strided(qs[g], dil), to_strided(ks[g], dil),
                                  to_strided(vs[g], dil), win // dil)
        outs.append(from_strided(o, n, dil))
        lses.append(from_strided(lse, n, dil))
        keep = min(win, l)
        bufs.append(jnp.stack([ks[g][:, l - keep:], vs[g][:, l - keep:]], axis=2))
    y = merge_groups(outs, lses).reshape(n, l, ATTN_WIDTH).astype(u.dtype)
    return (y * jax.nn.silu(gate)) @ w_out, bufs

def attn_sample(u, w_in, w_out, bufs):
    n, t, _ = u.shape
    qs, ks, vs, gate = attn_project(u, w_in, PAST_LEN + jnp.arange(t))
    outs, lses, new_bufs = [], [], []
    for g, (win, dil) in enumerate(DILATED_GROUPS):
        buf = bufs[g].astype(u.dtype)
        wb = buf.shape[1]
        kc = jnp.concatenate([buf[:, :, 0], ks[g]], axis=1)
        vc = jnp.concatenate([buf[:, :, 1], vs[g]], axis=1)
        o, lse = dilated_decode_attention(qs[g], kc, vc, wb, dil, win // dil)
        outs.append(o)
        lses.append(lse)
        keep = min(win, PAST_LEN + t)
        new_bufs.append(jnp.stack([kc[:, -keep:], vc[:, -keep:]], axis=2))
    y = merge_groups(outs, lses).reshape(n, t, ATTN_WIDTH).astype(u.dtype)
    return (y * jax.nn.silu(gate)) @ w_out, new_bufs

def causal_conv(x, prev, w, b):
    xp = jnp.concatenate([prev.astype(x.dtype), x], axis=1)
    c = x.shape[-1]
    y = lax.conv_general_dilated(xp, w.astype(x.dtype)[:, None, :], window_strides=(1,),
                                 padding='VALID', dimension_numbers=('NWC', 'WIO', 'NWC'),
                                 feature_group_count=c)
    return y + b.astype(x.dtype), xp[:, -(SSD_CONV - 1):]

def ssd_scan(x, dt, a, bm, cm, h0):
    n, l, g, e, p = x.shape
    s_dim = bm.shape[-1]
    q = min(SSD_CHUNK, l)
    pad = (-l) % q
    lp = l + pad
    c = lp // q
    f32 = jnp.float32

    def chunks(t):
        t = jnp.pad(t.astype(f32), ((0, 0), (0, pad)) + ((0, 0),) * (t.ndim - 2))
        return t.reshape((n, c, q) + t.shape[2:])

    xc, dtc, bc, cc = chunks(x), chunks(dt), chunks(bm), chunks(cm)
    dt_t = jnp.transpose(dtc, (0, 1, 3, 4, 2))
    acs = jnp.cumsum(dt_t * a.astype(f32)[None, None, :, :, None], axis=-1)
    tri = jnp.tril(jnp.ones((q, q), dtype=bool))
    seg = acs[..., :, None] - acs[..., None, :]
    decay = jnp.exp(jnp.where(tri, seg, -jnp.inf))
    cb = jnp.einsum('ncigs,ncjgs->ncgij', cc, bc)
    wts = cb[:, :, :, None] * decay * dt_t[..., None, :]
    y_diag = jnp.einsum('ncgeij,ncjgep->ncigep', wts, xc)
    decay_end = jnp.exp(acs[..., -1:] - acs) * dt_t
    states = jnp.einsum('ncjgs,ncgej,ncjgep->ncgeps', bc, decay_end, xc)
    chunk_decay = jnp.exp(acs[..., -1])

    def step(h, inp):
        dec, st = inp
        return dec[..., None, None] * h + st, h

    h_final, h_starts = lax.scan(step, h0.astype(f32),
                                 (jnp.moveaxis(chunk_decay, 1, 0), jnp.moveaxis(states, 1, 0)))
    h_starts = jnp.moveaxis(h_starts, 0, 1)
    y_off = jnp.einsum('ncigs,ncgeps,ncgei->ncigep', cc, h_starts, jnp.exp(acs))
    y = (y_diag + y_off).reshape(n, lp, g, e, p)[:, :l]
    return y, h_final

def ssd_mixer(u, w_in, conv_w, conv_b, dt_bias, a_log, d_skip, norm_w, w_out, h0, conv0):
    n, l, _ = u.shape
    z, xbc, dt_raw = split_sizes(u @ w_in, SSD_SPLITS)
    xbc, conv_new = causal_conv(xbc, conv0, conv_w, conv_b)
    xbc = jax.nn.silu(xbc)
    xs, bm, cm = split_sizes(xbc, [SSD_D_INNER, SSD_GROUPS * SSD_STATE, SSD_GROUPS * SSD_STATE])
    xs = xs.reshape(n, l, SSD_GROUPS, SSD_HEADS_PER_GROUP, SSD_HEAD_DIM)
    bm = bm.reshape(n, l, SSD_GROUPS, SSD_STATE)
    cm = cm.reshape(n, l, SSD_GROUPS, SSD_STATE)
    dt = jax.nn.softplus(dt_raw.astype(jnp.float32) + dt_bias.astype(jnp.float32))
    dt = dt.reshape(n, l, SSD_GROUPS, SSD_HEADS_PER_GROUP)
    a = -jnp.exp(a_log.astype(jnp.float32)).reshape(SSD_GROUPS, SSD_HEADS_PER_GROUP)
    h0g = h0.reshape(n, SSD_GROUPS, SSD_HEADS_PER_GROUP, SSD_HEAD_DIM, SSD_STATE)
    y, h_new = ssd_scan(xs, dt, a, bm, cm, h0g)
    y = y + d_skip.astype(jnp.float32).reshape(SSD_GROUPS, SSD_HEADS_PER_GROUP, 1) * xs.astype(jnp.float32)
    y = y.reshape(n, l, SSD_D_INNER) * jax.nn.silu(z.astype(jnp.float32))
    yg = y.reshape(n, l, SSD_GROUPS, SSD_D_INNER // SSD_GROUPS)
    yg = yg * lax.rsqrt(jnp.mean(yg * yg, axis=-1, keepdims=True) + NORM_EPS)
    y = (yg.reshape(n, l, SSD_D_INNER) * norm_w.astype(jnp.float32)).astype(u.dtype)
    h_new = h_new.reshape(n, SSD_HEADS, SSD_HEAD_DIM, SSD_STATE).astype(h0.dtype)
    return y @ w_out, h_new, conv_new

def setup_inputs(seed: int = 0) -> dict:
    key = jax.random.key(seed)
    ks = jax.random.split(key, 20)
    f32 = jnp.float32

    def nrm(k, shape, scale):
        return scale * jax.random.normal(k, shape, f32)

    def kv_shape(win, batch, past):
        return (N_ATTN_LAYERS, batch, min(win, past), 2, ATTN_KV_HEADS, HEAD_DIM)

    dt0 = jnp.exp(jax.random.uniform(ks[15], (N_SSD_LAYERS, SSD_HEADS), f32,
                                     math.log(1e-3), math.log(1e-1)))
    return {
        "x_prompt": nrm(ks[0], (BATCH, SEQ, D_MODEL), 1.0),
        "x_sample": nrm(ks[1], (DEC_BATCH, DEC_SEQ, D_MODEL), 1.0),
        "cache_kv_w128": nrm(ks[2], kv_shape(DILATED_GROUPS[0][0], DEC_BATCH, PAST_LEN), 1.0),
        "cache_kv_w512": nrm(ks[3], kv_shape(DILATED_GROUPS[1][0], DEC_BATCH, PAST_LEN), 1.0),
        "cache_kv_w2048": nrm(ks[4], kv_shape(DILATED_GROUPS[2][0], DEC_BATCH, PAST_LEN), 1.0),
        "state_ssm": nrm(ks[5], (N_SSD_LAYERS, DEC_BATCH, SSD_HEADS, SSD_HEAD_DIM, SSD_STATE), 0.1),
        "state_conv": nrm(ks[6], (N_SSD_LAYERS, DEC_BATCH, SSD_CONV - 1, SSD_CONV_DIM), 1.0),
        "norm_pre": 1.0 + nrm(ks[7], (DEPTH, D_MODEL), 0.05),
        "norm_post": 1.0 + nrm(ks[8], (DEPTH, D_MODEL), 0.05),
        "attn_w_in": nrm(ks[9], (N_ATTN_LAYERS, D_MODEL, ATTN_IN_DIM), D_MODEL ** -0.5),
        "attn_w_out": nrm(ks[10], (N_ATTN_LAYERS, ATTN_WIDTH, D_MODEL), ATTN_WIDTH ** -0.5),
        "ssd_w_in": nrm(ks[11], (N_SSD_LAYERS, D_MODEL, SSD_IN_DIM), D_MODEL ** -0.5),
        "ssd_conv_w": nrm(ks[12], (N_SSD_LAYERS, SSD_CONV, SSD_CONV_DIM), SSD_CONV ** -0.5),
        "ssd_conv_b": nrm(ks[13], (N_SSD_LAYERS, SSD_CONV_DIM), 0.02),
        "ssd_dt_bias": dt0 + jnp.log(-jnp.expm1(-dt0)),
        "ssd_a_log": jnp.log(jax.random.uniform(ks[14], (N_SSD_LAYERS, SSD_HEADS), f32, 1.0, 16.0)),
        "ssd_d": 1.0 + nrm(ks[16], (N_SSD_LAYERS, SSD_HEADS), 0.1),
        "ssd_norm_w": 1.0 + nrm(ks[17], (N_SSD_LAYERS, SSD_D_INNER), 0.05),
        "ssd_w_out": nrm(ks[18], (N_SSD_LAYERS, SSD_D_INNER, D_MODEL), SSD_D_INNER ** -0.5),
    }

def reference(x_prompt, x_sample, cache_kv_w128, cache_kv_w512, cache_kv_w2048, state_ssm, state_conv,
              norm_pre, norm_post, attn_w_in, attn_w_out, ssd_w_in, ssd_conv_w, ssd_conv_b,
              ssd_dt_bias, ssd_a_log, ssd_d, ssd_norm_w, ssd_w_out):
    hp, hs = x_prompt, x_sample
    p_kv, s_kv = [[], [], []], [[], [], []]
    p_ssm, p_conv, s_ssm, s_conv = [], [], [], []
    for i in range(DEPTH):
        j = i // N_MIXERS
        up = rmsnorm(hp, norm_pre[i])
        us = rmsnorm(hs, norm_pre[i])
        if i % N_MIXERS == 0:
            yp, bufs_p = attn_prompt(up, attn_w_in[j], attn_w_out[j])
            ys, bufs_s = attn_sample(us, attn_w_in[j], attn_w_out[j],
                                     [cache_kv_w128[j], cache_kv_w512[j], cache_kv_w2048[j]])
            for g in range(len(DILATED_GROUPS)):
                p_kv[g].append(bufs_p[g])
                s_kv[g].append(bufs_s[g])
        else:
            n_p = up.shape[0]
            h0p = jnp.zeros((n_p, SSD_HEADS, SSD_HEAD_DIM, SSD_STATE), up.dtype)
            c0p = jnp.zeros((n_p, SSD_CONV - 1, SSD_CONV_DIM), up.dtype)
            yp, hp_new, cp_new = ssd_mixer(up, ssd_w_in[j], ssd_conv_w[j], ssd_conv_b[j], ssd_dt_bias[j],
                                           ssd_a_log[j], ssd_d[j], ssd_norm_w[j], ssd_w_out[j], h0p, c0p)
            ys, hs_new, cs_new = ssd_mixer(us, ssd_w_in[j], ssd_conv_w[j], ssd_conv_b[j], ssd_dt_bias[j],
                                           ssd_a_log[j], ssd_d[j], ssd_norm_w[j], ssd_w_out[j],
                                           state_ssm[j], state_conv[j])
            p_ssm.append(hp_new)
            p_conv.append(cp_new)
            s_ssm.append(hs_new)
            s_conv.append(cs_new)
        hp = hp + rmsnorm(yp, norm_post[i])
        hs = hs + rmsnorm(ys, norm_post[i])
    p_kv_w128, p_kv_w512, p_kv_w2048 = jnp.stack(p_kv[0]), jnp.stack(p_kv[1]), jnp.stack(p_kv[2])
    s_kv_w128, s_kv_w512, s_kv_w2048 = jnp.stack(s_kv[0]), jnp.stack(s_kv[1]), jnp.stack(s_kv[2])
    p_ssm_a, p_conv_a = jnp.stack(p_ssm), jnp.stack(p_conv)
    s_ssm_a, s_conv_a = jnp.stack(s_ssm), jnp.stack(s_conv)
    return (hp, hs, p_kv_w128, p_kv_w512, p_kv_w2048, p_ssm_a, p_conv_a,
            s_kv_w128, s_kv_w512, s_kv_w2048, s_ssm_a, s_conv_a)


_drawn_inputs = setup_inputs


def setup_inputs(seed=0):
    import zlib

    import numpy as np

    out = dict(_drawn_inputs(seed))
    spreads = {}
    factors = {}
    for name, (base, spread) in spreads.items():
        noise = np.random.default_rng([zlib.crc32(name.encode()), seed]).standard_normal(out[name].shape)
        drawn = base * np.exp(spread * noise) if base else spread * noise
        out[name] = __import__('jax').numpy.asarray(drawn.astype(out[name].dtype))
    for name, factor in factors.items():
        out[name] = (out[name] * factor).astype(out[name].dtype)
    return out
```

```python
from contextlib import ExitStack

import numpy as np

import concourse.bass as bass
from concourse import mybir

F32 = mybir.dt.float32
F32R = mybir.dt.float32r
ALU = mybir.AluOpType
ACT = mybir.ActivationFunctionType
AX = mybir.AxisListType.X

P = 128
D = 1024
KD = D // P
SEQ = 512
NB, NT = 8, 4
NS = NB * NT
TOK = SEQ + NS
HALF = TOK // 2
TT = SEQ // P + 1
ROWS = [P] * (TT - 1) + [NS]
PAST = 256
HD = 128
NG = 4
NH = 4
PAIR = 2
WINDOWS = ((128, 1), (512, 4), (2048, 16))
NW = len(WINDOWS)
INNER = 2048
KI = INNER // P
EPS = 1e-6
BIG = -1e30


class Mem:

    def __init__(self, nc, ctx, tag):
        self.nc, self.ctx, self.tag = nc, ctx, tag

    def sb(self, name, shape, dt=F32):
        return self.ctx.enter_context(self.nc.sbuf_tensor(f"{self.tag}_{name}", shape, dt))

    def ps(self, name, shape, dt=F32):
        return self.ctx.enter_context(self.nc.psum_tensor(f"{self.tag}_{name}", shape, dt))

    def sem(self, name):
        return self.nc.alloc_semaphore(name=f"{self.tag}_{name}")


def halves(ps, rows=P):
    return ps[0:rows, :, 0:HALF]


def two(ap):
    return ap.rearrange("p (b c) -> p b c", b=2)


def bcast_rows(ap):
    return ap.partition_broadcast(P)


def norm_phase(nc, tag, xt, ident, uhi, ulo, post, pre, src, dst):
    with ExitStack() as ctx:
        m = Mem(nc, ctx, tag)
        if post is not None:
            w_post = m.sb("w_post", [P, D])
            back = m.ps("back", [P, 2, 2, 512])
        if pre is not None:
            w_pre = m.sb("w_pre", [P, D])
            normed = m.sb("normed", [P, 2, D])
            turned = m.ps("turned", [P, 2, 2, 512])
        scaled = m.sb("scaled", [P, 2, D])
        square = m.sb("square", [P, D])
        stats = m.sb("stats", [P, TT, 6])
        w_in = m.sem("w_in")
        x_in = [m.sem(f"x_in{i}") for i in range(TT)]
        back_ready = m.sem("back_ready")
        sum1_ready = m.sem("sum1_ready")
        inv1_ready = m.sem("inv1_ready")
        rstd1_ready = m.sem("rstd1_ready")
        scaled_ready = m.sem("scaled_ready")
        h_ready = m.sem("h_ready")
        sum2_ready = m.sem("sum2_ready")
        inv2_ready = m.sem("inv2_ready")
        rstd2_ready = m.sem("rstd2_ready")
        normed_ready = m.sem("normed_ready")
        turned_ready = m.sem("turned_ready")
        hi_ready = m.sem("hi_ready")
        lo_ready = m.sem("lo_ready")
        mean_ready = m.sem("mean_ready")
        stored = m.sem("stored")
        block = ctx.enter_context(nc.Block())
        span = [slice(i * P, i * P + ROWS[i]) for i in range(TT)]

        @block.sync
        def _(sp):
            n = 0
            if post is not None:
                sp.dma_start(w_post[:, :], bcast_rows(post)).then_inc(w_in, 16)
            if pre is not None:
                sp.dma_start(w_pre[:, :], bcast_rows(pre)).then_inc(w_in, 16)
            if src is not None and post is None:
                for i in range(TT):
                    rows = src[0][span[i], :] if i < TT - 1 else src[1]
                    sp.dma_start(xt[0:ROWS[i], i, :], rows).then_inc(x_in[i], 16)
            if dst is not None:
                for i in range(TT):
                    sp.wait_ge(h_ready, i + 1)
                    rows = dst[0][span[i], :] if i < TT - 1 else dst[1]
                    sp.dma_start(rows, xt[0:ROWS[i], i, :]).then_inc(stored, 16)
                sp.wait_ge(stored, 16 * TT)

        @block.tensor
        def _(pe):
            def to_tokens(i):
                if i >= 2:
                    pe.wait_ge(scaled_ready, i - 1)
                for k in range(KD):
                    last = pe.transpose(back[0:ROWS[i], i % 2, k // 4, (k % 4) * P:(k % 4 + 1) * P],
                                        src[:, k, span[i]], ident[:, :])
                last.then_inc(back_ready, 1)

            def to_features(i):
                pe.wait_ge(normed_ready, i + 1)
                if i >= 2:
                    pe.wait_ge(lo_ready, i - 1)
                r = ROWS[i]
                for k in range(KD):
                    last = pe.transpose(turned[:, i % 2, k // 4, (k % 4) * r:(k % 4 + 1) * r],
                                        normed[0:r, i % 2, k * P:(k + 1) * P], ident[0:r, 0:r])
                last.then_inc(turned_ready, 1)

            for i in range(TT + 1):
                if post is not None and i < TT:
                    to_tokens(i)
                if pre is not None and i >= 1:
                    to_features(i - 1)

        @block.scalar
        def _(act):
            def sum_squares(i, ins, slot, signal):
                act.activation(square[0:ROWS[i], :].rearrange("p (a c) -> p a c", a=2), ins, ACT.Square,
                               accum_out=stats[0:ROWS[i], i, slot:slot + 1]).then_inc(signal, 1)

            def root(i, slot, ready, signal):
                act.wait_ge(ready, i + 1)
                act.activation(stats[0:ROWS[i], i, slot + 2:slot + 3], stats[0:ROWS[i], i, slot + 1:slot + 2],
                               ACT.Sqrt).then_inc(signal, 1)

            def split(i):
                r = ROWS[i]
                act.wait_ge(turned_ready, i + 1)
                act.activation(uhi[:, :, span[i]].rearrange("p (a k) c -> p a k c", a=2),
                               turned[:, i % 2, :, 0:4 * r].rearrange("p a (k c) -> p a k c", k=4),
                               ACT.Copy).then_inc(hi_ready, 1)

            for i in range(TT + 1):
                if i < TT and post is not None:
                    act.wait_ge(back_ready, i + 1)
                    if i:
                        act.wait_ge(sum2_ready if pre is not None else sum1_ready, i)
                    sum_squares(i, back[0:ROWS[i], i % 2], 0, sum1_ready)
                    root(i, 0, inv1_ready, rstd1_ready)
                if i < TT and pre is not None:
                    if post is not None:
                        act.wait_ge(h_ready, i + 1)
                        act.wait_ge(sum1_ready, i + 1)
                    else:
                        act.wait_ge(x_in[i], 16)
                        if i:
                            act.wait_ge(sum2_ready, i)
                    sum_squares(i, xt[0:ROWS[i], i, :].rearrange("p (a c) -> p a c", a=2), 3, sum2_ready)
                    root(i, 3, inv2_ready, rstd2_ready)
                if i >= 1 and pre is not None:
                    split(i - 1)

        @block.vector
        def _(dve):
            dve.wait_ge(w_in, 16 * ((post is not None) + (pre is not None)))
            means = 0

            def inverse(i, slot, ready, signal):
                nonlocal means
                dve.wait_ge(ready, i + 1)
                s = stats[0:ROWS[i], i, slot:slot + 1]
                inv = stats[0:ROWS[i], i, slot + 1:slot + 2]
                dve.tensor_scalar(s, s, 1.0 / D, EPS, ALU.mult, ALU.add).then_inc(mean_ready, 1)
                means += 1
                dve.wait_ge(mean_ready, means)
                dve.reciprocal(inv, s).then_inc(signal, 1)

            def rest(i):
                dve.wait_ge(hi_ready, i + 1)
                r = ROWS[i]
                dve.tensor_tensor(ulo[:, :, span[i]].rearrange("p (a k) c -> p a k c", a=2),
                                  turned[:, i % 2, :, 0:4 * r].rearrange("p a (k c) -> p a k c", k=4),
                                  uhi[:, :, span[i]].bitcast(F32).rearrange("p (a k) c -> p a k c", a=2),
                                  ALU.subtract).then_inc(lo_ready, 1)

            for i in range(TT + 1):
                if i < TT:
                    r = ROWS[i]
                    if post is not None:
                        inverse(i, 0, sum1_ready, inv1_ready)
                        dve.wait_ge(rstd1_ready, i + 1)
                        if i >= 2:
                            dve.wait_ge(h_ready, i - 1)
                        dve.scalar_tensor_tensor(
                            out=scaled[0:r, i % 2, :].rearrange("p (a c) -> p a c", a=2), in0=back[0:r, i % 2],
                            scalar=stats[0:r, i, 2:3], in1=w_post[0:r, :].rearrange("p (a c) -> p a c", a=2),
                            op0=ALU.mult, op1=ALU.mult).then_inc(scaled_ready, 1)
                        dve.wait_ge(scaled_ready, i + 1)
                        dve.tensor_tensor(xt[0:r, i, :], xt[0:r, i, :], scaled[0:r, i % 2, :],
                                          ALU.add).then_inc(h_ready, 1)
                    if pre is not None:
                        inverse(i, 3, sum2_ready, inv2_ready)
                        dve.wait_ge(rstd2_ready, i + 1)
                        if i >= 2:
                            dve.wait_ge(turned_ready, i - 1)
                        dve.scalar_tensor_tensor(out=normed[0:r, i % 2, :], in0=xt[0:r, i, :],
                                                 scalar=stats[0:r, i, 5:6], in1=w_pre[0:r, :],
                                                 op0=ALU.mult, op1=ALU.mult).then_inc(normed_ready, 1)
                if i >= 1 and pre is not None:
                    rest(i - 1)


def out_phase(nc, tag, w_out, y_dram, out_fm, xt=None, x_src=None):
    with ExitStack() as ctx:
        m = Mem(nc, ctx, tag)
        RING = 2
        YC = 2
        NY = KI // YC
        y = m.sb("y", [P, 2, YC, TOK])
        yhi = m.sb("yhi", [P, KI, TOK], F32R)
        ylo = m.sb("ylo", [P, KI, TOK], F32R)
        w = m.sb("w", [P, RING, KI * P])
        whi = m.sb("whi", [P, RING, KI * P], F32R)
        wlo = m.sb("wlo", [P, RING, KI * P], F32R)
        acc = m.ps("acc", [P, RING, 2, 512])
        w_in = [m.sem(f"w_in{r}") for r in range(RING)]
        y_in = [m.sem(f"y_in{k}") for k in range(2)]
        x_in = m.sem("x_in")
        whi_ready = m.sem("whi_ready")
        wlo_ready = m.sem("wlo_ready")
        yhi_ready = m.sem("yhi_ready")
        ylo_ready = m.sem("ylo_ready")
        acc_ready = m.sem("acc_ready")
        acc_free = m.sem("acc_free")
        block = ctx.enter_context(nc.Block())
        ROUNDS = KD // RING

        def w_tile(o):
            return w_out.rearrange("(k p) n -> p k n", p=P)[:, :, bass.ts(o, P)]

        @block.sync
        def _(sp):
            sp.dma_start(w[:, 0].rearrange("p (k n) -> p k n", k=KI), w_tile(0)).then_inc(w_in[0], 16)
            for k in range(NY):
                if k >= 2:
                    sp.wait_ge(ylo_ready, k - 1)
                sp.dma_start(y[:, k % 2], y_dram[YC * k:YC * k + YC].rearrange("k p t -> p k t")) \
                    .then_inc(y_in[k % 2], 16)
                if k == 1:
                    sp.dma_start(w[:, 1].rearrange("p (k n) -> p k n", k=KI), w_tile(1)).then_inc(w_in[1], 16)
            with sp.Fori(0, ROUNDS - 1) as i:
                for r in range(RING):
                    sp.wait_ge(wlo_ready, RING * i + r + 1)
                    sp.dma_start(w[:, r].rearrange("p (k n) -> p k n", k=KI), w_tile(RING * i + RING + r)) \
                        .then_inc(w_in[r], 16)
            if x_src is not None:
                for i in range(TT):
                    rows = x_src[0][i * P:(i + 1) * P, :] if i < TT - 1 else x_src[1]
                    sp.dma_start(xt[0:ROWS[i], i, :], rows).then_inc(x_in, 16)
                sp.wait_ge(x_in, 16 * TT)

        @block.scalar
        def _(act):
            def w_high(i, r):
                act.wait_ge(w_in[r], 16 * i + 16)
                act.activation(whi[:, r], w[:, r], ACT.Copy).then_inc(whi_ready, 1)

            def evacuate(i, r):
                act.wait_ge(acc_ready, RING * i + r + 1)
                act.activation(two(out_fm[:, bass.ds(RING * i + r, 1), :].rearrange("p o t -> p (o t)")),
                               halves(acc[:, r]), ACT.Copy).then_inc(acc_free, 1)

            w_high(0, 0)
            for k in range(NY):
                act.wait_ge(y_in[k % 2], 16 * (k // 2) + 16)
                act.activation(yhi[:, YC * k:YC * k + YC, :], y[:, k % 2], ACT.Copy).then_inc(yhi_ready, 1)
            w_high(0, 1)
            with act.Fori(0, ROUNDS - 1) as i:
                for r in range(RING):
                    act.wait_ge(acc_ready, RING * i + r + 1)
                    w_high(i + 1, r)
                    evacuate(i, r)
            for r in range(RING):
                evacuate(ROUNDS - 1, r)

        @block.vector
        def _(dve):
            def w_low(i, r):
                dve.wait_ge(whi_ready, RING * i + r + 1)
                dve.tensor_tensor(wlo[:, r], w[:, r], whi[:, r].bitcast(F32), ALU.subtract) \
                    .then_inc(wlo_ready, 1)

            w_low(0, 0)
            for k in range(NY):
                dve.wait_ge(yhi_ready, k + 1)
                dve.tensor_tensor(ylo[:, YC * k:YC * k + YC, :], y[:, k % 2],
                                  yhi[:, YC * k:YC * k + YC, :].bitcast(F32), ALU.subtract).then_inc(ylo_ready, 1)
            w_low(0, 1)
            with dve.Fori(0, ROUNDS - 1) as i:
                for r in range(RING):
                    w_low(i + 1, r)

        @block.tensor
        def _(pe):
            pe.sem_inc(acc_free, RING)
            with pe.Fori(0, ROUNDS) as i:
                for r in range(RING):
                    pe.wait_ge(wlo_ready, RING * i + r + 1)
                    pe.wait_ge(acc_free, RING * i + r + 1)
                    for k in range(KI):
                        if k % YC == 0:
                            pe.wait_ge(ylo_ready, k // YC + 1)
                        for a, b in ((whi, yhi), (whi, ylo), (wlo, yhi)):
                            for h in range(2):
                                last = pe.matmul(acc[:, r, h, 0:HALF], a[:, r, k * P:(k + 1) * P],
                                                 b[:, k, h * HALF:(h + 1) * HALF],
                                                 start=(k == 0 and a is whi and b is yhi),
                                                 stop=(k == KI - 1 and a is wlo))
                    last.then_inc(acc_ready, 1)


TILES = NW * (2 + NH) + NH
CH = (P, P, P, 64)
CW = sum(CH)
SW = CW + NW * NS
SCALE = float(HD) ** -0.5
MERGE = 9


def attn_columns(t, g):
    if t >= NW * (2 + NH):
        return 3 * INNER + 6 * NG * HD + g * (NH * HD) + (t - NW * (2 + NH)) * HD
    w, j = divmod(t, 2 + NH)
    if j == 0:
        return 3 * INNER + w * NG * HD + g * HD
    if j == 1:
        return 3 * INNER + (NW + w) * NG * HD + g * HD
    return w * INNER + g * (NH * HD) + (j - 2) * HD


def attn_kind(t):
    if t >= NW * (2 + NH):
        return "G", t - NW * (2 + NH)
    w, j = divmod(t, 2 + NH)
    return ("K", w) if j == 0 else ("V", w) if j == 1 else ("Q", w, j - 2)


ROPED = [t for t in range(TILES) if attn_kind(t)[0] in "KQ"]
UNITS = {0: [[(1, 0), (1, 1), (2, 1), (2, 2)], [(3, 2), (3, 3), (0, 0)]],
         1: [[(i, i) for i in range(4)]], 2: [[(i, i) for i in range(4)]]}
SLOT = {(0, 0): 0, (0, 1): 1, (1, 0): 2, (2, 0): 3}

ATTN_PLAN = {t: [] for t in range(TILES)}
for _w in range(NW):
    ATTN_PLAN[6 * _w + 3] += [("V", _w), ("K", _w), ("X", _w)]
    for _h in range(NH):
        ATTN_PLAN[6 * _w + 3 + _h] += [("S", _w, _h, u) for u in range(len(UNITS[_w]))]
for _i, _t in enumerate((10, 11, 13, 14)):
    ATTN_PLAN[_t] += [("KT", 0, _i)]
ATTN_PLAN[19] += [("SC", 0), ("SN", 0)] + [("KT", 1, i) for i in range(4)]
ATTN_PLAN[20] += [("PC", 0), ("PN", 0), ("OS", 0), ("SC", 1), ("SN", 1)] \
    + [("M", w) for w in range(NW)] + [("D", w) for w in range(NW)]
ATTN_PLAN[21] += [("PC", 1), ("PN", 1), ("OS", 1), ("F",)]
HEADS = [("PT", h, w, u) for h in range(NH) for w, u in SLOT]
ATTN_PLAN[21] += HEADS
ATTN_BANKED = [item for t in range(TILES) for item in ATTN_PLAN[t] if item[0] != "OS"]
NU = len(ATTN_BANKED)
assert NU % 2 == 0
SCORES = [item for item in ATTN_BANKED if item[0] == "S"]


def behind(t, what):
    return [i for i in ATTN_PLAN.get(t - 1, []) if i[0] == what]


def attention_phase(nc, uhi, ulo, ident, w_in_dram, tables, caches, y_dram, p_kv, s_kv):
    with ExitStack() as ctx:
        m = Mem(nc, ctx, "at")
        cos = m.sb("cos", [P, TOK])
        sin = m.sb("sin", [P, TOK])
        masks = m.sb("masks", [P, 3, P])
        mask_s = m.sb("mask_s", [P, 2 * SW - CW])
        w = m.sb("w", [P, PAIR, KD * P])
        whi = m.sb("whi", [P, PAIR, KD * P], F32R)
        wlo = m.sb("wlo", [P, PAIR, KD * P], F32R)
        q = m.sb("q", [P, NH, SEQ])
        qs = m.sb("qs", [P, NW, 4, NH, 8])
        k = m.sb("k", [P, SEQ])
        ks = m.sb("ks", [P, NW, NS])
        v = m.sb("v", [P, TOK])
        v_rows = m.sb("v_rows", [P, NW, 4, HD])
        k_rows = m.sb("k_rows", [P, 4, HD])
        new_rows = m.sb("new_rows", [NS, NW, 2, HD])
        straight = m.sb("straight", [P, TOK])
        crossed = m.sb("crossed", [P, TOK])
        probs = m.sb("probs", [P, NH, 4, 512])
        top = m.sb("top", [P, NW, 4, NH])
        neg_top = m.sb("neg_top", [P, NW, 4, NH])
        den = m.sb("den", [P, NW, 4, NH])
        factor = m.sb("factor", [P, NW, 4, NH])
        row_top = m.sb("row_top", [NH, NW, SEQ])
        row_den = m.sb("row_den", [NH, NW, SEQ])
        row_all = m.sb("row_all", [NH, SEQ])
        probs_t = m.sb("probs_t", [P, 2, 512])
        k_cache = m.sb("k_cache", [P, 4, 4, HD])
        v_cache = m.sb("v_cache", [P, 4, 4, HD])
        keys_t = m.sb("keys_t", [P, 4, CW])
        probs_s = m.sb("probs_s", [P, SW])
        stat_s = m.sb("stat_s", [P, 4])
        cached_t = m.sb("cached_t", [P, 4, P])
        new_t = m.sb("new_t", [NS, NW, P])
        yg = m.sb("yg", [P, NH, TOK])
        proj = m.ps("proj", [P, PAIR, 2, 512])
        small = [m.ps(f"small{b}", [P, 512]) for b in range(2)]
        out_t = [m.ps(f"out_t{b}", [P, 512]) for b in range(2)]

        held_back = m.sem("held_back")
        consts_in = m.sem("consts_in")
        w_in = [m.sem(f"w_in{r}") for r in range(PAIR)]
        whi_ready = m.sem("whi_ready")
        wlo_ready = m.sem("wlo_ready")
        proj_ready = m.sem("proj_ready")
        proj_free = [m.sem(f"proj_free{r}") for r in range(PAIR)]
        turned_ready = m.sem("turned_ready")
        qk_ready = m.sem("qk_ready")
        v_ready = m.sem("v_ready")
        small_ready = [m.sem(f"small_ready{b}") for b in range(2)]
        small_free = [m.sem(f"small_free{b}") for b in range(2)]
        masked_ready = m.sem("masked_ready")
        top_ready = m.sem("top_ready")
        neg_ready = m.sem("neg_ready")
        probs_ready = m.sem("probs_ready")
        kv_rows_ready = m.sem("kv_rows_ready")
        kv_stored = m.sem("kv_stored")
        k_cache_in = m.sem("k_cache_in")
        v_cache_in = m.sem("v_cache_in")
        keys_ready = m.sem("keys_ready")
        s_masked = m.sem("s_masked")
        s_top = m.sem("s_top")
        s_neg = m.sem("s_neg")
        s_exp = m.sem("s_exp")
        s_inv = m.sem("s_inv")
        s_probs = m.sem("s_probs")
        s_turned = m.sem("s_turned")
        s_out = m.sem("s_out")
        rows_ready = m.sem("rows_ready")
        merge = m.sem("merge")
        shift_exp = m.sem("shift_exp")
        factor_ready = m.sem("factor_ready")
        scaled_ready = m.sem("scaled_ready")
        probs_t_ready = m.sem("probs_t_ready")
        head_done = m.sem("head_done")
        silu_ready = m.sem("silu_ready")
        out_free = [m.sem(f"out_free{b}") for b in range(2)]
        yg_ready = m.sem("yg_ready")
        y_stored = m.sem("y_stored")
        caches_copied = m.sem("caches_copied")
        block = ctx.enter_context(nc.Block())

        def bank(item):
            return small[ATTN_BANKED.index(item) % 2]

        def filled(eng, g, item):
            n = ATTN_BANKED.index(item)
            eng.wait_ge(small_ready[n % 2], NU // 2 * g + n // 2 + 1)

        def last_round(eng, g):
            for b in range(2):
                eng.wait_ge(small_ready[b], NU // 2 * g)

        def freed(item):
            return small_free[ATTN_BANKED.index(item) % 2]

        def strided(ap, w_, i):
            d = WINDOWS[w_][1]
            if d == 1:
                return ap[:, i * P:(i + 1) * P]
            if d == 4:
                return ap.rearrange("p (m r) -> p r m", r=4)[:, i, :]
            return ap.rearrange("p (m r) -> p r m", r=16)[:, 4 * i:4 * i + 4, :]

        def square(ap, w_):
            return ap.rearrange("p (r m) -> p r m", r=4) if WINDOWS[w_][1] == 16 else ap

        STORES = (6, 6, 12)

        @block.sync
        def _(sp):
            def load_w(g, t, slot):
                src = w_in_dram.rearrange("(k p) n -> p k n", p=P)[:, :, bass.ds(attn_columns(t, g), P)]
                sp.dma_start(w[:, slot].rearrange("p (k n) -> p k n", k=KD), src).then_inc(w_in[slot], 16)

            def load_cache(g, s, kv, dst, signal):
                for c, (cache, rows) in enumerate(((0, slice(0, P)), (1, slice(0, P)), (1, slice(P, 2 * P)))):
                    src = caches[cache][0, 4 * s:4 * s + 4, rows, kv, bass.ds(g, 1), :]
                    sp.dma_start(dst[:, :, c, :], src.rearrange("n p g d -> p n (g d)")).then_inc(signal, 16)
                for t in range(NT):
                    src = caches[2][0, 4 * s:4 * s + 4, :, kv, bass.ds(g, 1), :] \
                        .rearrange("n (m r) g d -> r m n (g d)", r=16)[t]
                    sp.dma_start(dst[16 * t:16 * t + 16, :, 3, :], src).then_inc(signal, 16)

            def store_rows(w_, g, kv, rows):
                out = p_kv[w_][0, :, kv, bass.ds(g, 1), :]
                if w_ == 0:
                    sp.dma_start(out.rearrange("p g d -> p (g d)"), rows[:, 3, :]).then_inc(kv_stored, 16)
                elif w_ == 1:
                    sp.dma_start(out.rearrange("(p r) g d -> p r (g d)", r=4), rows).then_inc(kv_stored, 16)
                else:
                    for r in range(4):
                        sp.dma_start(out.rearrange("(m i r) g d -> r m i (g d)", i=4, r=4)[r],
                                     rows[32 * r:32 * r + 32]).then_inc(kv_stored, 16)

            def store_new(w_, g):
                keep = s_kv[w_].shape[2]
                out = s_kv[w_][0, :, keep - NT:keep, :, bass.ds(g, 1), :]
                for t in range(NT):
                    sp.dma_start(out[:, t].rearrange("n k g d -> n k (g d)"), new_rows[t:NS:NT, w_]) \
                        .then_inc(kv_stored, 16)

            sp.dma_start(cos[:, :], tables["cos"]).then_inc(consts_in, 16)
            for t in range(PAIR):
                load_w(0, t, t)
            sp.dma_start(sin[:, :], tables["sin"]).then_inc(consts_in, 16)
            sp.dma_start(masks[:, :, :], tables["masks"]).then_inc(consts_in, 16)
            sp.dma_start(mask_s[:, :], tables["mask_s"]).then_inc(consts_in, 16)
            for t in range(PAIR):
                sp.wait_ge(wlo_ready, t + 1)
                load_w(0, PAIR + t, t)
            with sp.Fori(0, NG) as g:
                for t in range(TILES):
                    sp.wait_ge(wlo_ready, TILES * g + t + PAIR + 1)
                    nxt = t + 2 * PAIR
                    load_w(g + nxt // TILES, nxt % TILES, t % PAIR)
                    if t == 0:
                        last_round(sp, g)
                        load_cache(g, 0, 0, k_cache, k_cache_in)
                        sp.wait_ge(s_out, 2 * g)
                        load_cache(g, 0, 1, v_cache, v_cache_in)
                    if t in (1, 2, 4, 5, 7, 8):
                        i, j = divmod((1, 2, 4, 5, 7, 8).index(t), 2)
                        c_rows, keep = caches[i].shape[2], s_kv[i].shape[2]
                        skip = c_rows - (keep - NT)
                        sp.dma_start(s_kv[i][0, bass.ds(2 * g + j, 1), 0:keep - NT].rearrange("n s k h d -> (n s) (k h d)"),
                                     caches[i][0, bass.ds(2 * g + j, 1), skip:].rearrange("n s k h d -> (n s) (k h d)")) \
                            .then_inc(caches_copied, 16)
                    for w_ in range(NW):
                        if t == 6 * w_ + 4:
                            sp.wait_ge(kv_rows_ready, 3 * (NW * g + w_) + 3)
                            store_rows(w_, g, 1, v_rows[:, w_])
                            store_rows(w_, g, 0, k_rows[:, :, :])
                            store_new(w_, g)
                    if t == 16:
                        filled(sp, g, ("KT", 0, 3))
                        load_cache(g, 1, 0, k_cache, k_cache_in)
                sp.wait_ge(s_out, 2 * g + 1)
                load_cache(g, 1, 1, v_cache, v_cache_in)
                sp.wait_ge(yg_ready, (NH + 4) * (g + 1))
                sp.dma_start(y_dram[bass.ds(NH * g, NH)].rearrange("h p t -> p h t"), yg[:, :, :]).then_inc(y_stored, 16)
            sp.wait_ge(y_stored, 16 * NG)
            sp.wait_ge(kv_stored, 16 * sum(STORES) * NG)
            sp.wait_ge(caches_copied, 16 * 2 * NW * NG)
            for r in range(PAIR):
                sp.wait_ge(w_in[r], 16 * (TILES * NG // PAIR + 2))

        @block.tensor
        def _(pe):
            def project(g, t):
                r = t % PAIR
                pe.wait_ge(wlo_ready, TILES * g + t + 1)
                pe.wait_ge(proj_free[r], TILES // PAIR * g + t // PAIR)
                for kk in range(KD):
                    for a, b in ((whi, uhi), (whi, ulo), (wlo, uhi)):
                        for h in range(2):
                            last = pe.matmul(proj[:, r, h, 0:HALF], a[:, r, kk * P:(kk + 1) * P],
                                             b[:, kk, h * HALF:(h + 1) * HALF],
                                             start=(kk == 0 and a is whi and b is uhi),
                                             stop=(kk == KD - 1 and a is wlo))
                last.then_inc(proj_ready, 1)

            def turn(out, ins, one):
                return pe.matmul(out, ins, one, is_transpose=True, start=True, stop=True)

            def roped(g, t):
                pe.wait_ge(qk_ready, 2 * len(ROPED) * g + 2 * ROPED.index(t) + 2)

            def small_item(g, item):
                n = ATTN_BANKED.index(item)
                b = small[n % 2]
                pe.wait_ge(small_free[n % 2], NU // 2 * g + n // 2)
                what = item[0]
                if what == "V":
                    pe.wait_ge(v_ready, NW * g + item[1] + 1)
                    for i in range(4):
                        last = turn(b[:, i * HD:(i + 1) * HD], v[:, i * P:(i + 1) * P], ident[:, :])
                elif what == "K":
                    roped(g, 6 * item[1])
                    for i in range(3 if item[1] == 0 else 0, 4):
                        last = turn(b[:, i * HD:(i + 1) * HD], k[:, i * P:(i + 1) * P], ident[:, :])
                elif what == "X":
                    turn(b[0:NS, 0:HD], ks[:, item[1], :], ident[:, :])
                    last = turn(b[0:NS, HD:2 * HD], v[:, SEQ:TOK], ident[:, :])
                elif what == "S":
                    _, w_, h, u = item
                    roped(g, 6 * w_ + 2 + h)
                    for j, (qt, kt) in enumerate(UNITS[w_][u]):
                        last = pe.matmul(b[:, j * P:(j + 1) * P], q[:, h, qt * P:(qt + 1) * P],
                                         k[:, kt * P:(kt + 1) * P], start=True, stop=True)
                elif what == "KT":
                    _, s, ni = item
                    pe.wait_ge(k_cache_in, 16 * 7 * (2 * g + s + 1))
                    for c, rows in enumerate(CH):
                        last = turn(b[:, c * P:c * P + rows], k_cache[0:rows, ni, c, :],
                                            ident[0:rows, 0:rows])
                elif what in ("SC", "SN"):
                    s = item[1]
                    roped(g, ROPED[-1])
                    pe.wait_ge(keys_ready, 8 * g + 4 * s + 4)
                    for ni in range(4):
                        pair = (4 * s + ni) // 2
                        for w_ in range(NW):
                            if what == "SC":
                                at = (0, P, 3 * P)[w_]
                                cols = (P, 2 * P, 64)[w_]
                                rhs, o = keys_t[:, ni, at:at + cols], b[32 * ni:32 * ni + 32, at:at + cols]
                            else:
                                rhs, o = ks[:, w_, :], b[32 * ni:32 * ni + 32, w_ * NS:(w_ + 1) * NS]
                            last = pe.matmul(o, qs[:, w_, pair].rearrange("p h t -> p (h t)"), rhs, start=True, stop=True)
                elif what == "M":
                    pe.wait_ge(top_ready, len(SCORES) * (g + 1))
                    for i in range(4):
                        last = turn(strided(b[0:NH, :], item[1], i), top[:, item[1], i, :], square(ident[:, :], item[1]))
                elif what == "D":
                    pe.wait_ge(probs_ready, len(SCORES) * (g + 1))
                    for i in range(4):
                        last = turn(strided(b[0:NH, :], item[1], i), den[:, item[1], i, :], square(ident[:, :], item[1]))
                elif what == "PC":
                    pe.wait_ge(s_probs, 2 * g + item[1] + 1)
                    for c, rows in enumerate(CH):
                        last = turn(b[0:rows, c * P:(c + 1) * P], probs_s[:, c * P:c * P + rows], ident[:, :])
                elif what == "PN":
                    for w_ in range(NW):
                        last = turn(b[0:NS, w_ * P:(w_ + 1) * P],
                                            probs_s[:, CW + w_ * NS:CW + (w_ + 1) * NS], ident[:, :])
                elif what == "F":
                    pe.wait_ge(merge, MERGE * g + MERGE)
                    pe.sem_inc(held_back, 1)
                    for w_ in range(NW):
                        for i in range(4):
                            at = (w_ * 4 + i) * NH
                            row = row_den[:, 2, i * P:(i + 1) * P] if w_ == 2 else strided(row_top[:, w_, :], w_, i)
                            last = turn(b[:, at:at + NH], row, ident[0:NH, 0:NH])
                elif what == "PT":
                    _, h, w_, u = item
                    pe.wait_ge(scaled_ready, len(HEADS) * g + HEADS.index(item) + 1)
                    for j in range(len(UNITS[w_][u])):
                        last = turn(b[:, j * P:(j + 1) * P], probs[:, h, SLOT[w_, u], j * P:(j + 1) * P],
                                            ident[:, :])
                last.then_inc(small_ready[n % 2], 1)

            def sample_out(g, s):
                pe.wait_ge(s_turned, 4 * g + 2 * s + 2)
                pe.wait_ge(v_cache_in, 16 * 7 * (2 * g + s + 1))
                pe.wait_ge(kv_rows_ready, 3 * NW * (g + 1))
                pe.wait_ge(out_free[s], 3 * g)
                for ni in range(4):
                    o = out_t[s][:, 32 * ni:32 * ni + 32]
                    for c, rows in enumerate(CH):
                        pe.matmul(o, v_cache[0:rows, ni, c, :], cached_t[0:rows, c, 32 * ni:32 * ni + 32],
                                  start=(c == 0), stop=False)
                    for w_ in range(NW):
                        last = pe.matmul(o, new_rows[:, w_, 1, :], new_t[:, w_, 32 * ni:32 * ni + 32],
                                         start=False, stop=(w_ == NW - 1))
                last.then_inc(s_out, 1)

            def weigh(g, n):
                _, h, w_, u = HEADS[n]
                pe.wait_ge(probs_t_ready, len(HEADS) * g + n + 1)
                if SLOT[w_, u] == 0:
                    pe.wait_ge(out_free[h % 2], 3 * g + 1 + h // 2)
                for j, (qt, kt) in enumerate(UNITS[w_][u]):
                    last = pe.matmul(strided(out_t[h % 2][:, :], w_, qt), v_rows[:, w_, kt, :],
                                     square(probs_t[:, n % 2, j * P:(j + 1) * P], w_),
                                     start=(SLOT[w_, u] == 0 and j == 0), stop=(SLOT[w_, u] == 3 and j == 3),
                                     skip_group_check=True)
                last.then_inc(head_done, 1)

            with pe.Fori(0, NG) as g:
                for t in range(TILES):
                    project(g, t)
                    for item in ATTN_PLAN[t]:
                        if item[0] == "OS":
                            sample_out(g, item[1])
                        else:
                            small_item(g, item)
                            if item[0] == "PT" and HEADS.index(item) >= 1:
                                weigh(g, HEADS.index(item) - 1)
                weigh(g, len(HEADS) - 1)

        @block.scalar
        def _(act):
            def w_high(g, t):
                act.wait_ge(w_in[t % PAIR], TILES // PAIR * 16 * g + 16 * (t // PAIR) + 16)
                act.activation(whi[:, t % PAIR], w[:, t % PAIR], ACT.Copy).then_inc(whi_ready, 1)

            def exps(g, item):
                _, w_, h, u = item
                n = SCORES.index(item)
                act.wait_ge(neg_ready, len(SCORES) * g + n + 1)
                blocks = UNITS[w_][u]
                for qt in dict.fromkeys(b[0] for b in blocks):
                    js = [j for j, b in enumerate(blocks) if b[0] == qt]
                    x = probs[:, h, SLOT[w_, u], js[0] * P:(js[-1] + 1) * P]
                    last = act.activation(x, x, ACT.Exp, bias=neg_top[:, w_, qt, h:h + 1], scale=SCALE,
                                          accum_out=den[:, w_, qt, h:h + 1])
                last.then_inc(probs_ready, 1)

            def copied(g, item, dst, src, signal, value):
                filled(act, g, item)
                act.activation(dst, src, ACT.Copy).then_inc(signal, 1)
                act.wait_ge(signal, value)
                act.sem_inc(freed(item), 1)

            for t in range(PAIR):
                w_high(0, t)
            with act.Fori(0, NG) as g:
                for t in range(TILES):
                    act.wait_ge(proj_ready, TILES * g + t + 1)
                    nxt = t + PAIR
                    w_high(g + nxt // TILES, nxt % TILES)
                    what = attn_kind(t)
                    if what[0] == "V":
                        if what[1] == 0:
                            last_round(act, g)
                        d = WINDOWS[what[1]][1]
                        order = v[:, 0:SEQ].rearrange("p (r m) -> p m r", r=d)
                        for h, (a, z) in enumerate(((0, HALF), (HALF, SEQ))):
                            act.activation(order[:, a // d:z // d, :],
                                           proj[:, t % PAIR, h, 0:z - a].rearrange("p (m r) -> p m r", r=d), ACT.Copy)
                        act.activation(v[:, SEQ:TOK], proj[:, t % PAIR, 1, SEQ - HALF:HALF], ACT.Copy).then_inc(v_ready, 1)
                        act.wait_ge(v_ready, NW * g + what[1] + 1)
                        act.sem_inc(proj_free[t % PAIR], 1)
                    if what[0] == "G":
                        if what[1] == 0:
                            act.wait_ge(y_stored, 16 * g)
                        act.activation(two(yg[:, what[1], :]), halves(proj[:, t % PAIR]), ACT.Silu) \
                            .then_inc(silu_ready, 1)
                        act.wait_ge(silu_ready, NH * g + what[1] + 1)
                        act.sem_inc(proj_free[t % PAIR], 1)
                    for item in behind(t, "S"):
                        exps(g, item)
                    for item in ATTN_PLAN[t]:
                        if item[0] == "V":
                            w_ = item[1]
                            act.wait_ge(kv_stored, 16 * (sum(STORES) * g + sum(STORES[:w_])))
                            act.wait_ge(head_done, len(HEADS) * g)
                            copied(g, item, v_rows[:, w_], bank(item)[:, :].rearrange("p (i d) -> p i d", i=4),
                                   kv_rows_ready, 3 * (NW * g + w_) + 1)
                        elif item[0] == "K":
                            w_ = item[1]
                            lo = 3 if w_ == 0 else 0
                            copied(g, item, k_rows[:, lo:4],
                                   bank(item)[:, lo * HD:4 * HD].rearrange("p (i d) -> p i d", d=HD),
                                   kv_rows_ready, 3 * (NW * g + w_) + 2)
                        elif item[0] == "X":
                            w_ = item[1]
                            act.wait_ge(s_out, 2 * g)
                            copied(g, item, new_rows[:, w_],
                                   bank(item)[0:NS, 0:2 * HD].rearrange("p (i d) -> p i d", d=HD),
                                   kv_rows_ready, 3 * (NW * g + w_) + 3)
                        elif item[0] == "KT":
                            _, s, ni = item
                            if s == 1:
                                filled(act, g, ("SC", 0))
                            copied(g, item, keys_t[:, ni, :], bank(item)[:, 0:CW], keys_ready, 8 * g + 4 * s + ni + 1)
                        elif item[0] == "SN":
                            act.wait_ge(s_neg, 2 * g + item[1] + 1)
                            act.activation(probs_s[:, :], probs_s[:, :], ACT.Exp, bias=stat_s[:, 1:2], scale=SCALE,
                                           accum_out=stat_s[:, 2:3]).then_inc(s_exp, 1)
                        elif item[0] in ("M", "D"):
                            dst = row_top if item[0] == "M" else row_den
                            copied(g, item, dst[:, item[1], :], bank(item)[0:NH, :], rows_ready,
                                   2 * NW * g + (0 if item[0] == "M" else NW) + item[1] + 1)
                        elif item[0] == "PC":
                            s = item[1]
                            b = bank(item)
                            filled(act, g, item)
                            act.wait_ge(s_out, 2 * g + s)
                            act.activation(cached_t[:, 0:3, :], b[:, 0:3 * P].rearrange("p (c q) -> p c q", c=3), ACT.Copy)
                            act.activation(cached_t[0:64, 3, :], b[0:64, 3 * P:4 * P], ACT.Copy).then_inc(s_turned, 1)
                            act.wait_ge(s_turned, 4 * g + 2 * s + 1)
                            act.sem_inc(freed(item), 1)
                        elif item[0] == "PN":
                            copied(g, item, new_t[:, :, :],
                                   bank(item)[0:NS, 0:NW * P].rearrange("p (w q) -> p w q", w=NW),
                                   s_turned, 4 * g + 2 * item[1] + 2)
                        elif item[0] == "PT":
                            n = HEADS.index(item)
                            act.wait_ge(head_done, len(HEADS) * g + max(n - 1, 0))
                            cols = len(UNITS[item[2]][item[3]]) * P
                            copied(g, item, probs_t[:, n % 2, 0:cols], bank(item)[:, 0:cols], probs_t_ready,
                                   len(HEADS) * g + n + 1)
                    if t == 20:
                        act.wait_ge(merge, MERGE * g + 3)
                        act.activation(row_top[:, :, :], row_top[:, :, :], ACT.Exp, scale=SCALE).then_inc(shift_exp, 1)

        @block.vector
        def _(dve):
            dve.wait_ge(consts_in, 64)

            def rotate(g, t):
                n = ROPED.index(t)
                r = t % PAIR
                x = proj[:, r]
                dve.wait_ge(qk_ready, 2 * len(ROPED) * g + 2 * n)
                dve.tensor_tensor(two(straight[:, :]), halves(x), two(cos[:, :]), ALU.mult).then_inc(turned_ready, 1)
                dve.tensor_tensor(two(crossed[0:64, :]), x[64:P, :, 0:HALF], two(sin[64:P, :]), ALU.mult) \
                    .then_inc(turned_ready, 1)
                dve.tensor_tensor(two(crossed[64:P, :]), x[0:64, :, 0:HALF], two(sin[0:64, :]), ALU.mult) \
                    .then_inc(turned_ready, 1)
                dve.wait_ge(turned_ready, 3 * len(ROPED) * g + 3 * n + 3)
                dve.sem_inc(proj_free[r], 1)

            def blocks(ap, n):
                return ap.rearrange("p (j c) -> p j c", j=n)

            def mask_and_top(g, item):
                _, w_, h, u = item
                n = len(SCORES) * g + SCORES.index(item)
                b = bank(item)
                filled(dve, g, item)
                dst = probs[:, h, SLOT[w_, u], :]
                if w_ == 0:
                    c = 2 if u == 0 else 1
                    band = masks[:, 0:2, :].rearrange("p a c -> p (a c)")
                    last = dve.tensor_tensor(blocks(dst[:, 0:256 * c], c), blocks(b[:, 0:256 * c], c),
                                             band.unsqueeze(1).broadcast_to([P, c, 256]), ALU.add)
                    if u == 1:
                        last = dve.tensor_tensor(dst[:, 256:384], b[:, 256:384], masks[:, 1, :], ALU.add)
                else:
                    last = dve.tensor_tensor(blocks(dst, 4), blocks(b[:, :], 4),
                                             masks[:, w_, :].unsqueeze(1).broadcast_to([P, 4, P]), ALU.add)
                last.then_inc(masked_ready, 1)
                dve.wait_ge(masked_ready, n + 1)
                dve.sem_inc(freed(item), 1)
                if w_ == 0:
                    tops = [(1, 3, 0, 512)] if u == 0 else [(3, 4, 0, 256), (0, 1, 256, 384)]
                else:
                    tops = [(0, 4, 0, 512)]
                for a, z, lo, hi in tops:
                    last = dve.tensor_reduce(top[:, w_, a:z, h], blocks(dst[:, lo:hi], z - a), AX, ALU.max)
                last.then_inc(top_ready, 1)
                dve.wait_ge(top_ready, n + 1)
                for a, z, _, _ in tops:
                    last = dve.tensor_scalar(neg_top[:, w_, a:z, h], top[:, w_, a:z, h], -SCALE, None, ALU.mult)
                last.then_inc(neg_ready, 1)

            def sample_top(g, s):
                filled(dve, g, ("SC", s))
                dve.tensor_tensor(probs_s[:, 0:CW], bank(("SC", s))[:, 0:CW], mask_s[:, 0:CW], ALU.add) \
                    .then_inc(s_masked, 1)
                filled(dve, g, ("SN", s))
                dve.tensor_tensor(probs_s[:, CW:SW], bank(("SN", s))[:, 0:SW - CW],
                                  mask_s[:, CW + (SW - CW) * s:CW + (SW - CW) * (s + 1)], ALU.add) \
                    .then_inc(s_masked, 1)
                dve.wait_ge(s_masked, 4 * g + 2 * s + 2)
                dve.sem_inc(freed(("SC", s)), 1)
                dve.sem_inc(freed(("SN", s)), 1)
                dve.tensor_reduce(stat_s[:, 0:1], probs_s[:, :], AX, ALU.max).then_inc(s_top, 1)
                dve.wait_ge(s_top, 2 * g + s + 1)
                dve.tensor_scalar(stat_s[:, 1:2], stat_s[:, 0:1], -SCALE, None, ALU.mult).then_inc(s_neg, 1)

            def sample_normalise(g, s):
                dve.wait_ge(s_exp, 2 * g + s + 1)
                dve.reciprocal(stat_s[:, 3:4], stat_s[:, 2:3]).then_inc(s_inv, 1)
                dve.wait_ge(s_inv, 2 * g + s + 1)
                dve.tensor_scalar(probs_s[:, :], probs_s[:, :], stat_s[:, 3:4], None, ALU.mult).then_inc(s_probs, 1)

            def sample_gate(g, s):
                dve.wait_ge(s_out, 2 * g + s + 1)
                dve.wait_ge(silu_ready, NH * (g + 1))
                for j in range(2):
                    o = out_t[s][:, 0:P].rearrange("p (i j h k t) -> p j k h i t", i=2, j=2, h=NH, k=2)[:, j, j]
                    dst = yg[:, :, SEQ + 16 * s:SEQ + 16 * s + 16].rearrange("p h (i j t) -> p j h i t", i=2, j=2)[:, j]
                    dve.tensor_tensor(dst, o, dst, ALU.mult).then_inc(yg_ready, 1)
                dve.wait_ge(yg_ready, (NH + 4) * g + 2 * s + 2)
                dve.sem_inc(out_free[s], 1)

            def merge_windows(g):
                steps = MERGE * g

                def then(ins, n):
                    ins.then_inc(merge, 1)
                    dve.wait_ge(merge, steps + n)

                dve.wait_ge(rows_ready, 2 * NW * (g + 1))
                t = row_all[:, :]
                then(dve.tensor_tensor(t, row_top[:, 0, :], row_top[:, 1, :], ALU.max), 1)
                then(dve.tensor_tensor(t, t, row_top[:, 2, :], ALU.max), 2)
                wide = row_all[:, :].unsqueeze(1).broadcast_to([NH, NW, SEQ])
                then(dve.tensor_tensor(row_top[:, :, :], row_top[:, :, :], wide, ALU.subtract), 3)
                dve.wait_ge(shift_exp, g + 1)
                then(dve.tensor_tensor(row_den[:, :, :], row_den[:, :, :], row_top[:, :, :], ALU.mult), 4)
                then(dve.tensor_tensor(t, row_den[:, 0, :], row_den[:, 1, :], ALU.add), 5)
                then(dve.tensor_tensor(t, t, row_den[:, 2, :], ALU.add), 6)
                then(dve.reciprocal(t, t), 7)
                then(dve.tensor_tensor(row_top[:, 0:2, :], row_top[:, 0:2, :], wide[:, 0:2, :], ALU.mult), 8)
                then(dve.tensor_tensor(row_den[:, 2, :].rearrange("p (r m) -> p m r", r=16),
                                       row_top[:, 2, :].rearrange("p (m r) -> p m r", r=16),
                                       t.rearrange("p (m r) -> p m r", r=16), ALU.mult), 9)

            def get_factors(g):
                filled(dve, g, ("F",))
                dve.tensor_copy(factor[:, :, :, :].rearrange("p w i h -> p (w i h)"),
                                bank(("F",))[:, 0:NW * 4 * NH]).then_inc(factor_ready, 1)
                dve.wait_ge(factor_ready, g + 1)
                dve.sem_inc(freed(("F",)), 1)

            def scale(n):
                _, h, w_, u = HEADS[n]
                dst = probs[:, h, SLOT[w_, u], :]
                if w_ == 0:
                    parts = [(1, 3, 0, 512)] if u == 0 else [(3, 4, 0, 256), (0, 1, 256, 384)]
                else:
                    parts = [(0, 4, 0, 512)]
                for a, z, lo, hi in parts:
                    x = blocks(dst[:, lo:hi], z - a)
                    f = factor[:, w_, a:z, h].unsqueeze(2).broadcast_to([P, z - a, (hi - lo) // (z - a)])
                    last = dve.tensor_tensor(x, x, f, ALU.mult)
                last.then_inc(scaled_ready, 1)

            def gate(g, h):
                dve.wait_ge(head_done, len(HEADS) * g + 4 * h + 4)
                dve.tensor_tensor(yg[:, h, 0:SEQ], yg[:, h, 0:SEQ], out_t[h % 2][:, :], ALU.mult).then_inc(yg_ready, 1)
                dve.wait_ge(yg_ready, (NH + 4) * g + 4 + h + 1)
                dve.sem_inc(out_free[h % 2], 1)

            with dve.Fori(0, NG) as g:
                for t in range(TILES):
                    if attn_kind(t)[0] in "KQ":
                        dve.wait_ge(proj_ready, TILES * g + t + 1)
                        rotate(g, t)
                    for item in ATTN_PLAN[t]:
                        if item[0] == "S":
                            mask_and_top(g, item)
                        elif item[0] == "SN":
                            if item[1] == 1:
                                filled(dve, g, ("PN", 0))
                            sample_top(g, item[1])
                    if t == 19:
                        sample_normalise(g, 0)
                    if t == 20:
                        sample_normalise(g, 1)
                        merge_windows(g)
                for s in range(2):
                    sample_gate(g, s)
                get_factors(g)
                for n in range(len(HEADS)):
                    scale(n)
                    if n % 4 == 3 and n > 4:
                        gate(g, n // 4 - 1)
                gate(g, NH - 1)

        @block.gpsimd
        def _(pool):
            def w_low(g, t):
                r = t % PAIR
                pool.wait_ge(whi_ready, TILES * g + t + 1)
                pool.tensor_tensor(wlo[:, r], w[:, r], whi[:, r].bitcast(F32), ALU.subtract).then_inc(wlo_ready, 1)

            for t in range(PAIR):
                w_low(0, t)
            with pool.Fori(0, NG) as g:
                for t in range(TILES):
                    nxt = t + PAIR
                    w_low(g + nxt // TILES, nxt % TILES)
                    what = attn_kind(t)
                    if what[0] not in "KQ":
                        continue
                    n = ROPED.index(t)
                    w_ = what[1]
                    pool.wait_ge(turned_ready, 3 * len(ROPED) * g + 3 * n + 3)
                    if t == 0:
                        last_round(pool, g)
                    elif what[0] == "K":
                        filled(pool, g, ("S", w_ - 1, NH - 1, len(UNITS[w_ - 1]) - 1))
                    elif w_:
                        filled(pool, g, ("S", w_ - 1, what[2], len(UNITS[w_ - 1]) - 1))
                    dst, new = (k[:, :], ks[:, w_, :]) if what[0] == "K" else (q[:, what[2], :], qs[:, w_, :, what[2], :])
                    d = WINDOWS[w_][1]
                    a, b = straight[:, 0:SEQ], crossed[:, 0:SEQ]
                    if d > 1:
                        dst = dst.rearrange("p (r m) -> p m r", r=d)
                        a, b = (x.rearrange("p (m r) -> p m r", r=d) for x in (a, b))
                    pool.tensor_tensor(dst, a, b, ALU.add).then_inc(qk_ready, 1)
                    a, b = straight[:, SEQ:TOK], crossed[:, SEQ:TOK]
                    if what[0] == "Q":
                        a, b = (x.rearrange("p (i t) -> p i t", i=4) for x in (a, b))
                    pool.tensor_tensor(new, a, b, ALU.add).then_inc(qk_ready, 1)


GT = 10
XBC = 6
HG = 8
PD = 64
GW = HG * PD
ST = 128
TAPS = 4
PRE = TAPS - 1
WIDE = SEQ + PRE + NB * (NT + PRE)
COMP = WIDE - PRE
PAR = NB * PRE + TAPS + 1
TAIL = PRE + NB * PRE


B_AT, C_AT, X_AT = 0, 4, (1, 2, 3, 5)
RUNS = ((B_AT, 1), (X_AT[0], 3), (C_AT, 1), (X_AT[3], 1))


def ssd_columns(t, e):
    if t == B_AT:
        return 2 * INNER + e * ST
    if t == C_AT:
        return 2 * INNER + NG * ST + e * ST
    if t < XBC:
        return INNER + e * GW + X_AT.index(t) * P
    return e * GW + (t - XBC) * P


def channel(t, e):
    return ssd_columns(t, e) - INNER


SSD_PLAN = {t: [] for t in range(-1, GT)}
SSD_PLAN[-1] += [("PAR",), ("AC",), ("AT",), ("AS",)]
SSD_PLAN[2] += [("BT",), ("BS",)]
SSD_PLAN[5] += [("CB",), ("CS",), ("DEC",), ("HT", 0), ("HT", 1)]
SSD_PLAN[6] += [("X", 0), ("BA", 0), ("BB", 0), ("HT", 2), ("HT", 3)]
SSD_PLAN[7] += [("TB",), ("X", 1), ("BA", 1), ("BB", 1), ("ST", 0), ("YD", 0), ("HT", 4), ("HT", 5)]
SSD_PLAN[8] += [("TX",), ("X", 2), ("BA", 2), ("BB", 2), ("YO", 1), ("ST", 1), ("YD", 1), ("HT", 6), ("HT", 7), ("OQ",)]
SSD_PLAN[9] += [("X", 3), ("BA", 3), ("BB", 3), ("YO", 2), ("ST", 2), ("YD", 2),
            ("X", 4), ("BA", 4), ("BB", 4), ("YO", 3), ("ST", 3), ("YD", 3),
            ("YO", 4), ("YD", 4), ("FS",)] + [("HN", i) for i in range(8)] \
    + [("Z", c) for c in range(TT)] + [("YT", c) for c in range(TT)]
SSD_BANKED = [i for t in SSD_PLAN for i in SSD_PLAN[t] if i != ("OQ",)]
BANKS = 3
ORDER = {item: n for n, item in enumerate(SSD_BANKED)}
SSD_CONSTS = 11
Y_STEPS = 2 * (TT - 1)
PER = [len(SSD_BANKED[b::BANKS]) for b in range(BANKS)]


def ssd_phase(nc, uhi, ulo, ident, w_in_dram, tables, params, states, y_dram, p_out, s_out_dram):
    conv_w, conv_b, dt_bias, a_log, d_skip, norm_w = params
    state_ssm, state_conv = states
    p_ssm, p_conv = p_out
    s_ssm, s_conv = s_out_dram
    with ExitStack() as ctx:
        m = Mem(nc, ctx, "sd")
        tri = m.sb("tri", [P, P])
        tri_s = m.sb("tri_s", [NS, NS])
        mask = m.sb("mask", [P, P])
        mask_s = m.sb("mask_s", [NS, NS])
        own = m.sb("own", [NS, NB])
        pick_f = m.sb("pick_f", [HG, HG * P])
        pick = m.sb("pick", [HG, HG * P], F32R)
        spread = m.sb("spread", [HG, 4, P])
        zero = m.sb("zero", [P, 1])
        rows = m.sb("rows", [P, 3, NG * HG])
        a_neg = m.sb("a_neg", [P, NG * HG])
        w = m.sb("w", [P, PAIR, KD * P])
        whi = m.sb("whi", [P, PAIR, KD * P], F32R)
        wlo = m.sb("wlo", [P, PAIR, KD * P], F32R)
        wd = m.sb("wd", [P, KD, NG * HG])
        wdhi = m.sb("wdhi", [P, KD, NG * HG], F32R)
        wdlo = m.sb("wdlo", [P, KD, NG * HG], F32R)
        dt_f = m.sb("dt_f", [NG * HG, TOK])
        dt = m.sb("dt", [P, TT, NG * HG])
        dta = m.sb("dta", [P, TT, NG * HG])
        sp_a = m.sb("sp_a", [P, TT, NG * HG])
        sp_b = m.sb("sp_b", [P, TT, NG * HG])
        sp_c = m.sb("sp_c", [P, TT, NG * HG])
        dt_e = m.sb("dt_e", [P, TT, HG])
        dta_e = m.sb("dta_e", [P, TT, HG])
        d_e = m.sb("d_e", [P, HG])
        acs = m.sb("acs", [P, TT, HG])
        acs_exp = m.sb("acs_exp", [P, TT, HG])
        acs_f = m.sb("acs_f", [HG, TOK])
        acs_hi = m.sb("acs_hi", [HG, TOK], F32R)
        acs_lo = m.sb("acs_lo", [HG, TOK], F32R)
        last_exp = m.sb("last_exp", [HG, NB])
        decay_rows = m.sb("decay_rows", [P, 4, NB])
        par_rows = m.sb("par_rows", [PAR, XBC * P])
        par = m.sb("par", [P, XBC, PAR])
        raw = m.sb("raw", [P, WIDE])
        conv = m.sb("conv", [P, 2, WIDE])
        tails = m.sb("tails", [P, XBC, TAIL])
        tail_rows = m.sb("tail_rows", [TAIL, XBC * P])
        xbc = m.sb("xbc", [P, XBC, TOK])
        z = m.sb("z", [P, 4, TOK])
        b_rows = m.sb("b_rows", [P, TT, ST])
        b_own = m.sb("b_own", [NS, NB, ST])
        cb = m.sb("cb", [P, TT, P])
        norm_row = m.sb("norm_row", [P, GW])
        x_rows = m.sb("x_rows", [P, GW])
        x_dt = m.sb("x_dt", [P, 2, GW])
        x_end = m.sb("x_end", [P, 2, GW])
        x_d = m.sb("x_d", [P, 2, GW])
        decay = m.sb("decay", [P, 2, HG, P])
        to_end = m.sb("to_end", [P, 2, HG])
        chunk_decay = m.sb("chunk_decay", [P, 2, HG])
        state = m.sb("state", [P, GW])
        state_rows = m.sb("state_rows", [P, 4, ST])
        h0 = m.sb("h0", [P, 4, NB, ST])
        h0_t = m.sb("h0_t", [P, 2, 4 * P])
        off_t = m.sb("off_t", [P, 4 * NS])
        y = m.sb("y", [P, TT, GW])
        z_rows = m.sb("z_rows", [P, 2, GW])
        square = m.sb("square", [P, GW])
        stats = m.sb("stats", [P, 3, TT])
        proj = m.ps("proj", [P, PAIR, 2, 512])
        small = [m.ps(f"small{b}", [P, 512]) for b in range(BANKS)]
        held = m.ps("held", [P, 512])

        s = m.sem
        held_back = s("held_back")
        consts_in, w_in, = s("consts_in"), [s(f"w_in{r}") for r in range(PAIR)]
        whi_ready, wlo_ready, proj_ready = s("whi_ready"), s("wlo_ready"), s("proj_ready")
        proj_free = [s(f"proj_free{r}") for r in range(PAIR)]
        small_ready = [s(f"small_ready{b}") for b in range(BANKS)]
        small_free = [s(f"small_free{b}") for b in range(BANKS)]
        setup = s("setup")
        setup_act = s("setup_act")
        setup_pe = s("setup_pe")
        par_in, h0_in, norm_in = s("par_in"), s("h0_in"), s("norm_in")
        slices_ready = s("slices_ready")
        par_ready, acs_ready, acs_exp_ready = s("par_ready"), s("acs_ready"), s("acs_exp_ready")
        acs_f_ready, acs_hi_ready, acs_lo_ready = s("acs_f_ready"), s("acs_hi_ready"), s("acs_lo_ready")
        last_exp_ready, decay_rows_ready = s("last_exp_ready"), s("decay_rows_ready")
        raw_ready, past_ready, tail_ready, raw_free = s("raw_ready"), s("past_ready"), s("tail_ready"), s("raw_free")
        tap0_ready, conv_ready, xbc_ready, z_ready = s("tap0_ready"), s("conv_ready"), s("xbc_ready"), s("z_ready")
        b_rows_ready, b_own_ready, cb_ready = s("b_rows_ready"), s("b_own_ready"), s("cb_ready")
        h0_t_ready, off_done, off_t_ready = s("h0_t_ready"), s("off_done"), s("off_t_ready")
        x_rows_ready, x_dt_ready, x_d_ready, x_end_ready = s("x_rows_ready"), s("x_dt_ready"), s("x_d_ready"), s("x_end_ready")
        seg_ready, decay_ready, chunk_decay_ready = s("seg_ready"), s("decay_ready"), s("chunk_decay_ready")
        to_end_ready, weights_ready = s("to_end_ready"), s("weights_ready")
        state_step, state_ready = s("state_step"), s("state_ready")
        y_step, y_ready = s("y_step"), s("y_ready")
        tails_ready, tails_stored = s("tails_ready"), s("tails_stored")
        final_ready, final_stored = s("final_ready"), s("final_stored")
        h0_scaled, h0_new, h0_stored = s("h0_scaled"), s("h0_new"), s("h0_stored")
        z_rows_ready, gated, squares, mean_ready, inv_ready, rstd_ready = \
            s("z_rows_ready"), s("gated"), s("squares"), s("mean_ready"), s("inv_ready"), s("rstd_ready")
        normed, out_ready, y_stored = s("normed"), s("out_ready"), s("y_stored")
        block = ctx.enter_context(nc.Block())
        span = [slice(c * P, c * P + ROWS[c]) for c in range(TT)]

        def bank(item):
            return small[ORDER[item] % BANKS]

        def filled(eng, e, item):
            n = ORDER[item]
            eng.wait_ge(small_ready[n % BANKS], PER[n % BANKS] * e + n // BANKS + 1)

        def last_round(eng, e):
            for b in range(BANKS):
                eng.wait_ge(small_ready[b], PER[b] * e)

        def hold(eng):
            eng.sem_inc(held_back, 1)

        def free(eng, item):
            eng.sem_inc(small_free[ORDER[item] % BANKS], 1)

        def heads(ap):
            return ap.rearrange("p (h d) -> p h d", h=HG)

        def per_head(ap):
            return ap.unsqueeze(2).broadcast_to([ap.shape[0], HG, PD])

        @block.sync
        def _(sp):
            def load_w(e, t, slot):
                src = w_in_dram.rearrange("(k p) n -> p k n", p=P)[:, :, bass.ds(ssd_columns(t, e), P)]
                sp.dma_start(w[:, slot].rearrange("p (k n) -> p k n", k=KD), src).then_inc(w_in[slot], 16)

            consts = ((wd[:, :, :], w_in_dram.rearrange("(k p) n -> p k n", p=P)[:, :, 2 * INNER + 2 * NG * ST:]),
                      (rows[:, 0, :], bcast_rows(dt_bias)), (rows[:, 1, :], bcast_rows(a_log)),
                      (rows[:, 2, :], bcast_rows(d_skip)),
                      (tri[:, :], tables["tri"]), (tri_s[:, :], tables["tri_s"]), (mask[:, :], tables["mask"]),
                      (mask_s[:, :], tables["mask_ss"]), (own[:, :], tables["own"]), (pick_f[:, :], tables["pick"]),
                      (spread[:, :, :], tables["spread"]))
            assert len(consts) == SSD_CONSTS
            for dst, src in consts:
                sp.dma_start(dst, src).then_inc(consts_in, 16)
            for t in range(PAIR):
                load_w(0, t, t)
            for t in range(PAIR):
                sp.wait_ge(wlo_ready, t + 1)
                load_w(0, PAIR + t, t)
            with sp.Fori(0, NG) as e:
                last_round(sp, e)
                for t, n in RUNS:
                    lo, hi, at = t * P, (t + n) * P, bass.ds(channel(t, e), n * P)
                    sp.dma_start(par_rows[0:NB * PRE, lo:hi], state_conv[0].rearrange("n k c -> (n k) c")[:, at]) \
                        .then_inc(par_in, 16)
                    sp.dma_start(par_rows[NB * PRE:NB * PRE + TAPS, lo:hi], conv_w[0][:, at]).then_inc(par_in, 16)
                    sp.dma_start(par_rows[NB * PRE + TAPS:PAR, lo:hi], conv_b[:, at]).then_inc(par_in, 16)
                sp.wait_ge(normed, TT * e)
                sp.dma_start(norm_row[:, :], norm_w[0, bass.ds(GW * e, GW)].partition_broadcast(P)).then_inc(norm_in, 16)
                sp.wait_ge(h0_stored, 16 * 4 * e)
                for j in range(4):
                    src = state_ssm[0].rearrange("n h p s -> (h p) n s")[bass.ds(GW * e + P * j, P)]
                    sp.dma_start(h0[:, j], src).then_inc(h0_in, 16)
                for t in range(GT):
                    sp.wait_ge(wlo_ready, GT * e + t + PAIR + 1)
                    nxt = t + 2 * PAIR
                    hold(sp)
                    load_w(e + nxt // GT, nxt % GT, t % PAIR)
                sp.wait_ge(tails_ready, 2 * e + 2)
                for t, n in RUNS:
                    lo, hi, at = t * P, (t + n) * P, bass.ds(channel(t, e), n * P)
                    sp.dma_start(p_conv[0, 0][:, at], tail_rows[0:PRE, lo:hi]).then_inc(tails_stored, 16)
                    sp.dma_start(s_conv[0].rearrange("n k c -> (n k) c")[:, at], tail_rows[PRE:TAIL, lo:hi]) \
                        .then_inc(tails_stored, 16)
                sp.wait_ge(final_ready, e + 1)
                sp.dma_start(p_ssm[0, 0].rearrange("h p s -> (h p) s")[bass.ds(GW * e, GW)]
                             .rearrange("(j q) s -> q j s", q=P), state_rows[:, :, :]).then_inc(final_stored, 16)
                for j in range(4):
                    sp.wait_ge(h0_new, 8 * e + 2 * j + 2)
                    sp.dma_start(s_ssm[0].rearrange("n h p s -> (h p) n s")[bass.ds(GW * e + P * j, P)], h0[:, j]) \
                        .then_inc(h0_stored, 16)
                sp.wait_ge(out_ready, TT * e + TT)
                sp.dma_start(y_dram[bass.ds(4 * e, 4)].rearrange("k p t -> p k t"), z[:, :, :]).then_inc(y_stored, 16)
            sp.wait_ge(y_stored, 16 * NG)
            sp.wait_ge(h0_stored, 16 * 4 * NG)
            sp.wait_ge(final_stored, 16 * NG)
            sp.wait_ge(tails_stored, 16 * 2 * len(RUNS) * NG)
            for r in range(PAIR):
                sp.wait_ge(w_in[r], 16 * (GT * NG // PAIR + 2))

        @block.tensor
        def _(pe):
            def turn(out, ins, one):
                return pe.matmul(out, ins, one, is_transpose=True, start=True, stop=True)

            def project(e, t):
                r = t % PAIR
                pe.wait_ge(wlo_ready, GT * e + t + 1)
                pe.wait_ge(proj_free[r], GT // PAIR * e + t // PAIR + 1)
                for kk in range(KD):
                    for a, b in ((whi, uhi), (whi, ulo), (wlo, uhi)):
                        for h in range(2):
                            last = pe.matmul(proj[:, r, h, 0:HALF], a[:, r, kk * P:(kk + 1) * P],
                                             b[:, kk, h * HALF:(h + 1) * HALF],
                                             start=(kk == 0 and a is whi and b is uhi),
                                             stop=(kk == KD - 1 and a is wlo))
                last.then_inc(proj_ready, 1)

            def item_(e, item):
                n = ORDER[item]
                b = bank(item)
                pe.wait_ge(small_free[n % BANKS], PER[n % BANKS] * e + n // BANKS)
                what = item[0]
                c = item[1] if len(item) > 1 else None
                if what == "PAR":
                    pe.wait_ge(par_in, 16 * 3 * len(RUNS) * (e + 1))
                    hold(pe)
                    for j in range(XBC):
                        last = turn(b[:, j * PAR:(j + 1) * PAR], par_rows[:, j * P:(j + 1) * P], ident[0:PAR, 0:PAR])
                elif what == "AC":
                    pe.wait_ge(slices_ready, 3 * e + 3)
                    for i in range(TT - 1):
                        last = pe.matmul(b[:, i * HG:(i + 1) * HG], tri[:, :], dta_e[:, i, :], start=True, stop=True)
                    last = pe.matmul(b[0:NS, (TT - 1) * HG:TT * HG], tri_s[:, :], dta_e[0:NS, TT - 1, :],
                                     start=True, stop=True)
                elif what == "AT":
                    for i in range(TT - 1):
                        last = pe.matmul(b[0:HG, span[i]], dta_e[:, i, :], tri[:, :], start=True, stop=True)
                elif what == "AS":
                    hold(pe)
                    last = pe.matmul(b[0:HG, 0:NS], dta_e[0:NS, TT - 1, :], tri_s[:, :], start=True, stop=True)
                elif what == "BT":
                    pe.wait_ge(xbc_ready, XBC * e + B_AT + 1)
                    for i in range(TT - 1):
                        last = turn(b[:, i * ST:(i + 1) * ST], xbc[:, B_AT, span[i]], ident[:, :])
                elif what == "BS":
                    last = turn(b[0:NS, 0:ST], xbc[:, B_AT, span[TT - 1]], ident[:, :])
                elif what == "CB":
                    pe.wait_ge(xbc_ready, XBC * e + C_AT + 1)
                    for i in range(TT - 1):
                        last = pe.matmul(b[:, i * P:(i + 1) * P], xbc[:, B_AT, span[i]], xbc[:, C_AT, span[i]],
                                         start=True, stop=True)
                elif what == "CS":
                    hold(pe)
                    last = pe.matmul(b[0:NS, 0:NS], xbc[:, B_AT, span[TT - 1]], xbc[:, C_AT, span[TT - 1]],
                                     start=True, stop=True)
                elif what == "DEC":
                    pe.wait_ge(last_exp_ready, e + 1)
                    for j in range(4):
                        last = pe.matmul(b[:, j * NB:(j + 1) * NB], spread[:, j, :], last_exp[:, :],
                                         start=True, stop=True)
                elif what == "HT":
                    pe.wait_ge(h0_in, 16 * 4 * (e + 1))
                    for i in range(4):
                        last = turn(b[:, i * P:(i + 1) * P], h0[:, c // 2, 4 * (c % 2) + i, :], ident[:, :])
                elif what == "TB":
                    pe.wait_ge(tail_ready, 2 * XBC * e + 8)
                    for j in range(4):
                        last = turn(b[0:TAIL, j * P:(j + 1) * P], tails[:, j, :], ident[:, :])
                elif what == "TX":
                    pe.wait_ge(tail_ready, 2 * XBC * e + 2 * XBC)
                    for j in range(2):
                        last = turn(b[0:TAIL, j * P:(j + 1) * P], tails[:, 4 + j, :], ident[:, :])
                elif what == "X":
                    pe.wait_ge(xbc_ready, XBC * (e + 1))
                    for j in range(4):
                        last = turn(b[0:ROWS[c], j * P:(j + 1) * P], xbc[:, X_AT[j], span[c]], ident[:, :])
                elif what in ("BA", "BB"):
                    pe.wait_ge(acs_lo_ready, e + 1)
                    r = ROWS[c]
                    for i in range(4):
                        h = i + (4 if what == "BB" else 0)
                        pe.matmul(b[0:P, i * r:(i + 1) * r], pick[:, h * P:(h + 1) * P], acs_hi[:, span[c]],
                                  start=True, stop=False)
                        last = pe.matmul(b[0:P, i * r:(i + 1) * r], pick[:, h * P:(h + 1) * P], acs_lo[:, span[c]],
                                         start=False, stop=True)
                elif what == "ST":
                    pe.wait_ge(x_end_ready, TT * e + c + 1)
                    pe.wait_ge(b_rows_ready, 2 * e + 1)
                    last = pe.matmul(b[:, :], b_rows[:, c, :], x_end[:, c % 2, :], start=True, stop=True)
                elif what == "YD":
                    pe.wait_ge(weights_ready, TT * e + c + 1)
                    pe.wait_ge(x_dt_ready, TT * e + c + 1)
                    r = ROWS[c]
                    if r < P:
                        hold(pe)
                    for h in range(HG):
                        last = pe.matmul(b[0:r, h * PD:(h + 1) * PD], decay[0:r, c % 2, h, 0:r],
                                         x_dt[0:r, c % 2, h * PD:(h + 1) * PD], start=True, stop=True)
                elif what == "YO":
                    if c < TT - 1:
                        pe.wait_ge(state_ready, 4 * e + c)
                        last = pe.matmul(b[:, :], xbc[:, C_AT, span[c]], state[:, :], start=True, stop=True)
                    else:
                        pe.wait_ge(off_t_ready, e + 1)
                        for j in range(4):
                            last = turn(b[0:NS, j * P:(j + 1) * P], off_t[:, j * NS:(j + 1) * NS], ident[:, :])
                elif what == "FS":
                    pe.wait_ge(state_ready, 4 * e + 4)
                    for j in range(4):
                        last = turn(b[:, j * P:(j + 1) * P], state[:, j * P:(j + 1) * P], ident[:, :])
                elif what == "HN":
                    pe.wait_ge(x_end_ready, TT * e + TT)
                    pe.wait_ge(b_own_ready, e + 1)
                    j, half = c // 2, c % 2
                    last = pe.matmul(b[:, :], x_end[0:NS, 0, j * P:(j + 1) * P],
                                     b_own[:, 4 * half:4 * half + 4, :].rearrange("p n s -> p (n s)"),
                                     start=True, stop=True)
                elif what == "Z":
                    pe.wait_ge(z_ready, 4 * e + 4)
                    for j in range(4):
                        last = turn(b[0:ROWS[c], j * P:(j + 1) * P], z[:, j, span[c]], ident[:, :])
                elif what == "YT":
                    pe.wait_ge(normed, TT * e + c + 1)
                    r = ROWS[c]
                    if r < P:
                        hold(pe)
                    for j in range(4):
                        last = turn(b[:, j * r:(j + 1) * r], y[0:r, c, j * P:(j + 1) * P], ident[0:r, 0:r])
                last.then_inc(small_ready[n % BANKS], 1)

            def from_old(e, i):
                pe.wait_ge(h0_t_ready, 8 * e + i + 1)
                if i == 0:
                    pe.wait_ge(off_t_ready, e)
                for n in range(4):
                    seq = 4 * (i % 2) + n
                    at = (i // 2) * NS + NT * seq
                    last = pe.matmul(held[:, at:at + NT], h0_t[:, i % 2, n * P:(n + 1) * P],
                                     xbc[:, C_AT, SEQ + NT * seq:SEQ + NT * seq + NT], start=True, stop=True)
                last.then_inc(off_done, 1)

            pe.wait_ge(setup, 2)
            for kk in range(KD):
                for a, b in ((wdhi, uhi), (wdhi, ulo), (wdlo, uhi)):
                    for h in range(2):
                        last = pe.matmul(proj[0:NG * HG, 0, h, 0:HALF], a[:, kk, :], b[:, kk, h * HALF:(h + 1) * HALF],
                                         start=(kk == 0 and a is wdhi and b is uhi), stop=(kk == KD - 1 and a is wdlo))
            last.then_inc(setup_pe, 1)
            pe.wait_ge(setup_act, 2)
            for c in range(TT):
                last = turn(proj[0:ROWS[c], 1, 0, c * NG * HG:(c + 1) * NG * HG], dt_f[:, span[c]],
                            ident[0:NG * HG, 0:NG * HG])
            last.then_inc(setup_pe, 1)
            with pe.Fori(0, NG) as e:
                for t in range(GT):
                    project(e, t)
                    for item in (SSD_PLAN[-1] if t == 0 else []) + SSD_PLAN[t]:
                        if item == ("OQ",):
                            from_old(e, 7)
                            continue
                        item_(e, item)
                        if item[0] == "HT" and item[1] >= 1:
                            from_old(e, item[1] - 1)

        @block.scalar
        def _(act):
            def w_high(e, t):
                act.wait_ge(w_in[t % PAIR], GT // PAIR * 16 * e + 16 * (t // PAIR) + 16)
                act.activation(whi[:, t % PAIR], w[:, t % PAIR], ACT.Copy).then_inc(whi_ready, 1)

            def copied(e, item, dst, src, signal, value):
                filled(act, e, item)
                act.activation(dst, src, ACT.Copy).then_inc(signal, 1)
                act.wait_ge(signal, value)
                free(act, item)

            def convolved(e, t):
                x = proj[:, t % PAIR]
                act.wait_ge(raw_free, XBC * e + t)
                act.activation(raw[:, PRE:PRE + HALF], x[:, 0, 0:HALF], ACT.Copy)
                act.activation(raw[:, PRE + HALF:PRE + SEQ], x[:, 1, 0:SEQ - HALF], ACT.Copy)
                new = raw[:, PRE + SEQ:WIDE].rearrange("p (n k) -> p n k", n=NB)[:, :, PRE:PRE + NT]
                act.activation(new, x[:, 1, SEQ - HALF:HALF].rearrange("p (n k) -> p n k", n=NB), ACT.Copy) \
                    .then_inc(raw_ready, 1)
                act.wait_ge(raw_ready, XBC * e + t + 1)
                act.sem_inc(proj_free[t % PAIR], 1)
                act.wait_ge(past_ready, XBC * e + t + 1)
                act.activation(conv[:, 0, 0:COMP], raw[:, 0:COMP], ACT.Identity, scale=par[:, t, NB * PRE:NB * PRE + 1],
                               bias=par[:, t, PAR - 1:PAR]).then_inc(tap0_ready, 1)

            def silu(e, t):
                act.wait_ge(conv_ready, 3 * (XBC * e + t) + 3)
                act.activation(xbc[:, t, 0:SEQ], conv[:, 1, 0:SEQ], ACT.Silu)
                runs = conv[:, 1, SEQ + PRE:WIDE].rearrange("p (n k) -> p n k", n=NB)
                act.activation(xbc[:, t, SEQ:TOK].rearrange("p (n k) -> p n k", n=NB), runs[:, :, 0:NT], ACT.Silu) \
                    .then_inc(xbc_ready, 1)

            act.wait_ge(consts_in, 16 * SSD_CONSTS)
            act.activation(wdhi[:, :, :], wd[:, :, :], ACT.Copy).then_inc(setup_act, 1)
            for t in range(PAIR):
                w_high(0, t)
            act.wait_ge(setup_pe, 1)
            act.activation(two(dt_f[:, :]), proj[0:NG * HG, 0, :, 0:HALF], ACT.Copy).then_inc(setup_act, 1)
            act.activation(pick[:, :], pick_f[:, :], ACT.Copy).then_inc(setup_act, 1)
            act.activation(a_neg[:, :], rows[:, 1, :], ACT.Exp).then_inc(setup_act, 1)
            act.wait_ge(setup, 7)
            act.activation(sp_b[:, :, :], sp_b[:, :, :], ACT.Exp).then_inc(setup_act, 1)

            with act.Fori(0, NG) as e:
                for t in range(-1, GT):
                    if t >= 0:
                        act.wait_ge(proj_ready, GT * e + t + 1)
                        nxt = t + PAIR
                        w_high(e + nxt // GT, nxt % GT)
                    if 0 <= t < XBC:
                        if t == 0:
                            last_round(act, e)
                        convolved(e, t)
                        if t >= 1:
                            silu(e, t - 1)
                    if t == XBC:
                        silu(e, XBC - 1)
                    if t >= XBC:
                        if t == XBC:
                            act.wait_ge(y_stored, 16 * e)
                        act.activation(two(z[:, t - XBC, :]), halves(proj[:, t % PAIR]), ACT.Copy).then_inc(z_ready, 1)
                        act.wait_ge(z_ready, 4 * e + t - XBC + 1)
                        act.sem_inc(proj_free[t % PAIR], 1)
                    for item in SSD_PLAN[t]:
                        what = item[0]
                        c = item[1] if len(item) > 1 else None
                        b = bank(item) if what != "OQ" else None
                        if what == "PAR":
                            copied(e, item, par[:, :, :].rearrange("p t k -> p (t k)"), b[:, 0:XBC * PAR], par_ready, e + 1)
                        elif what == "AC":
                            filled(act, e, item)
                            act.activation(acs[:, 0:TT - 1, :].rearrange("p c h -> p (c h)"), b[:, 0:(TT - 1) * HG], ACT.Copy)
                            act.activation(acs[0:NS, TT - 1, :], b[0:NS, (TT - 1) * HG:TT * HG], ACT.Copy)
                            act.activation(acs_exp[:, 0:TT - 1, :].rearrange("p c h -> p (c h)"), b[:, 0:(TT - 1) * HG], ACT.Exp)
                            act.activation(acs_exp[0:NS, TT - 1, :], b[0:NS, (TT - 1) * HG:TT * HG], ACT.Exp) \
                                .then_inc(acs_ready, 1)
                            act.wait_ge(acs_ready, e + 1)
                            free(act, item)
                        elif what == "AT":
                            copied(e, item, acs_f[:, 0:SEQ], b[0:HG, :], acs_f_ready, 2 * e + 1)
                        elif what == "AS":
                            filled(act, e, item)
                            act.activation(last_exp[:, :], b[0:HG, 0:NS].rearrange("p (n t) -> p n t", t=NT)[:, :, NT - 1],
                                           ACT.Exp).then_inc(last_exp_ready, 1)
                            copied(e, item, acs_f[:, SEQ:TOK], b[0:HG, 0:NS], acs_f_ready, 2 * e + 2)
                            act.activation(acs_hi[:, :], acs_f[:, :], ACT.Copy).then_inc(acs_hi_ready, 1)
                        elif what == "BT":
                            copied(e, item, b_rows[:, 0:TT - 1, :].rearrange("p c s -> p (c s)"), b[:, :], b_rows_ready, 2 * e + 1)
                        elif what == "BS":
                            copied(e, item, b_rows[0:NS, TT - 1, :], b[0:NS, 0:ST], b_rows_ready, 2 * e + 2)
                        elif what == "CB":
                            copied(e, item, cb[:, 0:TT - 1, :].rearrange("p c i -> p (c i)"), b[:, :], cb_ready, 2 * e + 1)
                        elif what == "CS":
                            copied(e, item, cb[0:NS, TT - 1, 0:NS], b[0:NS, 0:NS], cb_ready, 2 * e + 2)
                        elif what == "DEC":
                            copied(e, item, decay_rows[:, :, :].rearrange("p j n -> p (j n)"), b[:, 0:4 * NB],
                                   decay_rows_ready, e + 1)
                        elif what == "HT":
                            if c >= 2:
                                act.wait_ge(off_done, 8 * e + c - 1)
                            copied(e, item, h0_t[:, c % 2, :], b[:, :], h0_t_ready, 8 * e + c + 1)
                        elif what == "TB":
                            act.wait_ge(tails_stored, 16 * 2 * len(RUNS) * e)
                            copied(e, item, tail_rows[:, 0:4 * P], b[0:TAIL, :], tails_ready, 2 * e + 1)
                        elif what == "TX":
                            copied(e, item, tail_rows[:, 4 * P:], b[0:TAIL, 0:2 * P], tails_ready, 2 * e + 2)
                        elif what == "X":
                            act.wait_ge(x_d_ready, TT * e + c)
                            copied(e, item, x_rows[0:ROWS[c], :], b[0:ROWS[c], :], x_rows_ready, TT * e + c + 1)
                        elif what == "BB":
                            r = ROWS[c]
                            act.wait_ge(seg_ready, TT * e + c + 1)
                            if c < TT - 1:
                                for i, it in enumerate((("BA", c), ("BB", c))):
                                    last = act.activation(chunk_decay[:, c % 2, 4 * i:4 * i + 4],
                                                          bank(it)[:, :].rearrange("p (h i) -> p h i", h=4)[:, :, P - 1],
                                                          ACT.Exp)
                                last.then_inc(chunk_decay_ready, 1)
                            act.activation(decay[0:r, c % 2, :, 0:r], decay[0:r, c % 2, :, 0:r], ACT.Exp) \
                                .then_inc(decay_ready, 1)
                        elif what == "OQ":
                            act.wait_ge(off_done, 8 * e + 8)
                            act.activation(off_t[:, :], held[:, 0:4 * NS], ACT.Copy).then_inc(off_t_ready, 1)
                        elif what == "FS":
                            act.wait_ge(final_stored, 16 * e)
                            copied(e, item, state_rows[:, :, :].rearrange("p j s -> p (j s)"), b[:, :], final_ready, e + 1)
                        elif what == "Z":
                            r = ROWS[c]
                            filled(act, e, item)
                            act.wait_ge(gated, TT * e + max(c - 1, 0))
                            act.activation(z_rows[0:r, c % 2, :], b[0:r, :], ACT.Silu).then_inc(z_rows_ready, 1)
                            act.wait_ge(z_rows_ready, TT * e + c + 1)
                            free(act, item)
                            act.wait_ge(gated, TT * e + c + 1)
                            act.wait_ge(squares, TT * e + c)
                            act.activation(square[0:r, :], y[0:r, c, :], ACT.Square, accum_out=stats[0:r, 0, c:c + 1]) \
                                .then_inc(squares, 1)
                            if c == TT - 1:
                                act.wait_ge(inv_ready, e + 1)
                                act.activation(stats[:, 2, :], stats[:, 1, :], ACT.Sqrt).then_inc(rstd_ready, 1)
                        elif what == "YT":
                            r = ROWS[c]
                            copied(e, item, z[:, :, span[c]], b[:, 0:4 * r].rearrange("p (j t) -> p j t", j=4),
                                   out_ready, TT * e + c + 1)

        @block.vector
        def _(dve):
            steps = 0

            def then(ins):
                nonlocal steps
                ins.then_inc(setup, 1)
                steps += 1
                dve.wait_ge(setup, steps)

            dve.wait_ge(consts_in, 16 * SSD_CONSTS)
            then(dve.memset(raw[:, :], 0.0))
            dve.wait_ge(setup_act, 1)
            then(dve.tensor_tensor(wdlo[:, :, :], wd[:, :, :], wdhi[:, :, :].bitcast(F32), ALU.subtract))
            dve.wait_ge(setup_pe, 2)
            n = NG * HG
            then(dve.memset(sp_a[:, :, :], 0.0))
            bias = rows[:, 0, :].unsqueeze(1).broadcast_to([P, TT - 1, n])
            dve.tensor_tensor(sp_a[:, 0:TT - 1, :], proj[:, 1, 0, 0:(TT - 1) * n].rearrange("p (c h) -> p c h", h=n),
                              bias, ALU.add)
            then(dve.tensor_tensor(sp_a[0:NS, TT - 1, :], proj[0:NS, 1, 0, (TT - 1) * n:TT * n], rows[0:NS, 0, :],
                                   ALU.add))
            dve.sem_inc(proj_free[0], 1)
            dve.sem_inc(proj_free[1], 1)
            a_, b_, c_ = (x[:, :, :] for x in (sp_a, sp_b, sp_c))
            then(dve.tensor_scalar(b_, a_, -1.0, None, ALU.mult))
            then(dve.tensor_tensor(b_, a_, b_, ALU.min))
            then(dve.tensor_scalar(a_, a_, 0.0, None, ALU.max))
            dve.wait_ge(setup_act, 5)
            then(dve.tensor_scalar(c_, b_, 2.0, None, ALU.add))
            then(dve.reciprocal(c_, c_))
            then(dve.tensor_tensor(b_, b_, c_, ALU.mult))
            then(dve.tensor_tensor(c_, b_, b_, ALU.mult))
            poly = dt[:, :, :]
            then(dve.tensor_scalar(poly, c_, 1.0 / 19, 1.0 / 17, ALU.mult, ALU.add))
            for k in (15, 13, 11, 9, 7, 5, 3, 1):
                then(dve.tensor_tensor(poly, poly, c_, ALU.mult))
                then(dve.tensor_scalar(poly, poly, 1.0 / k, None, ALU.add))
            then(dve.tensor_tensor(poly, poly, b_, ALU.mult))
            then(dve.scalar_tensor_tensor(out=poly, in0=poly, scalar=2.0, in1=a_, op0=ALU.mult, op1=ALU.add))
            dve.wait_ge(setup_act, 4)
            then(dve.tensor_scalar(a_neg[:, :], a_neg[:, :], -1.0, None, ALU.mult))
            then(dve.tensor_tensor(dta[:, :, :], poly, a_neg[:, :].unsqueeze(1).broadcast_to([P, TT, n]), ALU.mult))
            then(dve.memset(stats[:, :, :], 1.0))

            def taps(e, t):
                dve.wait_ge(tap0_ready, XBC * e + t + 1)
                dve.wait_ge(xbc_ready, XBC * e + t)
                at = 3 * (XBC * e + t)
                for k in range(1, TAPS):
                    dve.scalar_tensor_tensor(out=conv[:, k % 2, 0:COMP], in0=raw[:, k:k + COMP],
                                             scalar=par[:, t, NB * PRE + k:NB * PRE + k + 1],
                                             in1=conv[:, (k - 1) % 2, 0:COMP], op0=ALU.mult, op1=ALU.add) \
                        .then_inc(conv_ready, 1)
                    dve.wait_ge(conv_ready, at + k)
                dve.wait_ge(tail_ready, 2 * (XBC * e + t) + 2)
                dve.sem_inc(raw_free, 1)

            with dve.Fori(0, NG) as e:
                cols = bass.ds(HG * e, HG)
                last_round(dve, e)
                dve.tensor_copy(dt_e[:, :, :], dt[:, :, cols]).then_inc(slices_ready, 1)
                dve.tensor_copy(dta_e[:, :, :], dta[:, :, cols]).then_inc(slices_ready, 1)
                dve.tensor_copy(d_e[:, :], rows[:, 2, cols]).then_inc(slices_ready, 1)
                ys = 0
                for t in range(-1, GT):
                    if 0 <= t < XBC:
                        taps(e, t)
                    for item in SSD_PLAN[t]:
                        what = item[0]
                        c = item[1] if len(item) > 1 else None
                        b = bank(item) if what != "OQ" else None
                        if what == "AS":
                            dve.wait_ge(acs_hi_ready, e + 1)
                            dve.tensor_tensor(acs_lo[:, :], acs_f[:, :], acs_hi[:, :].bitcast(F32), ALU.subtract) \
                                .then_inc(acs_lo_ready, 1)
                        elif what == "BS":
                            dve.wait_ge(b_rows_ready, 2 * e + 2)
                            dve.tensor_tensor(b_own[:, :, :], b_rows[0:NS, TT - 1, :].unsqueeze(1).broadcast_to([NS, NB, ST]),
                                              own[:, :].unsqueeze(2).broadcast_to([NS, NB, ST]), ALU.mult) \
                                .then_inc(b_own_ready, 1)
                        elif what in ("BA", "BB"):
                            r = ROWS[c]
                            filled(dve, e, item)
                            dve.wait_ge(acs_ready, e + 1)
                            for i in range(4):
                                h = i + (4 if what == "BB" else 0)
                                last = dve.scalar_tensor_tensor(
                                    out=decay[0:r, c % 2, h, 0:r], in0=b[0:r, i * r:(i + 1) * r],
                                    scalar=acs[0:r, c, h:h + 1], in1=(mask if c < TT - 1 else mask_s)[0:r, 0:r],
                                    op0=ALU.subtract, op1=ALU.add)
                            if what == "BB":
                                last.then_inc(seg_ready, 1)
                                dve.wait_ge(seg_ready, TT * e + c + 1)
                                if c < TT - 1:
                                    dve.wait_ge(chunk_decay_ready, 4 * e + c + 1)
                                free(dve, ("BA", c))
                                free(dve, ("BB", c))
                                dve.wait_ge(decay_ready, TT * e + c + 1)
                                if c < TT - 1:
                                    dve.tensor_copy(to_end[:, c % 2, :], decay[:, c % 2, :, P - 1]) \
                                        .then_inc(to_end_ready, 1)
                                else:
                                    dve.tensor_reduce(to_end[0:NS, c % 2, :],
                                                      decay[0:NS, c % 2, :, NT - 1:NS:NT], AX, ALU.add) \
                                        .then_inc(to_end_ready, 1)
                                dve.wait_ge(to_end_ready, TT * e + c + 1)
                                dve.wait_ge(cb_ready, 2 * e + (1 if c < TT - 1 else 2))
                                dve.tensor_tensor(decay[0:r, c % 2, :, 0:r], decay[0:r, c % 2, :, 0:r],
                                                  cb[0:r, c, 0:r].unsqueeze(1).broadcast_to([r, HG, r]), ALU.mult) \
                                    .then_inc(weights_ready, 1)
                        elif what == "ST":
                            filled(dve, e, item)
                            if c == 0:
                                dve.tensor_copy(state[:, :], b[:, :]).then_inc(state_ready, 1)
                            else:
                                dve.wait_ge(chunk_decay_ready, 4 * e + c + 1)
                                dve.tensor_tensor(heads(state[:, :]), heads(state[:, :]),
                                                  per_head(chunk_decay[:, c % 2, :]), ALU.mult).then_inc(state_step, 1)
                                dve.wait_ge(state_step, 3 * e + c)
                                dve.tensor_tensor(state[:, :], state[:, :], b[:, :], ALU.add).then_inc(state_ready, 1)
                            dve.wait_ge(state_ready, 4 * e + c + 1)
                            free(dve, item)
                        elif what == "YO":
                            r = ROWS[c]
                            filled(dve, e, item)
                            dve.tensor_tensor(heads(y[0:r, c, :]), heads(b[0:r, :]), per_head(acs_exp[0:r, c, :]),
                                              ALU.mult).then_inc(y_step, 1)
                            ys += 1
                            dve.wait_ge(y_step, Y_STEPS * e + ys)
                            free(dve, item)
                        elif what == "YD":
                            r = ROWS[c]
                            filled(dve, e, item)
                            dve.wait_ge(x_d_ready, TT * e + c + 1)
                            if c:
                                dve.tensor_tensor(y[0:r, c, :], y[0:r, c, :], b[0:r, :], ALU.add).then_inc(y_step, 1)
                                ys += 1
                                dve.wait_ge(y_step, Y_STEPS * e + ys)
                                free(dve, item)
                                dve.tensor_tensor(y[0:r, c, :], y[0:r, c, :], x_d[0:r, c % 2, :], ALU.add) \
                                    .then_inc(y_ready, 1)
                            else:
                                dve.tensor_tensor(y[0:r, c, :], b[0:r, :], x_d[0:r, c % 2, :], ALU.add) \
                                    .then_inc(y_ready, 1)
                                dve.wait_ge(y_ready, TT * e + 1)
                                free(dve, item)
                        elif what == "HN":
                            j, half = c // 2, c % 2
                            filled(dve, e, item)
                            dve.wait_ge(h0_scaled, 8 * e + c + 1)
                            x = h0[:, j, 4 * half:4 * half + 4, :].rearrange("p n s -> p (n s)")
                            dve.tensor_tensor(x, x, b[:, :], ALU.add).then_inc(h0_new, 1)
                            dve.wait_ge(h0_new, 8 * e + c + 1)
                            free(dve, item)
                        elif what == "Z":
                            r = ROWS[c]
                            dve.wait_ge(z_rows_ready, TT * e + c + 1)
                            dve.wait_ge(y_ready, TT * e + c + 1)
                            dve.tensor_tensor(y[0:r, c, :], y[0:r, c, :], z_rows[0:r, c % 2, :], ALU.mult) \
                                .then_inc(gated, 1)
                        elif what == "YT":
                            if c == 0:
                                dve.wait_ge(squares, TT * (e + 1))
                                dve.tensor_scalar(stats[:, 1, :], stats[:, 0, :], 1.0 / GW, EPS, ALU.mult, ALU.add) \
                                    .then_inc(mean_ready, 1)
                                dve.wait_ge(mean_ready, e + 1)
                                dve.reciprocal(stats[:, 1, :], stats[:, 1, :]).then_inc(inv_ready, 1)
                                dve.wait_ge(rstd_ready, e + 1)
                                dve.wait_ge(norm_in, 16 * (e + 1))
                            r = ROWS[c]
                            dve.scalar_tensor_tensor(out=y[0:r, c, :], in0=y[0:r, c, :], scalar=stats[0:r, 2, c:c + 1],
                                                     in1=norm_row[0:r, :], op0=ALU.mult, op1=ALU.mult).then_inc(normed, 1)

        @block.gpsimd
        def _(pool):
            def w_low(e, t):
                r = t % PAIR
                pool.wait_ge(whi_ready, GT * e + t + 1)
                pool.tensor_tensor(wlo[:, r], w[:, r], whi[:, r].bitcast(F32), ALU.subtract).then_inc(wlo_ready, 1)

            for t in range(PAIR):
                w_low(0, t)
            pool.wait_ge(setup, 1)
            with pool.Fori(0, NG) as e:
                for t in range(-1, GT):
                    if t >= 0:
                        nxt = t + PAIR
                        w_low(e + nxt // GT, nxt % GT)
                    if 0 <= t < XBC:
                        pool.wait_ge(raw_ready, XBC * e + t + 1)
                        if t == 0:
                            pool.wait_ge(par_ready, e + 1)
                            pool.wait_ge(tails_ready, 2 * e)
                        hold(pool)
                        runs = raw[:, PRE + SEQ:WIDE].rearrange("p (n k) -> p n k", n=NB)
                        pool.tensor_copy(runs[:, :, 0:PRE], par[:, t, 0:NB * PRE].rearrange("p (n k) -> p n k", n=NB)) \
                            .then_inc(past_ready, 1)
                        pool.tensor_copy(tails[:, t, 0:PRE], raw[:, SEQ:SEQ + PRE]).then_inc(tail_ready, 1)
                        pool.tensor_copy(tails[:, t, PRE:TAIL].rearrange("p (n k) -> p n k", n=NB), runs[:, :, NT:NT + PRE]) \
                            .then_inc(tail_ready, 1)
                    for item in SSD_PLAN[t]:
                        if item[0] == "X":
                            c = item[1]
                            r = ROWS[c]
                            pool.wait_ge(x_rows_ready, TT * e + c + 1)
                            if c >= 2:
                                pool.wait_ge(y_ready, TT * e + c - 1)
                                filled(pool, e, ("YD", c - 2))
                            pool.tensor_tensor(heads(x_dt[0:r, c % 2, :]), heads(x_rows[0:r, :]), per_head(dt_e[0:r, c, :]),
                                               ALU.mult).then_inc(x_dt_ready, 1)
                            pool.tensor_tensor(heads(x_d[0:r, c % 2, :]), heads(x_rows[0:r, :]), per_head(d_e[0:r, :]),
                                               ALU.mult).then_inc(x_d_ready, 1)
                        elif item[0] == "BB":
                            c = item[1]
                            r = ROWS[c]
                            pool.wait_ge(x_dt_ready, TT * e + c + 1)
                            pool.wait_ge(to_end_ready, TT * e + c + 1)
                            if c >= 2:
                                filled(pool, e, ("ST", c - 2))
                            pool.tensor_tensor(heads(x_end[0:r, c % 2, :]), heads(x_dt[0:r, c % 2, :]),
                                               per_head(to_end[0:r, c % 2, :]), ALU.mult).then_inc(x_end_ready, 1)
                        elif item[0] == "HN":
                            c = item[1]
                            j, half = c // 2, c % 2
                            if c == 0:
                                pool.wait_ge(decay_rows_ready, e + 1)
                                filled(pool, e, ("HT", 7))
                            x = h0[:, j, 4 * half:4 * half + 4, :]
                            pool.tensor_tensor(x, x, decay_rows[:, j, 4 * half:4 * half + 4].unsqueeze(2)
                                               .broadcast_to([P, 4, ST]), ALU.mult).then_inc(h0_scaled, 1)


def load_phase(nc, ident, ident_dram):
    with ExitStack() as ctx:
        m = Mem(nc, ctx, "ld")
        ident_in = m.sem("ident_in")
        block = ctx.enter_context(nc.Block())

        @block.sync
        def _(sp):
            sp.dma_start(ident[:, :], ident_dram).then_inc(ident_in, 16)
            sp.wait_ge(ident_in, 16)


def build(nc, x, t, out, scratch):
    y_dram, h_dram, hs_dram = scratch
    pre, post = x["norm_pre"], x["norm_post"]
    ssd_params = (x["ssd_conv_w"], x["ssd_conv_b"], x["ssd_dt_bias"][0], x["ssd_a_log"][0], x["ssd_d"][0], x["ssd_norm_w"])
    source = (x["x_prompt"][0], x["x_sample"].rearrange("n t d -> (n t) d"))
    target = (out["y_prompt"][0], out["y_sample"].rearrange("n t d -> (n t) d"))
    windows = ("w128", "w512", "w2048")
    with nc.sbuf_tensor("ident", [P, P], F32) as ident, \
            nc.sbuf_tensor("uhi", [P, KD, TOK], F32R) as uhi, nc.sbuf_tensor("ulo", [P, KD, TOK], F32R) as ulo:
        with nc.cleanup_on_exit():
            load_phase(nc, ident, t["ident"])
            with nc.sbuf_tensor("x0", [P, TT, D], F32) as xt:
                norm_phase(nc, "n0", xt, ident, uhi, ulo, None, pre[0], source, None)
        with nc.cleanup_on_exit():
            attention_phase(nc, uhi, ulo, ident, x["attn_w_in"][0], t, [x["cache_kv_" + w] for w in windows], y_dram,
                            [out["p_kv_" + w][0] for w in windows], [out["s_kv_" + w] for w in windows])
        with nc.cleanup_on_exit():
            with nc.sbuf_tensor("x1", [P, TT, D], F32) as xt, nc.sbuf_tensor("yo1", [P, KD, TOK], F32) as yo:
                out_phase(nc, "o1", x["attn_w_out"][0], y_dram, yo, xt, source)
                norm_phase(nc, "n1", xt, ident, uhi, ulo, post[0], pre[1], yo, (h_dram, hs_dram))
        with nc.cleanup_on_exit():
            ssd_phase(nc, uhi, ulo, ident, x["ssd_w_in"][0], t, ssd_params, (x["state_ssm"], x["state_conv"]), y_dram,
                      (out["p_ssm"], out["p_conv"]), (out["s_ssm"], out["s_conv"]))
        with nc.cleanup_on_exit():
            with nc.sbuf_tensor("x2", [P, TT, D], F32) as xt, nc.sbuf_tensor("yo2", [P, KD, TOK], F32) as yo:
                out_phase(nc, "o2", x["ssd_w_out"][0], y_dram, yo, xt, (h_dram, hs_dram))
                norm_phase(nc, "n2", xt, ident, None, None, post[1], None, yo, target)


def tables():
    half = HD // 2
    inv = (np.float32(10000.0) ** (-np.arange(half, dtype=np.float32) / np.float32(half))).astype(np.float32)
    pos = np.concatenate([np.arange(SEQ), np.tile(PAST + np.arange(NT), NB)]).astype(np.float32)
    angle = (pos[None, :] * inv[:, None]).astype(np.float32)
    cos, sin = np.cos(angle), np.sin(angle)

    def z(ok):
        return np.where(ok, 0.0, BIG).astype(np.float32)

    def ones(ok):
        return ok.astype(np.float32)

    i, j = np.arange(P)[:, None], np.arange(P)[None, :]
    masks = np.stack([z(j >= i), z(j <= i), z((j // 32 == i // 32) & (j % 32 <= i % 32))], 1)
    seq, token = i // 32, i % 4
    cached = np.concatenate([j >= token, (np.arange(2 * P)[None, :] % 4) == token,
                             (np.arange(64)[None, :] // 16) == token], 1)
    new, new_token = np.arange(NS)[None, :] // NT, np.arange(NS)[None, :] % NT
    fresh = [(new == 4 * s + seq) & ((new_token <= token) if w == 0 else (new_token == token))
             for s in range(2) for w in range(NW)]
    tri = i <= j
    si, sj = np.arange(NS)[:, None], np.arange(NS)[None, :]
    tri_s = (si <= sj) & (si // NT == sj // NT)
    head = np.arange(HG)[:, None, None]
    return {
        "ident": np.eye(P, dtype=np.float32),
        "cos": np.concatenate([cos, cos]).astype(np.float32),
        "sin": np.concatenate([sin, -sin]).astype(np.float32),
        "masks": masks,
        "mask_s": z(np.concatenate([cached] + fresh, 1)),
        "tri": ones(tri), "tri_s": ones(tri_s), "mask": z(tri), "mask_ss": z(tri_s),
        "own": ones(si // NT == np.arange(NB)[None, :]),
        "pick": ones(np.broadcast_to(head == np.arange(HG)[None, :, None], (HG, HG, P))).reshape(HG, HG * P),
        "spread": ones(head == 2 * np.arange(4)[None, :, None] + np.arange(P)[None, None, :] // PD),
    }


_INS = ["x_prompt", "x_sample", "cache_kv_w128", "cache_kv_w512", "cache_kv_w2048", "state_ssm", "state_conv",
        "norm_pre", "norm_post", "attn_w_in", "attn_w_out", "ssd_w_in", "ssd_conv_w", "ssd_conv_b", "ssd_dt_bias",
        "ssd_a_log", "ssd_d", "ssd_norm_w", "ssd_w_out"]
_OUTS = {
    "y_prompt": (1, SEQ, D), "y_sample": (NB, NT, D),
    "p_kv_w128": (1, 1, 128, 2, NG, HD), "p_kv_w512": (1, 1, SEQ, 2, NG, HD), "p_kv_w2048": (1, 1, SEQ, 2, NG, HD),
    "p_ssm": (1, 1, NG * HG, PD, ST), "p_conv": (1, 1, PRE, INNER + 2 * NG * ST),
    "s_kv_w128": (1, NB, 128, 2, NG, HD), "s_kv_w512": (1, NB, PAST + NT, 2, NG, HD),
    "s_kv_w2048": (1, NB, PAST + NT, 2, NG, HD),
    "s_ssm": (1, NB, NG * HG, PD, ST), "s_conv": (1, NB, PRE, INNER + 2 * NG * ST),
}


def kernel(**inputs):
    import concourse.bacc as bacc
    from concourse.bass_utils import run_bass_kernel_spmd

    nc = bacc.Bacc("TRN2", target_bir_lowering=False, num_devices=1)
    arrays = {}

    def given(name, a):
        arrays[f"in_{name}_dram"] = a
        return nc.dram_tensor(f"in_{name}_dram", a.shape, F32, kind="ExternalInput").ap()

    x = {n: given(n, np.ascontiguousarray(inputs[n])) for n in _INS}
    t = {n: given(n, a) for n, a in tables().items()}
    out = {n: nc.dram_tensor(f"out_{n}_dram", shape, F32, kind="ExternalOutput").ap() for n, shape in _OUTS.items()}
    scratch = [nc.dram_tensor(n, shape, F32, kind="Internal").ap()
               for n, shape in (("mixed", (KI, P, TOK)), ("h_prompt", (SEQ, D)), ("h_sample", (NS, D)))]
    build(nc, x, t, out, scratch)
    r = run_bass_kernel_spmd(nc, [arrays], core_ids=[0])
    return tuple(r.results[0][f"out_{n}_dram"] for n in _OUTS)
```

```python
from contextlib import ExitStack

import numpy as np

import concourse.bass as bass
from concourse import mybir

F32 = mybir.dt.float32
F32R = mybir.dt.float32r
ALU = mybir.AluOpType
ACT = mybir.ActivationFunctionType
AX = mybir.AxisListType.X

P = 128
D = 1024
KD = D // P
SEQ = 512
NB, NT = 8, 4
NS = NB * NT
TOK = SEQ + NS
HALF = TOK // 2
TT = SEQ // P + 1
ROWS = [P] * (TT - 1) + [NS]
PAST = 256
HD = 128
NG = 4
NH = 4
PAIR = 2
WINDOWS = ((128, 1), (512, 4), (2048, 16))
NW = len(WINDOWS)
INNER = 2048
KI = INNER // P
EPS = 1e-6
BIG = -1e30


class Mem:

    def __init__(self, nc, ctx, tag):
        self.nc, self.ctx, self.tag = nc, ctx, tag

    def sb(self, name, shape, dt=F32):
        return self.ctx.enter_context(self.nc.sbuf_tensor(f"{self.tag}_{name}", shape, dt))

    def ps(self, name, shape, dt=F32):
        return self.ctx.enter_context(self.nc.psum_tensor(f"{self.tag}_{name}", shape, dt))

    def sem(self, name):
        return self.nc.alloc_semaphore(name=f"{self.tag}_{name}")


class Plan:

    def __init__(self, ahead, behind, tiles, banks, unbanked):
        self.ahead, self.behind, self.tiles, self.banks, self.unbanked = ahead, behind, tiles, banks, unbanked
        self.once = Stage(self, 0, None, [0] * banks).uses()
        self.each = Stage(self, 1, 0, [0] * banks).uses()

    def first(self):
        return Stage(self, 0, None, [0] * self.banks)

    def middle(self, i):
        return Stage(self, i + 1, i, [a + b * i for a, b in zip(self.once, self.each)])

    def last(self):
        return Stage(self, None, NG - 1, [a + b * (NG - 1) for a, b in zip(self.once, self.each)])


class Stage:

    def __init__(self, plan, head, tail, base):
        self.plan, self.head, self.tail, self.base = plan, head, tail, base
        self.banked = [i for t in range(-1, plan.tiles) for i, _ in self.items(t) if i[0] not in plan.unbanked]

    def items(self, t):
        return ([(i, self.tail) for i in self.plan.behind.get(t, []) if self.tail is not None] +
                [(i, self.head) for i in self.plan.ahead.get(t, []) if self.head is not None])

    def place(self, item):
        n = self.banked.index(item)
        return n % self.plan.banks, self.base[n % self.plan.banks] + n // self.plan.banks

    def uses(self):
        return [len(self.banked[b::self.plan.banks]) for b in range(self.plan.banks)]


def all_groups(eng, plan, stage):
    stage(plan.first())
    with eng.Fori(0, NG - 1) as i:
        stage(plan.middle(i))
    stage(plan.last())


def halves(ps, rows=P):
    return ps[0:rows, :, 0:HALF]


def two(ap):
    return ap.rearrange("p (b c) -> p b c", b=2)


def bcast_rows(ap):
    return ap.partition_broadcast(P)


def norm_phase(nc, tag, xt, ident, uhi, ulo, post, pre, src, dst):
    with ExitStack() as ctx:
        m = Mem(nc, ctx, tag)
        if post is not None:
            w_post = m.sb("w_post", [P, D])
            back = m.ps("back", [P, 2, 2, 512])
        if pre is not None:
            w_pre = m.sb("w_pre", [P, D])
            normed = m.sb("normed", [P, 2, D])
            turned = m.ps("turned", [P, 2, 2, 512])
        scaled = m.sb("scaled", [P, 2, D])
        square = m.sb("square", [P, D])
        stats = m.sb("stats", [P, TT, 6])
        w_in = m.sem("w_in")
        x_in = [m.sem(f"x_in{i}") for i in range(TT)]
        back_ready = m.sem("back_ready")
        sum1_ready = m.sem("sum1_ready")
        inv1_ready = m.sem("inv1_ready")
        rstd1_ready = m.sem("rstd1_ready")
        scaled_ready = m.sem("scaled_ready")
        h_ready = m.sem("h_ready")
        sum2_ready = m.sem("sum2_ready")
        inv2_ready = m.sem("inv2_ready")
        rstd2_ready = m.sem("rstd2_ready")
        normed_ready = m.sem("normed_ready")
        turned_ready = m.sem("turned_ready")
        hi_ready = m.sem("hi_ready")
        lo_ready = m.sem("lo_ready")
        mean_ready = m.sem("mean_ready")
        stored = m.sem("stored")
        block = ctx.enter_context(nc.Block())
        span = [slice(i * P, i * P + ROWS[i]) for i in range(TT)]

        @block.sync
        def _(sp):
            n = 0
            if post is not None:
                sp.dma_start(w_post[:, :], bcast_rows(post)).then_inc(w_in, 16)
            if pre is not None:
                sp.dma_start(w_pre[:, :], bcast_rows(pre)).then_inc(w_in, 16)
            if src is not None and post is None:
                for i in range(TT):
                    rows = src[0][span[i], :] if i < TT - 1 else src[1]
                    sp.dma_start(xt[0:ROWS[i], i, :], rows).then_inc(x_in[i], 16)
            if dst is not None:
                for i in range(TT):
                    sp.wait_ge(h_ready, i + 1)
                    rows = dst[0][span[i], :] if i < TT - 1 else dst[1]
                    sp.dma_start(rows, xt[0:ROWS[i], i, :]).then_inc(stored, 16)
                sp.wait_ge(stored, 16 * TT)

        @block.tensor
        def _(pe):
            def to_tokens(i):
                if i >= 2:
                    pe.wait_ge(scaled_ready, i - 1)
                for k in range(KD):
                    last = pe.transpose(back[0:ROWS[i], i % 2, k // 4, (k % 4) * P:(k % 4 + 1) * P],
                                        src[:, k, span[i]], ident[:, :])
                last.then_inc(back_ready, 1)

            def to_features(i):
                pe.wait_ge(normed_ready, i + 1)
                if i >= 2:
                    pe.wait_ge(lo_ready, i - 1)
                r = ROWS[i]
                for k in range(KD):
                    last = pe.transpose(turned[:, i % 2, k // 4, (k % 4) * r:(k % 4 + 1) * r],
                                        normed[0:r, i % 2, k * P:(k + 1) * P], ident[0:r, 0:r])
                last.then_inc(turned_ready, 1)

            for i in range(TT + 1):
                if post is not None and i < TT:
                    to_tokens(i)
                if pre is not None and i >= 1:
                    to_features(i - 1)

        @block.scalar
        def _(act):
            def sum_squares(i, ins, slot, signal):
                act.activation(square[0:ROWS[i], :].rearrange("p (a c) -> p a c", a=2), ins, ACT.Square,
                               accum_out=stats[0:ROWS[i], i, slot:slot + 1]).then_inc(signal, 1)

            def root(i, slot, ready, signal):
                act.wait_ge(ready, i + 1)
                act.activation(stats[0:ROWS[i], i, slot + 2:slot + 3], stats[0:ROWS[i], i, slot + 1:slot + 2],
                               ACT.Sqrt).then_inc(signal, 1)

            def split(i):
                r = ROWS[i]
                act.wait_ge(turned_ready, i + 1)
                act.activation(uhi[:, :, span[i]].rearrange("p (a k) c -> p a k c", a=2),
                               turned[:, i % 2, :, 0:4 * r].rearrange("p a (k c) -> p a k c", k=4),
                               ACT.Copy).then_inc(hi_ready, 1)

            for i in range(TT + 1):
                if i < TT and post is not None:
                    act.wait_ge(back_ready, i + 1)
                    if i:
                        act.wait_ge(sum2_ready if pre is not None else sum1_ready, i)
                    sum_squares(i, back[0:ROWS[i], i % 2], 0, sum1_ready)
                    root(i, 0, inv1_ready, rstd1_ready)
                if i < TT and pre is not None:
                    if post is not None:
                        act.wait_ge(h_ready, i + 1)
                        act.wait_ge(sum1_ready, i + 1)
                    else:
                        act.wait_ge(x_in[i], 16)
                        if i:
                            act.wait_ge(sum2_ready, i)
                    sum_squares(i, xt[0:ROWS[i], i, :].rearrange("p (a c) -> p a c", a=2), 3, sum2_ready)
                    root(i, 3, inv2_ready, rstd2_ready)
                if i >= 1 and pre is not None:
                    split(i - 1)

        @block.vector
        def _(dve):
            dve.wait_ge(w_in, 16 * ((post is not None) + (pre is not None)))
            means = 0

            def inverse(i, slot, ready, signal):
                nonlocal means
                dve.wait_ge(ready, i + 1)
                s = stats[0:ROWS[i], i, slot:slot + 1]
                inv = stats[0:ROWS[i], i, slot + 1:slot + 2]
                dve.tensor_scalar(s, s, 1.0 / D, EPS, ALU.mult, ALU.add).then_inc(mean_ready, 1)
                means += 1
                dve.wait_ge(mean_ready, means)
                dve.reciprocal(inv, s).then_inc(signal, 1)

            def rest(i):
                dve.wait_ge(hi_ready, i + 1)
                r = ROWS[i]
                dve.tensor_tensor(ulo[:, :, span[i]].rearrange("p (a k) c -> p a k c", a=2),
                                  turned[:, i % 2, :, 0:4 * r].rearrange("p a (k c) -> p a k c", k=4),
                                  uhi[:, :, span[i]].bitcast(F32).rearrange("p (a k) c -> p a k c", a=2),
                                  ALU.subtract).then_inc(lo_ready, 1)

            for i in range(TT + 1):
                if i < TT:
                    r = ROWS[i]
                    if post is not None:
                        inverse(i, 0, sum1_ready, inv1_ready)
                        dve.wait_ge(rstd1_ready, i + 1)
                        if i >= 2:
                            dve.wait_ge(h_ready, i - 1)
                        dve.scalar_tensor_tensor(
                            out=scaled[0:r, i % 2, :].rearrange("p (a c) -> p a c", a=2), in0=back[0:r, i % 2],
                            scalar=stats[0:r, i, 2:3], in1=w_post[0:r, :].rearrange("p (a c) -> p a c", a=2),
                            op0=ALU.mult, op1=ALU.mult).then_inc(scaled_ready, 1)
                        dve.wait_ge(scaled_ready, i + 1)
                        dve.tensor_tensor(xt[0:r, i, :], xt[0:r, i, :], scaled[0:r, i % 2, :],
                                          ALU.add).then_inc(h_ready, 1)
                    if pre is not None:
                        inverse(i, 3, sum2_ready, inv2_ready)
                        dve.wait_ge(rstd2_ready, i + 1)
                        if i >= 2:
                            dve.wait_ge(turned_ready, i - 1)
                        dve.scalar_tensor_tensor(out=normed[0:r, i % 2, :], in0=xt[0:r, i, :],
                                                 scalar=stats[0:r, i, 5:6], in1=w_pre[0:r, :],
                                                 op0=ALU.mult, op1=ALU.mult).then_inc(normed_ready, 1)
                if i >= 1 and pre is not None:
                    rest(i - 1)


def out_phase(nc, tag, w_out, y_dram, out_fm, xt=None, x_src=None):
    with ExitStack() as ctx:
        m = Mem(nc, ctx, tag)
        RING = 2
        YC = 2
        NY = KI // YC
        y = m.sb("y", [P, 2, YC, TOK])
        yhi = m.sb("yhi", [P, KI, TOK], F32R)
        ylo = m.sb("ylo", [P, KI, TOK], F32R)
        w = m.sb("w", [P, RING, KI * P])
        whi = m.sb("whi", [P, RING, KI * P], F32R)
        wlo = m.sb("wlo", [P, RING, KI * P], F32R)
        acc = m.ps("acc", [P, RING, 2, 512])
        w_in = [m.sem(f"w_in{r}") for r in range(RING)]
        y_in = [m.sem(f"y_in{k}") for k in range(2)]
        x_in = m.sem("x_in")
        whi_ready = m.sem("whi_ready")
        wlo_ready = m.sem("wlo_ready")
        yhi_ready = m.sem("yhi_ready")
        ylo_ready = m.sem("ylo_ready")
        acc_ready = m.sem("acc_ready")
        acc_free = m.sem("acc_free")
        block = ctx.enter_context(nc.Block())
        ROUNDS = KD // RING

        def w_tile(o):
            return w_out.rearrange("(k p) n -> p k n", p=P)[:, :, bass.ts(o, P)]

        @block.sync
        def _(sp):
            sp.dma_start(w[:, 0].rearrange("p (k n) -> p k n", k=KI), w_tile(0)).then_inc(w_in[0], 16)
            for k in range(NY):
                if k >= 2:
                    sp.wait_ge(ylo_ready, k - 1)
                sp.dma_start(y[:, k % 2], y_dram[YC * k:YC * k + YC].rearrange("k p t -> p k t")) \
                    .then_inc(y_in[k % 2], 16)
                if k == 1:
                    sp.dma_start(w[:, 1].rearrange("p (k n) -> p k n", k=KI), w_tile(1)).then_inc(w_in[1], 16)
            with sp.Fori(0, ROUNDS - 1) as i:
                for r in range(RING):
                    sp.wait_ge(wlo_ready, RING * i + r + 1)
                    sp.dma_start(w[:, r].rearrange("p (k n) -> p k n", k=KI), w_tile(RING * i + RING + r)) \
                        .then_inc(w_in[r], 16)
            if x_src is not None:
                for i in range(TT):
                    rows = x_src[0][i * P:(i + 1) * P, :] if i < TT - 1 else x_src[1]
                    sp.dma_start(xt[0:ROWS[i], i, :], rows).then_inc(x_in, 16)
                sp.wait_ge(x_in, 16 * TT)

        @block.scalar
        def _(act):
            def w_high(i, r):
                act.wait_ge(w_in[r], 16 * i + 16)
                act.activation(whi[:, r], w[:, r], ACT.Copy).then_inc(whi_ready, 1)

            def evacuate(i, r):
                act.wait_ge(acc_ready, RING * i + r + 1)
                act.activation(two(out_fm[:, bass.ds(RING * i + r, 1), :].rearrange("p o t -> p (o t)")),
                               halves(acc[:, r]), ACT.Copy).then_inc(acc_free, 1)

            w_high(0, 0)
            for k in range(NY):
                act.wait_ge(y_in[k % 2], 16 * (k // 2) + 16)
                act.activation(yhi[:, YC * k:YC * k + YC, :], y[:, k % 2], ACT.Copy).then_inc(yhi_ready, 1)
            w_high(0, 1)
            with act.Fori(0, ROUNDS - 1) as i:
                for r in range(RING):
                    act.wait_ge(acc_ready, RING * i + r + 1)
                    w_high(i + 1, r)
                    evacuate(i, r)
            for r in range(RING):
                evacuate(ROUNDS - 1, r)

        @block.vector
        def _(dve):
            def w_low(i, r):
                dve.wait_ge(whi_ready, RING * i + r + 1)
                dve.tensor_tensor(wlo[:, r], w[:, r], whi[:, r].bitcast(F32), ALU.subtract) \
                    .then_inc(wlo_ready, 1)

            w_low(0, 0)
            for k in range(NY):
                dve.wait_ge(yhi_ready, k + 1)
                dve.tensor_tensor(ylo[:, YC * k:YC * k + YC, :], y[:, k % 2],
                                  yhi[:, YC * k:YC * k + YC, :].bitcast(F32), ALU.subtract).then_inc(ylo_ready, 1)
            w_low(0, 1)
            with dve.Fori(0, ROUNDS - 1) as i:
                for r in range(RING):
                    w_low(i + 1, r)

        @block.tensor
        def _(pe):
            pe.sem_inc(acc_free, RING)
            with pe.Fori(0, ROUNDS) as i:
                for r in range(RING):
                    pe.wait_ge(wlo_ready, RING * i + r + 1)
                    pe.wait_ge(acc_free, RING * i + r + 1)
                    for k in range(KI):
                        if k % YC == 0:
                            pe.wait_ge(ylo_ready, k // YC + 1)
                        for a, b in ((whi, yhi), (whi, ylo), (wlo, yhi)):
                            for h in range(2):
                                last = pe.matmul(acc[:, r, h, 0:HALF], a[:, r, k * P:(k + 1) * P],
                                                 b[:, k, h * HALF:(h + 1) * HALF],
                                                 start=(k == 0 and a is whi and b is yhi),
                                                 stop=(k == KI - 1 and a is wlo))
                    last.then_inc(acc_ready, 1)


TILES = NW * (2 + NH) + NH
CH = (P, P, P, 64)
CW = sum(CH)
SW = CW + NW * NS
SCALE = float(HD) ** -0.5
MERGE = 9


def attn_columns(t, g):
    if t >= NW * (2 + NH):
        return 3 * INNER + 6 * NG * HD + g * (NH * HD) + (t - NW * (2 + NH)) * HD
    w, j = divmod(t, 2 + NH)
    if j == 0:
        return 3 * INNER + w * NG * HD + g * HD
    if j == 1:
        return 3 * INNER + (NW + w) * NG * HD + g * HD
    return w * INNER + g * (NH * HD) + (j - 2) * HD


def attn_kind(t):
    if t >= NW * (2 + NH):
        return "G", t - NW * (2 + NH)
    w, j = divmod(t, 2 + NH)
    return ("K", w) if j == 0 else ("V", w) if j == 1 else ("Q", w, j - 2)


ROPED = [t for t in range(TILES) if attn_kind(t)[0] in "KQ"]
UNITS = {0: [[(1, 0), (1, 1), (2, 1), (2, 2)], [(3, 2), (3, 3), (0, 0)]],
         1: [[(i, i) for i in range(4)]], 2: [[(i, i) for i in range(4)]]}
SLOT = {(0, 0): 0, (0, 1): 1, (1, 0): 2, (2, 0): 3}

ATTN_AHEAD = {t: [] for t in range(TILES)}
for _w in range(NW):
    ATTN_AHEAD[6 * _w + 3] += [("V", _w), ("K", _w), ("X", _w)]
    for _h in range(NH):
        ATTN_AHEAD[6 * _w + 3 + _h] += [("S", _w, _h, u) for u in range(len(UNITS[_w]))]
for _i, _t in enumerate((10, 11, 13, 14)):
    ATTN_AHEAD[_t] += [("KT", 0, _i)]
ATTN_AHEAD[18] += [("SC", 0), ("SN", 0)]
ATTN_AHEAD[19] += [("KT", 1, i) for i in range(4)] + [("M", w) for w in range(NW)]
ATTN_AHEAD[20] += [("D", w) for w in range(NW)] + [("PC", 0), ("PN", 0), ("SC", 1), ("SN", 1)]
ATTN_AHEAD[21] += [("OS", 0)]
HEADS = [("PT", h, w, u) for h in range(NH) for w, u in SLOT]
ATTN_BEHIND = {0: [("F",), ("PC", 1), ("PN", 1)], 1: HEADS[:4] + [("OS", 1)] + HEADS[4:5], 2: HEADS[5:11], 3: HEADS[11:]}
SCORES = [item for t in range(TILES) for item in ATTN_AHEAD[t] if item[0] == "S"]
ATTN = Plan(ATTN_AHEAD, ATTN_BEHIND, TILES, 2, ("OS",))


def attention_phase(nc, uhi, ulo, ident, w_in_dram, tables, caches, y_dram, p_kv, s_kv):

    with ExitStack() as ctx:
        m = Mem(nc, ctx, "at")
        cos = m.sb("cos", [P, TOK])
        sin = m.sb("sin", [P, TOK])
        masks = m.sb("masks", [P, 3, P])
        mask_s = m.sb("mask_s", [P, 2 * SW - CW])
        w = m.sb("w", [P, PAIR, KD * P])
        whi = m.sb("whi", [P, PAIR, KD * P], F32R)
        wlo = m.sb("wlo", [P, PAIR, KD * P], F32R)
        q = m.sb("q", [P, NH, SEQ])
        qs = m.sb("qs", [P, NW, 4, NH, 8])
        k = m.sb("k", [P, SEQ])
        ks = m.sb("ks", [P, NW, NS])
        v = m.sb("v", [P, TOK])
        v_rows = m.sb("v_rows", [P, NW, 4, HD])
        k_rows = m.sb("k_rows", [P, 4, HD])
        new_rows = m.sb("new_rows", [NS, NW, 2, HD])
        straight = m.sb("straight", [P, TOK])
        crossed = m.sb("crossed", [P, TOK])
        probs = m.sb("probs", [P, NH, 4, 512])
        top = m.sb("top", [P, NW, 4, NH])
        neg_top = m.sb("neg_top", [P, NW, 4, NH])
        den = m.sb("den", [P, NW, 4, NH])
        factor = m.sb("factor", [P, NW, 4, NH])
        row_top = m.sb("row_top", [NH, NW, SEQ])
        row_den = m.sb("row_den", [NH, NW, SEQ])
        row_all = m.sb("row_all", [NH, SEQ])
        probs_t = m.sb("probs_t", [P, 2, 512])
        k_cache = m.sb("k_cache", [P, 4, 4, HD])
        v_cache = m.sb("v_cache", [P, 4, 4, HD])
        keys_t = m.sb("keys_t", [P, 4, CW])
        probs_s = m.sb("probs_s", [P, SW])
        stat_s = m.sb("stat_s", [P, 4])
        cached_t = m.sb("cached_t", [P, 4, P])
        new_t = m.sb("new_t", [NS, NW, P])
        yg = m.sb("yg", [P, NH, TOK])
        proj = m.ps("proj", [P, PAIR, 2, 512])
        small = [m.ps(f"small{b}", [P, 512]) for b in range(2)]
        out_t = [m.ps(f"out_t{b}", [P, 512]) for b in range(2)]

        held_back = m.sem("held_back")
        consts_in = m.sem("consts_in")
        w_in = [m.sem(f"w_in{r}") for r in range(PAIR)]
        whi_ready = m.sem("whi_ready")
        wlo_ready = m.sem("wlo_ready")
        proj_ready = m.sem("proj_ready")
        proj_free = [m.sem(f"proj_free{r}") for r in range(PAIR)]
        turned_ready = m.sem("turned_ready")
        qk_ready = m.sem("qk_ready")
        v_ready = m.sem("v_ready")
        small_ready = [m.sem(f"small_ready{b}") for b in range(2)]
        small_free = [m.sem(f"small_free{b}") for b in range(2)]
        masked_ready = m.sem("masked_ready")
        top_ready = m.sem("top_ready")
        neg_ready = m.sem("neg_ready")
        probs_ready = m.sem("probs_ready")
        kv_rows_ready = m.sem("kv_rows_ready")
        kv_stored = m.sem("kv_stored")
        k_cache_in = m.sem("k_cache_in")
        v_cache_in = m.sem("v_cache_in")
        keys_ready = m.sem("keys_ready")
        s_masked = m.sem("s_masked")
        s_top = m.sem("s_top")
        s_neg = m.sem("s_neg")
        s_exp = m.sem("s_exp")
        s_inv = m.sem("s_inv")
        s_probs = m.sem("s_probs")
        s_turned = m.sem("s_turned")
        s_out = m.sem("s_out")
        rows_ready = m.sem("rows_ready")
        merge = m.sem("merge")
        shift_exp = m.sem("shift_exp")
        factor_ready = m.sem("factor_ready")
        scaled_ready = m.sem("scaled_ready")
        probs_t_ready = m.sem("probs_t_ready")
        head_done = m.sem("head_done")
        gates_ready = m.sem("gates_ready")
        silu_ready = m.sem("silu_ready")
        keys_odd_ready = m.sem("keys_odd_ready")
        out_free = [m.sem(f"out_free{b}") for b in range(2)]
        yg_ready = m.sem("yg_ready")
        y_stored = m.sem("y_stored")
        caches_copied = m.sem("caches_copied")
        block = ctx.enter_context(nc.Block())

        def bank(st, item):
            return small[st.place(item)[0]]

        def filled(eng, st, item):
            b, ahead = st.place(item)
            eng.wait_ge(small_ready[b], ahead + 1)

        def free(eng, st, item):
            eng.sem_inc(small_free[st.place(item)[0]], 1)

        def strided(ap, w_, i):
            d = WINDOWS[w_][1]
            if d == 1:
                return ap[:, i * P:(i + 1) * P]
            if d == 4:
                return ap.rearrange("p (m r) -> p r m", r=4)[:, i, :]
            return ap.rearrange("p (m r) -> p r m", r=16)[:, 4 * i:4 * i + 4, :]

        def square(ap, w_):
            return ap.rearrange("p (r m) -> p r m", r=4) if WINDOWS[w_][1] == 16 else ap

        STORES = (6, 6, 12)

        @block.sync
        def _(sp):
            def load_w(g, t, slot):
                src = w_in_dram.rearrange("(k p) n -> p k n", p=P)[:, :, bass.ds(attn_columns(t, g), P)]
                sp.dma_start(w[:, slot].rearrange("p (k n) -> p k n", k=KD), src).then_inc(w_in[slot], 16)

            def load_cache(g, s, kv, dst, signal):
                for c, (cache, rows) in enumerate(((0, slice(0, P)), (1, slice(0, P)), (1, slice(P, 2 * P)))):
                    src = caches[cache][0, 4 * s:4 * s + 4, rows, kv, bass.ds(g, 1), :]
                    sp.dma_start(dst[:, :, c, :], src.rearrange("n p g d -> p n (g d)")).then_inc(signal, 16)
                for t in range(NT):
                    src = caches[2][0, 4 * s:4 * s + 4, :, kv, bass.ds(g, 1), :] \
                        .rearrange("n (m r) g d -> r m n (g d)", r=16)[t]
                    sp.dma_start(dst[16 * t:16 * t + 16, :, 3, :], src).then_inc(signal, 16)

            def store_rows(w_, g, kv, rows):
                out = p_kv[w_][0, :, kv, bass.ds(g, 1), :]
                if w_ == 0:
                    sp.dma_start(out.rearrange("p g d -> p (g d)"), rows[:, 3, :]).then_inc(kv_stored, 16)
                elif w_ == 1:
                    sp.dma_start(out.rearrange("(p r) g d -> p r (g d)", r=4), rows).then_inc(kv_stored, 16)
                else:
                    for r in range(4):
                        sp.dma_start(out.rearrange("(m i r) g d -> r m i (g d)", i=4, r=4)[r],
                                     rows[32 * r:32 * r + 32]).then_inc(kv_stored, 16)

            def store_new(w_, g):
                keep = s_kv[w_].shape[2]
                out = s_kv[w_][0, :, keep - NT:keep, :, bass.ds(g, 1), :]
                for t in range(NT):
                    sp.dma_start(out[:, t].rearrange("n k g d -> n k (g d)"), new_rows[t:NS:NT, w_]) \
                        .then_inc(kv_stored, 16)

            sp.dma_start(cos[:, :], tables["cos"]).then_inc(consts_in, 16)
            for t in range(PAIR):
                load_w(0, t, t)
            sp.dma_start(sin[:, :], tables["sin"]).then_inc(consts_in, 16)
            sp.dma_start(masks[:, :, :], tables["masks"]).then_inc(consts_in, 16)
            sp.dma_start(mask_s[:, :], tables["mask_s"]).then_inc(consts_in, 16)
            for t in range(PAIR):
                sp.wait_ge(wlo_ready, t + 1)
                load_w(0, PAIR + t, t)

            def stage(st):
                g = st.head
                for t in range(TILES):
                    if t == 4 and st.tail is not None:
                        sp.wait_ge(yg_ready, (NH + 4) * (st.tail + 1))
                        sp.dma_start(y_dram[bass.ds(NH * st.tail, NH)].rearrange("h p t -> p h t"), yg[:, :, :]) \
                            .then_inc(y_stored, 16)
                    if g is None:
                        continue
                    sp.wait_ge(wlo_ready, TILES * g + t + PAIR + 1)
                    nxt = t + 2 * PAIR
                    load_w(g + nxt // TILES, nxt % TILES, t % PAIR)
                    if t == 0:
                        sp.wait_ge(keys_ready, 4 * g)
                        sp.wait_ge(keys_odd_ready, 4 * g)
                        load_cache(g, 0, 0, k_cache, k_cache_in)
                    if t == 5:
                        sp.wait_ge(s_out, 2 * g)
                        load_cache(g, 0, 1, v_cache, v_cache_in)
                    if t in (1, 2, 4, 5, 7, 8):
                        i, j = divmod((1, 2, 4, 5, 7, 8).index(t), 2)
                        c_rows, keep = caches[i].shape[2], s_kv[i].shape[2]
                        skip = c_rows - (keep - NT)
                        sp.dma_start(s_kv[i][0, bass.ds(2 * g + j, 1), 0:keep - NT].rearrange("n s k h d -> (n s) (k h d)"),
                                     caches[i][0, bass.ds(2 * g + j, 1), skip:].rearrange("n s k h d -> (n s) (k h d)")) \
                            .then_inc(caches_copied, 16)
                    for w_ in range(NW):
                        if t == 6 * w_ + 4:
                            sp.wait_ge(kv_rows_ready, 3 * (NW * g + w_) + 3)
                            store_rows(w_, g, 1, v_rows[:, w_])
                            store_rows(w_, g, 0, k_rows[:, :, :])
                            store_new(w_, g)
                    if t == 16:
                        sp.wait_ge(keys_ready, 4 * g + 2)
                        sp.wait_ge(keys_odd_ready, 4 * g + 2)
                        load_cache(g, 1, 0, k_cache, k_cache_in)
                if g is not None:
                    sp.wait_ge(s_out, 2 * g + 1)
                    load_cache(g, 1, 1, v_cache, v_cache_in)

            all_groups(sp, ATTN, stage)
            sp.wait_ge(y_stored, 16 * NG)
            sp.wait_ge(kv_stored, 16 * sum(STORES) * NG)
            sp.wait_ge(caches_copied, 16 * 2 * NW * NG)
            for r in range(PAIR):
                sp.wait_ge(w_in[r], 16 * (TILES * NG // PAIR + 2))

        @block.tensor
        def _(pe):
            def project(g, t):
                r = t % PAIR
                pe.wait_ge(wlo_ready, TILES * g + t + 1)
                pe.wait_ge(proj_free[r], TILES // PAIR * g + t // PAIR)
                for kk in range(KD):
                    for a, b in ((whi, uhi), (whi, ulo), (wlo, uhi)):
                        for h in range(2):
                            last = pe.matmul(proj[:, r, h, 0:HALF], a[:, r, kk * P:(kk + 1) * P],
                                             b[:, kk, h * HALF:(h + 1) * HALF],
                                             start=(kk == 0 and a is whi and b is uhi),
                                             stop=(kk == KD - 1 and a is wlo))
                last.then_inc(proj_ready, 1)

            def turn(out, ins, one):
                return pe.matmul(out, ins, one, is_transpose=True, start=True, stop=True)

            def roped(g, t):
                pe.wait_ge(qk_ready, 2 * len(ROPED) * g + 2 * ROPED.index(t) + 2)

            def small_item(st, g, item):
                n, ahead = st.place(item)
                b = small[n]
                pe.wait_ge(small_free[n], ahead)
                what = item[0]
                if what == "V":
                    pe.wait_ge(v_ready, NW * g + item[1] + 1)
                    for i in range(4):
                        last = turn(b[:, i * HD:(i + 1) * HD], v[:, i * P:(i + 1) * P], ident[:, :])
                elif what == "K":
                    roped(g, 6 * item[1])
                    for i in range(3 if item[1] == 0 else 0, 4):
                        last = turn(b[:, i * HD:(i + 1) * HD], k[:, i * P:(i + 1) * P], ident[:, :])
                elif what == "X":
                    turn(b[0:NS, 0:HD], ks[:, item[1], :], ident[:, :])
                    last = turn(b[0:NS, HD:2 * HD], v[:, SEQ:TOK], ident[:, :])
                elif what == "S":
                    _, w_, h, u = item
                    roped(g, 6 * w_ + 2 + h)
                    for j, (qt, kt) in enumerate(UNITS[w_][u]):
                        last = pe.matmul(b[:, j * P:(j + 1) * P], q[:, h, qt * P:(qt + 1) * P],
                                         k[:, kt * P:(kt + 1) * P], start=True, stop=True)
                elif what == "KT":
                    _, s, ni = item
                    pe.wait_ge(k_cache_in, 16 * 7 * (2 * g + s + 1))
                    for c, rows in enumerate(CH):
                        last = turn(b[:, c * P:c * P + rows], k_cache[0:rows, ni, c, :],
                                            ident[0:rows, 0:rows])
                elif what in ("SC", "SN"):
                    s = item[1]
                    roped(g, ROPED[-1])
                    pe.wait_ge(keys_ready, 4 * g + 2 * s + 2)
                    pe.wait_ge(keys_odd_ready, 4 * g + 2 * s + 2)
                    for ni in range(4):
                        pair = (4 * s + ni) // 2
                        for w_ in range(NW):
                            if what == "SC":
                                at = (0, P, 3 * P)[w_]
                                cols = (P, 2 * P, 64)[w_]
                                rhs, o = keys_t[:, ni, at:at + cols], b[32 * ni:32 * ni + 32, at:at + cols]
                            else:
                                rhs, o = ks[:, w_, :], b[32 * ni:32 * ni + 32, w_ * NS:(w_ + 1) * NS]
                            last = pe.matmul(o, qs[:, w_, pair].rearrange("p h t -> p (h t)"), rhs, start=True, stop=True)
                elif what == "M":
                    pe.wait_ge(top_ready, len(SCORES) * (g + 1))
                    for i in range(4):
                        last = turn(strided(b[0:NH, :], item[1], i), top[:, item[1], i, :], square(ident[:, :], item[1]))
                elif what == "D":
                    pe.wait_ge(probs_ready, len(SCORES) * (g + 1))
                    for i in range(4):
                        last = turn(strided(b[0:NH, :], item[1], i), den[:, item[1], i, :], square(ident[:, :], item[1]))
                elif what == "PC":
                    pe.wait_ge(s_probs, 2 * g + item[1] + 1)
                    for c, rows in enumerate(CH):
                        last = turn(b[0:rows, c * P:(c + 1) * P], probs_s[:, c * P:c * P + rows], ident[:, :])
                elif what == "PN":
                    for w_ in range(NW):
                        last = turn(b[0:NS, w_ * P:(w_ + 1) * P],
                                            probs_s[:, CW + w_ * NS:CW + (w_ + 1) * NS], ident[:, :])
                elif what == "F":
                    pe.wait_ge(merge, MERGE * g + MERGE)
                    pe.sem_inc(held_back, 1)
                    for w_ in range(NW):
                        for i in range(4):
                            at = (w_ * 4 + i) * NH
                            row = row_den[:, 2, i * P:(i + 1) * P] if w_ == 2 else strided(row_top[:, w_, :], w_, i)
                            last = turn(b[:, at:at + NH], row, ident[0:NH, 0:NH])
                elif what == "PT":
                    _, h, w_, u = item
                    pe.wait_ge(scaled_ready, len(HEADS) * g + HEADS.index(item) + 1)
                    for j in range(len(UNITS[w_][u])):
                        last = turn(b[:, j * P:(j + 1) * P], probs[:, h, SLOT[w_, u], j * P:(j + 1) * P],
                                            ident[:, :])
                last.then_inc(small_ready[n], 1)

            def sample_out(g, s):
                pe.wait_ge(s_turned, 4 * g + 2 * s + 2)
                pe.wait_ge(v_cache_in, 16 * 7 * (2 * g + s + 1))
                pe.wait_ge(kv_rows_ready, 3 * NW * (g + 1))
                pe.wait_ge(out_free[s], 3 * g)
                for ni in range(4):
                    o = out_t[s][:, 32 * ni:32 * ni + 32]
                    for c, rows in enumerate(CH):
                        pe.matmul(o, v_cache[0:rows, ni, c, :], cached_t[0:rows, c, 32 * ni:32 * ni + 32],
                                  start=(c == 0), stop=False)
                    for w_ in range(NW):
                        last = pe.matmul(o, new_rows[:, w_, 1, :], new_t[:, w_, 32 * ni:32 * ni + 32],
                                         start=False, stop=(w_ == NW - 1))
                last.then_inc(s_out, 1)

            def weigh(g, n):
                _, h, w_, u = HEADS[n]
                pe.wait_ge(probs_t_ready, len(HEADS) * g + n + 1)
                if SLOT[w_, u] == 0:
                    pe.wait_ge(out_free[h % 2], 3 * g + 1 + h // 2)
                for j, (qt, kt) in enumerate(UNITS[w_][u]):
                    last = pe.matmul(strided(out_t[h % 2][:, :], w_, qt), v_rows[:, w_, kt, :],
                                     square(probs_t[:, n % 2, j * P:(j + 1) * P], w_),
                                     start=(SLOT[w_, u] == 0 and j == 0), stop=(SLOT[w_, u] == 3 and j == 3),
                                     skip_group_check=True)
                last.then_inc(head_done, 1)

            def stage(st):
                for t in range(TILES):
                    if st.head is not None:
                        project(st.head, t)
                    for item, g in st.items(t):
                        if item[0] == "OS":
                            sample_out(g, item[1])
                            continue
                        small_item(st, g, item)
                        if item[0] == "PT" and item != HEADS[0]:
                            weigh(g, HEADS.index(item) - 1)
                        if item == HEADS[-1]:
                            weigh(g, len(HEADS) - 1)

            all_groups(pe, ATTN, stage)

        @block.scalar
        def _(act):
            def w_high(g, t):
                act.wait_ge(w_in[t % PAIR], TILES // PAIR * 16 * g + 16 * (t // PAIR) + 16)
                act.activation(whi[:, t % PAIR], w[:, t % PAIR], ACT.Copy).then_inc(whi_ready, 1)

            def exps(g, item):
                _, w_, h, u = item
                n = SCORES.index(item)
                act.wait_ge(neg_ready, len(SCORES) * g + n + 1)
                blocks = UNITS[w_][u]
                for qt in dict.fromkeys(b[0] for b in blocks):
                    js = [j for j, b in enumerate(blocks) if b[0] == qt]
                    x = probs[:, h, SLOT[w_, u], js[0] * P:(js[-1] + 1) * P]
                    last = act.activation(x, x, ACT.Exp, bias=neg_top[:, w_, qt, h:h + 1], scale=SCALE,
                                          accum_out=den[:, w_, qt, h:h + 1])
                last.then_inc(probs_ready, 1)

            def copied(st, item, dst, src, signal, value):
                filled(act, st, item)
                act.activation(dst, src, ACT.Copy).then_inc(signal, 1)
                act.wait_ge(signal, value)
                free(act, st, item)

            for t in range(PAIR):
                w_high(0, t)
            def projected(g, t):
                act.wait_ge(proj_ready, TILES * g + t + 1)
                nxt = t + PAIR
                w_high(g + nxt // TILES, nxt % TILES)
                what = attn_kind(t)
                if what[0] == "V":
                    if what[1] == 0:
                        act.wait_ge(kv_rows_ready, 3 * NW * g)
                    d = WINDOWS[what[1]][1]
                    order = v[:, 0:SEQ].rearrange("p (r m) -> p m r", r=d)
                    for h, (a, z) in enumerate(((0, HALF), (HALF, SEQ))):
                        act.activation(order[:, a // d:z // d, :],
                                       proj[:, t % PAIR, h, 0:z - a].rearrange("p (m r) -> p m r", r=d), ACT.Copy)
                    act.activation(v[:, SEQ:TOK], proj[:, t % PAIR, 1, SEQ - HALF:HALF], ACT.Copy).then_inc(v_ready, 1)
                    act.wait_ge(v_ready, NW * g + what[1] + 1)
                    act.sem_inc(proj_free[t % PAIR], 1)
                if what[0] == "G":
                    if what[1] == 0:
                        act.wait_ge(y_stored, 16 * g)
                    act.activation(two(yg[:, what[1], :]), halves(proj[:, t % PAIR]), ACT.Copy).then_inc(gates_ready, 1)
                    act.wait_ge(gates_ready, NH * g + what[1] + 1)
                    act.sem_inc(proj_free[t % PAIR], 1)

            def stage(st):
                for t in range(TILES):
                    if st.head is not None:
                        projected(st.head, t)
                    if t == 0 and st.tail is not None:
                        act.activation(yg[:, :, :], yg[:, :, :], ACT.Silu).then_inc(silu_ready, 1)
                    for item, g in st.items(t):
                        if item[0] == "V":
                            w_ = item[1]
                            act.wait_ge(kv_stored, 16 * (sum(STORES) * g + sum(STORES[:w_])))
                            act.wait_ge(head_done, len(HEADS) * g)
                            copied(st, item, v_rows[:, w_], bank(st, item)[:, :].rearrange("p (i d) -> p i d", i=4),
                                   kv_rows_ready, 3 * (NW * g + w_) + 1)
                        elif item[0] == "K":
                            w_ = item[1]
                            lo = 3 if w_ == 0 else 0
                            copied(st, item, k_rows[:, lo:4],
                                   bank(st, item)[:, lo * HD:4 * HD].rearrange("p (i d) -> p i d", d=HD),
                                   kv_rows_ready, 3 * (NW * g + w_) + 2)
                        elif item[0] == "X":
                            w_ = item[1]
                            act.wait_ge(s_out, 2 * g)
                            copied(st, item, new_rows[:, w_],
                                   bank(st, item)[0:NS, 0:2 * HD].rearrange("p (i d) -> p i d", d=HD),
                                   kv_rows_ready, 3 * (NW * g + w_) + 3)
                        elif item[0] == "KT":
                            _, s, ni = item
                            if ni % 2 == 0:
                                if s == 1:
                                    filled(act, st, ("SC", 0))
                                copied(st, item, keys_t[:, ni, :], bank(st, item)[:, 0:CW], keys_ready,
                                       4 * g + 2 * s + ni // 2 + 1)
                        elif item[0] == "SN":
                            act.wait_ge(s_neg, 2 * g + item[1] + 1)
                            act.activation(probs_s[:, :], probs_s[:, :], ACT.Exp, bias=stat_s[:, 1:2], scale=SCALE,
                                           accum_out=stat_s[:, 2:3]).then_inc(s_exp, 1)
                        elif item[0] in ("M", "D"):
                            dst = row_top if item[0] == "M" else row_den
                            copied(st, item, dst[:, item[1], :], bank(st, item)[0:NH, :], rows_ready,
                                   2 * NW * g + (0 if item[0] == "M" else NW) + item[1] + 1)
                        elif item[0] == "PC":
                            s = item[1]
                            b = bank(st, item)
                            filled(act, st, item)
                            act.wait_ge(s_out, 2 * g + s)
                            act.activation(cached_t[:, 0:3, :], b[:, 0:3 * P].rearrange("p (c q) -> p c q", c=3), ACT.Copy)
                            act.activation(cached_t[0:64, 3, :], b[0:64, 3 * P:4 * P], ACT.Copy).then_inc(s_turned, 1)
                            act.wait_ge(s_turned, 4 * g + 2 * s + 1)
                            free(act, st, item)
                        elif item[0] == "PN":
                            copied(st, item, new_t[:, :, :],
                                   bank(st, item)[0:NS, 0:NW * P].rearrange("p (w q) -> p w q", w=NW),
                                   s_turned, 4 * g + 2 * item[1] + 2)
                        elif item[0] == "PT":
                            n = HEADS.index(item)
                            act.wait_ge(head_done, len(HEADS) * g + max(n - 1, 0))
                            cols = len(UNITS[item[2]][item[3]]) * P
                            copied(st, item, probs_t[:, n % 2, 0:cols], bank(st, item)[:, 0:cols], probs_t_ready,
                                   len(HEADS) * g + n + 1)
                    if st.head is not None:
                        for item in ATTN_AHEAD.get(t - 1, []):
                            if item[0] == "S":
                                exps(st.head, item)
                    if t == 20 and st.head is not None:
                        g = st.head
                        act.wait_ge(merge, MERGE * g + 3)
                        act.activation(row_top[:, :, :], row_top[:, :, :], ACT.Exp, scale=SCALE).then_inc(shift_exp, 1)

            all_groups(act, ATTN, stage)

        @block.vector
        def _(dve):
            dve.wait_ge(consts_in, 64)

            def rotate(g, t):
                n = ROPED.index(t)
                r = t % PAIR
                x = proj[:, r]
                dve.wait_ge(qk_ready, 2 * len(ROPED) * g + 2 * n)
                dve.tensor_tensor(two(straight[:, :]), halves(x), two(cos[:, :]), ALU.mult).then_inc(turned_ready, 1)
                dve.tensor_tensor(two(crossed[0:64, :]), x[64:P, :, 0:HALF], two(sin[64:P, :]), ALU.mult) \
                    .then_inc(turned_ready, 1)
                dve.tensor_tensor(two(crossed[64:P, :]), x[0:64, :, 0:HALF], two(sin[0:64, :]), ALU.mult) \
                    .then_inc(turned_ready, 1)
                dve.wait_ge(turned_ready, 3 * len(ROPED) * g + 3 * n + 3)
                dve.sem_inc(proj_free[r], 1)

            def blocks(ap, n):
                return ap.rearrange("p (j c) -> p j c", j=n)

            def mask_and_top(st, g, item):
                _, w_, h, u = item
                n = len(SCORES) * g + SCORES.index(item)
                b = bank(st, item)
                filled(dve, st, item)
                dst = probs[:, h, SLOT[w_, u], :]
                if w_ == 0:
                    c = 2 if u == 0 else 1
                    band = masks[:, 0:2, :].rearrange("p a c -> p (a c)")
                    last = dve.tensor_tensor(blocks(dst[:, 0:256 * c], c), blocks(b[:, 0:256 * c], c),
                                             band.unsqueeze(1).broadcast_to([P, c, 256]), ALU.add)
                    if u == 1:
                        last = dve.tensor_tensor(dst[:, 256:384], b[:, 256:384], masks[:, 1, :], ALU.add)
                else:
                    last = dve.tensor_tensor(blocks(dst, 4), blocks(b[:, :], 4),
                                             masks[:, w_, :].unsqueeze(1).broadcast_to([P, 4, P]), ALU.add)
                last.then_inc(masked_ready, 1)
                dve.wait_ge(masked_ready, n + 1)
                free(dve, st, item)
                if w_ == 0:
                    tops = [(1, 3, 0, 512)] if u == 0 else [(3, 4, 0, 256), (0, 1, 256, 384)]
                else:
                    tops = [(0, 4, 0, 512)]
                for a, z, lo, hi in tops:
                    last = dve.tensor_reduce(top[:, w_, a:z, h], blocks(dst[:, lo:hi], z - a), AX, ALU.max)
                last.then_inc(top_ready, 1)
                dve.wait_ge(top_ready, n + 1)
                for a, z, _, _ in tops:
                    last = dve.tensor_scalar(neg_top[:, w_, a:z, h], top[:, w_, a:z, h], -SCALE, None, ALU.mult)
                last.then_inc(neg_ready, 1)

            def sample_top(st, g, s):
                filled(dve, st, ("SC", s))
                dve.tensor_tensor(probs_s[:, 0:CW], bank(st, ("SC", s))[:, 0:CW], mask_s[:, 0:CW], ALU.add) \
                    .then_inc(s_masked, 1)
                filled(dve, st, ("SN", s))
                dve.tensor_tensor(probs_s[:, CW:SW], bank(st, ("SN", s))[:, 0:SW - CW],
                                  mask_s[:, CW + (SW - CW) * s:CW + (SW - CW) * (s + 1)], ALU.add) \
                    .then_inc(s_masked, 1)
                dve.wait_ge(s_masked, 4 * g + 2 * s + 2)
                free(dve, st, ("SC", s))
                free(dve, st, ("SN", s))
                dve.tensor_reduce(stat_s[:, 0:1], probs_s[:, :], AX, ALU.max).then_inc(s_top, 1)
                dve.wait_ge(s_top, 2 * g + s + 1)
                dve.tensor_scalar(stat_s[:, 1:2], stat_s[:, 0:1], -SCALE, None, ALU.mult).then_inc(s_neg, 1)

            def sample_normalise(g, s):
                dve.wait_ge(s_exp, 2 * g + s + 1)
                dve.reciprocal(stat_s[:, 3:4], stat_s[:, 2:3]).then_inc(s_inv, 1)
                dve.wait_ge(s_inv, 2 * g + s + 1)
                dve.tensor_scalar(probs_s[:, :], probs_s[:, :], stat_s[:, 3:4], None, ALU.mult).then_inc(s_probs, 1)

            def sample_gate(g, s):
                dve.wait_ge(s_out, 2 * g + s + 1)
                dve.wait_ge(silu_ready, g + 1)
                for j in range(2):
                    o = out_t[s][:, 0:P].rearrange("p (i j h k t) -> p j k h i t", i=2, j=2, h=NH, k=2)[:, j, j]
                    dst = yg[:, :, SEQ + 16 * s:SEQ + 16 * s + 16].rearrange("p h (i j t) -> p j h i t", i=2, j=2)[:, j]
                    dve.tensor_tensor(dst, o, dst, ALU.mult).then_inc(yg_ready, 1)
                dve.wait_ge(yg_ready, (NH + 4) * g + 2 * s + 2)
                dve.sem_inc(out_free[s], 1)

            def merge_windows(g):
                steps = MERGE * g

                def then(ins, n):
                    ins.then_inc(merge, 1)
                    dve.wait_ge(merge, steps + n)

                dve.wait_ge(rows_ready, 2 * NW * (g + 1))
                t = row_all[:, :]
                then(dve.tensor_tensor(t, row_top[:, 0, :], row_top[:, 1, :], ALU.max), 1)
                then(dve.tensor_tensor(t, t, row_top[:, 2, :], ALU.max), 2)
                wide = row_all[:, :].unsqueeze(1).broadcast_to([NH, NW, SEQ])
                then(dve.tensor_tensor(row_top[:, :, :], row_top[:, :, :], wide, ALU.subtract), 3)
                dve.wait_ge(shift_exp, g + 1)
                then(dve.tensor_tensor(row_den[:, :, :], row_den[:, :, :], row_top[:, :, :], ALU.mult), 4)
                then(dve.tensor_tensor(t, row_den[:, 0, :], row_den[:, 1, :], ALU.add), 5)
                then(dve.tensor_tensor(t, t, row_den[:, 2, :], ALU.add), 6)
                then(dve.reciprocal(t, t), 7)
                then(dve.tensor_tensor(row_top[:, 0:2, :], row_top[:, 0:2, :], wide[:, 0:2, :], ALU.mult), 8)
                then(dve.tensor_tensor(row_den[:, 2, :].rearrange("p (r m) -> p m r", r=16),
                                       row_top[:, 2, :].rearrange("p (m r) -> p m r", r=16),
                                       t.rearrange("p (m r) -> p m r", r=16), ALU.mult), 9)

            def get_factors(st, g):
                filled(dve, st, ("F",))
                dve.tensor_copy(factor[:, :, :, :].rearrange("p w i h -> p (w i h)"),
                                bank(st, ("F",))[:, 0:NW * 4 * NH]).then_inc(factor_ready, 1)
                dve.wait_ge(factor_ready, g + 1)
                free(dve, st, ("F",))

            def scale(n):
                _, h, w_, u = HEADS[n]
                dst = probs[:, h, SLOT[w_, u], :]
                if w_ == 0:
                    parts = [(1, 3, 0, 512)] if u == 0 else [(3, 4, 0, 256), (0, 1, 256, 384)]
                else:
                    parts = [(0, 4, 0, 512)]
                for a, z, lo, hi in parts:
                    x = blocks(dst[:, lo:hi], z - a)
                    f = factor[:, w_, a:z, h].unsqueeze(2).broadcast_to([P, z - a, (hi - lo) // (z - a)])
                    last = dve.tensor_tensor(x, x, f, ALU.mult)
                last.then_inc(scaled_ready, 1)

            def gate(g, h):
                dve.wait_ge(head_done, len(HEADS) * g + 4 * h + 4)
                dve.tensor_tensor(yg[:, h, 0:SEQ], yg[:, h, 0:SEQ], out_t[h % 2][:, :], ALU.mult).then_inc(yg_ready, 1)
                dve.wait_ge(yg_ready, (NH + 4) * g + 4 + h + 1)
                dve.sem_inc(out_free[h % 2], 1)

            def stage(st):
                h = st.head
                for t in range(TILES):
                    if h is not None and attn_kind(t)[0] in "KQ":
                        dve.wait_ge(proj_ready, TILES * h + t + 1)
                        rotate(h, t)
                    for item, g in st.items(t):
                        if item[0] == "S":
                            mask_and_top(st, g, item)
                        elif item[0] == "KT" and item[2] % 2 == 1:
                            _, s, ni = item
                            filled(dve, st, item)
                            if s == 1:
                                filled(dve, st, ("SC", 0))
                            dve.tensor_copy(keys_t[:, ni, :], bank(st, item)[:, 0:CW]).then_inc(keys_odd_ready, 1)
                            dve.wait_ge(keys_odd_ready, 4 * g + 2 * s + ni // 2 + 1)
                            free(dve, st, item)
                        elif item[0] == "SN":
                            dve.wait_ge(s_turned, 4 * g + 2 * item[1])
                            sample_top(st, g, item[1])
                        elif item[0] == "F":
                            sample_gate(g, 0)
                            get_factors(st, g)
                            for n in range(6):
                                scale(n)
                        elif item[0] == "OS" and item[1] == 1:
                            sample_gate(g, 1)
                        elif item[0] == "PT":
                            n = HEADS.index(item)
                            if n + 5 >= 6 and n + 5 < len(HEADS):
                                scale(n + 5)
                            if n % 4 == 1 and n > 4:
                                gate(g, n // 4 - 1)
                            if n == len(HEADS) - 1:
                                gate(g, NH - 1)
                    if t == 19 and h is not None:
                        sample_normalise(h, 0)
                    if t == 20 and h is not None:
                        merge_windows(h)
                    if t == 21 and h is not None:
                        sample_normalise(h, 1)

            all_groups(dve, ATTN, stage)

        @block.gpsimd
        def _(pool):
            def w_low(g, t):
                r = t % PAIR
                pool.wait_ge(whi_ready, TILES * g + t + 1)
                pool.tensor_tensor(wlo[:, r], w[:, r], whi[:, r].bitcast(F32), ALU.subtract).then_inc(wlo_ready, 1)

            for t in range(PAIR):
                w_low(0, t)
            def stage(st):
                g = st.head
                for t in range(TILES if g is not None else 0):
                    nxt = t + PAIR
                    w_low(g + nxt // TILES, nxt % TILES)
                    what = attn_kind(t)
                    if what[0] not in "KQ":
                        continue
                    n = ROPED.index(t)
                    w_ = what[1]
                    pool.wait_ge(turned_ready, 3 * len(ROPED) * g + 3 * n + 3)
                    if t == 0:
                        pool.wait_ge(masked_ready, len(SCORES) * g)
                        pool.wait_ge(s_masked, 4 * g)
                        pool.wait_ge(kv_rows_ready, 3 * NW * g)
                    elif what[0] == "K":
                        filled(pool, st, ("S", w_ - 1, NH - 1, len(UNITS[w_ - 1]) - 1))
                    elif w_:
                        filled(pool, st, ("S", w_ - 1, what[2], len(UNITS[w_ - 1]) - 1))
                    dst, new = (k[:, :], ks[:, w_, :]) if what[0] == "K" else (q[:, what[2], :], qs[:, w_, :, what[2], :])
                    d = WINDOWS[w_][1]
                    a, b = straight[:, 0:SEQ], crossed[:, 0:SEQ]
                    if d > 1:
                        dst = dst.rearrange("p (r m) -> p m r", r=d)
                        a, b = (x.rearrange("p (m r) -> p m r", r=d) for x in (a, b))
                    pool.tensor_tensor(dst, a, b, ALU.add).then_inc(qk_ready, 1)
                    a, b = straight[:, SEQ:TOK], crossed[:, SEQ:TOK]
                    if what[0] == "Q":
                        a, b = (x.rearrange("p (i t) -> p i t", i=4) for x in (a, b))
                    pool.tensor_tensor(new, a, b, ALU.add).then_inc(qk_ready, 1)

            all_groups(pool, ATTN, stage)


GT = 10
XBC = 6
HG = 8
PD = 64
GW = HG * PD
ST = 128
TAPS = 4
PRE = TAPS - 1
WIDE = SEQ + PRE + NB * (NT + PRE)
COMP = WIDE - PRE
PAR = NB * PRE + TAPS + 1
TAIL = PRE + NB * PRE


B_AT, C_AT, X_AT = 0, 5, (1, 2, 3, 4)
RUNS = ((B_AT, 1), (X_AT[0], 4), (C_AT, 1))


def ssd_columns(t, e):
    if t == B_AT:
        return 2 * INNER + e * ST
    if t == C_AT:
        return 2 * INNER + NG * ST + e * ST
    if t < XBC:
        return INNER + e * GW + X_AT.index(t) * P
    return e * GW + (t - XBC) * P


def channel(t, e):
    return ssd_columns(t, e) - INNER


SSD_AHEAD = {
    -1: [("PAR",)],
    6: [("BT",), ("BS",), ("AC",), ("AT",), ("AS",), ("X", 0), ("X", 1)],
    7: [("CB",), ("CS",), ("DEC",), ("HT", 0), ("HT", 1), ("X", 2), ("BA", 0), ("BB", 0)],
    8: [("HT", 2), ("HT", 3), ("TB",), ("HT", 4), ("HT", 5), ("ST", 0), ("YD", 0), ("BA", 1), ("BB", 1)],
    9: [("HT", 6), ("HT", 7), ("TX",), ("X", 3), ("X", 4), ("YO", 1), ("ST", 1), ("YD", 1), ("OQ",),
        ("BA", 2), ("BB", 2)],
}
SSD_BEHIND = {
    0: [("YO", 2), ("ST", 2), ("YD", 2), ("BA", 3), ("BB", 3)],
    1: [("Z", 0), ("YO", 3), ("ST", 3), ("YD", 3), ("BA", 4), ("BB", 4)],
    2: [("YO", 4), ("Z", 1), ("YD", 4), ("FS",), ("HN", 0), ("HN", 1), ("Z", 2)],
    3: [("HN", 2), ("Z", 3), ("HN", 3), ("Z", 4), ("HN", 4), ("HN", 5)],
    4: [("HN", 6), ("HN", 7)],
    5: [("YT", c) for c in range(TT)],
}
BANKS = 3
SSD = Plan(SSD_AHEAD, SSD_BEHIND, GT, BANKS, ("OQ",))
SSD_CONSTS = 7
Y_STEPS = 2 * (TT - 1)


def ssd_phase(nc, uhi, ulo, ident, w_in_dram, tables, params, states, y_dram, p_out, s_out_dram):
    conv_w, conv_b, dt_bias, a_log, d_skip, norm_w = params
    state_ssm, state_conv = states
    p_ssm, p_conv = p_out
    s_ssm, s_conv = s_out_dram
    with ExitStack() as ctx:
        m = Mem(nc, ctx, "sd")
        tri = m.sb("tri", [P, P])
        tri_s = m.sb("tri_s", [NS, NS])
        mask = m.sb("mask", [P, P])
        mask_s = m.sb("mask_s", [NS, NS])
        own = m.sb("own", [NS, NB])
        pick_f = m.sb("pick_f", [HG, HG * P])
        pick = m.sb("pick", [HG, HG * P], F32R)
        spread = m.sb("spread", [HG, 4, P])
        zero = m.sb("zero", [P, 1])
        rows = m.sb("rows", [P, 3, NG * HG])
        a_neg = m.sb("a_neg", [P, NG * HG])
        w = m.sb("w", [P, PAIR, KD * P])
        whi = m.sb("whi", [P, PAIR, KD * P], F32R)
        wlo = m.sb("wlo", [P, PAIR, KD * P], F32R)
        wd = m.sb("wd", [P, KD, NG * HG])
        wdhi = m.sb("wdhi", [P, KD, NG * HG], F32R)
        wdlo = m.sb("wdlo", [P, KD, NG * HG], F32R)
        dt_f = m.sb("dt_f", [NG * HG, TOK])
        dt = m.sb("dt", [P, TT, NG * HG])
        dta = m.sb("dta", [P, TT, NG * HG])
        sp_a = m.sb("sp_a", [P, TT, NG * HG])
        sp_b = m.sb("sp_b", [P, TT, NG * HG])
        sp_c = m.sb("sp_c", [P, TT, NG * HG])
        dt_e = m.sb("dt_e", [P, TT, HG])
        dta_e = m.sb("dta_e", [P, TT, HG])
        d_e = m.sb("d_e", [P, HG])
        acs = m.sb("acs", [P, TT, HG])
        acs_exp = m.sb("acs_exp", [P, TT, HG])
        acs_f = m.sb("acs_f", [HG, TOK])
        acs_hi = m.sb("acs_hi", [HG, TOK], F32R)
        acs_lo = m.sb("acs_lo", [HG, TOK], F32R)
        last_exp = m.sb("last_exp", [HG, NB])
        decay_rows = m.sb("decay_rows", [P, 4, NB])
        par_rows = m.sb("par_rows", [PAR, XBC * P])
        par = m.sb("par", [P, XBC, PAR])
        raw = m.sb("raw", [P, WIDE])
        conv = m.sb("conv", [P, 2, WIDE])
        tails = m.sb("tails", [P, XBC, TAIL])
        tail_rows = m.sb("tail_rows", [TAIL, XBC * P])
        xbc = m.sb("xbc", [P, XBC, TOK])
        z = m.sb("z", [P, 4, TOK])
        b_rows = m.sb("b_rows", [P, TT, ST])
        b_own = m.sb("b_own", [NS, NB, ST])
        cb = m.sb("cb", [P, TT, P])
        norm_row = m.sb("norm_row", [P, GW])
        x_rows = m.sb("x_rows", [P, TT, GW])
        x_dt = m.sb("x_dt", [P, 2, GW])
        x_end = m.sb("x_end", [P, 2, GW])
        x_d = m.sb("x_d", [P, 2, GW])
        decay = m.sb("decay", [P, 2, HG, P])
        to_end = m.sb("to_end", [P, 2, HG])
        chunk_decay = m.sb("chunk_decay", [P, 2, HG])
        state = m.sb("state", [P, GW])
        state_rows = m.sb("state_rows", [P, 4, ST])
        h0 = m.sb("h0", [P, 4, NB, ST])
        h0_t = m.sb("h0_t", [P, 2, 4 * P])
        off_t = m.sb("off_t", [P, 4 * NS])
        y = m.sb("y", [P, TT, GW])
        z_rows = m.sb("z_rows", [P, 2, GW])
        square = m.sb("square", [P, GW])
        stats = m.sb("stats", [P, 3, TT])
        proj = m.ps("proj", [P, PAIR, 2, 512])
        small = [m.ps(f"small{b}", [P, 512]) for b in range(BANKS)]
        held = m.ps("held", [P, 512])

        s = m.sem
        held_back = s("held_back")
        wd_in, consts_in, w_in, = s("wd_in"), s("consts_in"), [s(f"w_in{r}") for r in range(PAIR)]
        whi_ready, wlo_ready, proj_ready = s("whi_ready"), s("wlo_ready"), s("proj_ready")
        proj_free = [s(f"proj_free{r}") for r in range(PAIR)]
        small_ready = [s(f"small_ready{b}") for b in range(BANKS)]
        small_free = [s(f"small_free{b}") for b in range(BANKS)]
        setup = s("setup")
        setup_act = s("setup_act")
        setup_pe = s("setup_pe")
        pick_ready = s("pick_ready")
        par_in, h0_in, norm_in = s("par_in"), s("h0_in"), s("norm_in")
        slices_ready = s("slices_ready")
        par_ready, acs_ready, acs_exp_ready = s("par_ready"), s("acs_ready"), s("acs_exp_ready")
        acs_f_ready, acs_hi_ready, acs_lo_ready = s("acs_f_ready"), s("acs_hi_ready"), s("acs_lo_ready")
        last_exp_ready, decay_rows_ready = s("last_exp_ready"), s("decay_rows_ready")
        raw_ready, past_ready, tail_ready, raw_free = s("raw_ready"), s("past_ready"), s("tail_ready"), s("raw_free")
        tap0_ready, conv_ready, xbc_ready, z_ready = s("tap0_ready"), s("conv_ready"), s("xbc_ready"), s("z_ready")
        b_rows_ready, b_own_ready, cb_ready = s("b_rows_ready"), s("b_own_ready"), s("cb_ready")
        h0_t_ready, off_done, off_t_ready = s("h0_t_ready"), s("off_done"), s("off_t_ready")
        x_rows_ready, x_dt_ready, x_d_ready, x_end_ready = s("x_rows_ready"), s("x_dt_ready"), s("x_d_ready"), s("x_end_ready")
        seg_ready, decay_ready, chunk_decay_ready = s("seg_ready"), s("decay_ready"), s("chunk_decay_ready")
        to_end_ready, weights_ready = s("to_end_ready"), s("weights_ready")
        state_step, state_ready = s("state_step"), s("state_ready")
        y_step, y_ready = s("y_step"), s("y_ready")
        tails_ready, tails_stored = s("tails_ready"), s("tails_stored")
        final_ready, final_stored = s("final_ready"), s("final_stored")
        h0_scaled, h0_new, h0_stored = s("h0_scaled"), s("h0_new"), s("h0_stored")
        z_rows_ready, gated, squares, mean_ready, inv_ready, rstd_ready = \
            s("z_rows_ready"), s("gated"), s("squares"), s("mean_ready"), s("inv_ready"), s("rstd_ready")
        normed, out_ready, y_stored = s("normed"), s("out_ready"), s("y_stored")
        block = ctx.enter_context(nc.Block())
        span = [slice(c * P, c * P + ROWS[c]) for c in range(TT)]

        def bank(st, item):
            return small[st.place(item)[0]]

        def filled(eng, st, item):
            b, ahead = st.place(item)
            eng.wait_ge(small_ready[b], ahead + 1)

        def hold(eng):
            eng.sem_inc(held_back, 1)

        def free(eng, st, item):
            eng.sem_inc(small_free[st.place(item)[0]], 1)

        def heads(ap):
            return ap.rearrange("p (h d) -> p h d", h=HG)

        def per_head(ap):
            return ap.unsqueeze(2).broadcast_to([ap.shape[0], HG, PD])

        @block.sync
        def _(sp):
            def load_w(e, t, slot):
                src = w_in_dram.rearrange("(k p) n -> p k n", p=P)[:, :, bass.ds(ssd_columns(t, e), P)]
                sp.dma_start(w[:, slot].rearrange("p (k n) -> p k n", k=KD), src).then_inc(w_in[slot], 16)

            consts = ((tri[:, :], tables["tri"]), (tri_s[:, :], tables["tri_s"]), (mask[:, :], tables["mask"]),
                      (mask_s[:, :], tables["mask_ss"]), (own[:, :], tables["own"]), (pick_f[:, :], tables["pick"]),
                      (spread[:, :, :], tables["spread"]))
            assert len(consts) == SSD_CONSTS

            def stage(st):
                e, g = st.head, st.tail
                for t in range(GT):
                    if t == 0 and e is not None:
                        sp.wait_ge(par_ready, e)
                        for k, n in RUNS:
                            lo, hi, at = k * P, (k + n) * P, bass.ds(channel(k, e), n * P)
                            past = state_conv[0].rearrange("n k c -> (n k) c")[:, at]
                            sp.dma_start(par_rows[0:NB * PRE, lo:hi], past).then_inc(par_in, 16)
                            sp.dma_start(par_rows[NB * PRE:NB * PRE + TAPS, lo:hi], conv_w[0][:, at]).then_inc(par_in, 16)
                            sp.dma_start(par_rows[NB * PRE + TAPS:PAR, lo:hi], conv_b[:, at]).then_inc(par_in, 16)
                    if e is not None:
                        if st.tail is None and t == 1:
                            for dst, src in consts:
                                sp.dma_start(dst, src).then_inc(consts_in, 16)
                        sp.wait_ge(wlo_ready, GT * e + t + PAIR + 1)
                        nxt = t + 2 * PAIR
                        hold(sp)
                        load_w(e + nxt // GT, nxt % GT, t % PAIR)
                    if t == 4 and g is not None:
                        sp.wait_ge(final_ready, g + 1)
                        sp.dma_start(p_ssm[0, 0].rearrange("h p s -> (h p) s")[bass.ds(GW * g, GW)]
                                     .rearrange("(j q) s -> q j s", q=P), state_rows[:, :, :]).then_inc(final_stored, 16)
                        for j in range(4):
                            sp.wait_ge(h0_new, 8 * g + 2 * j + 2)
                            sp.dma_start(s_ssm[0].rearrange("n h p s -> (h p) n s")[bass.ds(GW * g + P * j, P)], h0[:, j]) \
                                .then_inc(h0_stored, 16)
                        sp.wait_ge(out_ready, TT * g + TT)
                        sp.dma_start(y_dram[bass.ds(4 * g, 4)].rearrange("k p t -> p k t"), z[:, :, :]).then_inc(y_stored, 16)
                    if t == 4 and e is not None:
                        sp.wait_ge(normed, TT * e)
                        sp.dma_start(norm_row[:, :], norm_w[0, bass.ds(GW * e, GW)].partition_broadcast(P)) \
                            .then_inc(norm_in, 16)
                        sp.wait_ge(h0_stored, 16 * 4 * e)
                        for j in range(4):
                            src = state_ssm[0].rearrange("n h p s -> (h p) n s")[bass.ds(GW * e + P * j, P)]
                            sp.dma_start(h0[:, j], src).then_inc(h0_in, 16)
                if e is not None:
                    sp.wait_ge(tails_ready, 2 * e + 2)
                    hold(sp)
                    for k, n in RUNS:
                        lo, hi, at = k * P, (k + n) * P, bass.ds(channel(k, e), n * P)
                        sp.dma_start(p_conv[0, 0][:, at], tail_rows[0:PRE, lo:hi]).then_inc(tails_stored, 16)
                        sp.dma_start(s_conv[0].rearrange("n k c -> (n k) c")[:, at], tail_rows[PRE:TAIL, lo:hi]) \
                            .then_inc(tails_stored, 16)

            for t in range(PAIR):
                load_w(0, t, t)
            dt_in = ((wd[:, :, :], w_in_dram.rearrange("(k p) n -> p k n", p=P)[:, :, 2 * INNER + 2 * NG * ST:]),
                     (rows[:, 0, :], bcast_rows(dt_bias)), (rows[:, 1, :], bcast_rows(a_log)),
                     (rows[:, 2, :], bcast_rows(d_skip)))
            for dst, src in dt_in:
                sp.dma_start(dst, src).then_inc(wd_in, 16)
            for t in range(PAIR):
                sp.wait_ge(wlo_ready, t + 1)
                load_w(0, PAIR + t, t)
            all_groups(sp, SSD, stage)
            sp.wait_ge(y_stored, 16 * NG)
            sp.wait_ge(h0_stored, 16 * 4 * NG)
            sp.wait_ge(final_stored, 16 * NG)
            sp.wait_ge(tails_stored, 16 * 2 * len(RUNS) * NG)
            for r in range(PAIR):
                sp.wait_ge(w_in[r], 16 * (GT * NG // PAIR + 2))

        @block.tensor
        def _(pe):
            def turn(out, ins, one):
                return pe.matmul(out, ins, one, is_transpose=True, start=True, stop=True)

            def project(e, t):
                r = t % PAIR
                pe.wait_ge(wlo_ready, GT * e + t + 1)
                pe.wait_ge(proj_free[r], GT // PAIR * e + t // PAIR)
                for kk in range(KD):
                    for a, b in ((whi, uhi), (whi, ulo), (wlo, uhi)):
                        for h in range(2):
                            last = pe.matmul(proj[:, r, h, 0:HALF], a[:, r, kk * P:(kk + 1) * P],
                                             b[:, kk, h * HALF:(h + 1) * HALF],
                                             start=(kk == 0 and a is whi and b is uhi),
                                             stop=(kk == KD - 1 and a is wlo))
                last.then_inc(proj_ready, 1)

            def item_(st, e, item):
                n, ahead = st.place(item)
                b = small[n]
                pe.wait_ge(small_free[n], ahead)
                what = item[0]
                c = item[1] if len(item) > 1 else None
                if what == "PAR":
                    pe.wait_ge(par_in, 16 * 3 * len(RUNS) * (e + 1))
                    hold(pe)
                    for j in range(XBC):
                        last = turn(b[:, j * PAR:(j + 1) * PAR], par_rows[:, j * P:(j + 1) * P], ident[0:PAR, 0:PAR])
                elif what == "AC":
                    pe.wait_ge(slices_ready, 3 * e + 3)
                    pe.wait_ge(consts_in, 16 * SSD_CONSTS)
                    for i in range(TT - 1):
                        last = pe.matmul(b[:, i * HG:(i + 1) * HG], tri[:, :], dta_e[:, i, :], start=True, stop=True)
                    last = pe.matmul(b[0:NS, (TT - 1) * HG:TT * HG], tri_s[:, :], dta_e[0:NS, TT - 1, :],
                                     start=True, stop=True)
                elif what == "AT":
                    for i in range(TT - 1):
                        last = pe.matmul(b[0:HG, span[i]], dta_e[:, i, :], tri[:, :], start=True, stop=True)
                elif what == "AS":
                    hold(pe)
                    last = pe.matmul(b[0:HG, 0:NS], dta_e[0:NS, TT - 1, :], tri_s[:, :], start=True, stop=True)
                elif what == "BT":
                    pe.wait_ge(xbc_ready, XBC * e + B_AT + 1)
                    for i in range(TT - 1):
                        last = turn(b[:, i * ST:(i + 1) * ST], xbc[:, B_AT, span[i]], ident[:, :])
                elif what == "BS":
                    last = turn(b[0:NS, 0:ST], xbc[:, B_AT, span[TT - 1]], ident[:, :])
                elif what == "CB":
                    pe.wait_ge(xbc_ready, XBC * e + C_AT + 1)
                    for i in range(TT - 1):
                        last = pe.matmul(b[:, i * P:(i + 1) * P], xbc[:, B_AT, span[i]], xbc[:, C_AT, span[i]],
                                         start=True, stop=True)
                elif what == "CS":
                    hold(pe)
                    last = pe.matmul(b[0:NS, 0:NS], xbc[:, B_AT, span[TT - 1]], xbc[:, C_AT, span[TT - 1]],
                                     start=True, stop=True)
                elif what == "DEC":
                    pe.wait_ge(last_exp_ready, e + 1)
                    for j in range(4):
                        last = pe.matmul(b[:, j * NB:(j + 1) * NB], spread[:, j, :], last_exp[:, :],
                                         start=True, stop=True)
                elif what == "HT":
                    pe.wait_ge(h0_in, 16 * 4 * (e + 1))
                    for i in range(4):
                        last = turn(b[:, i * P:(i + 1) * P], h0[:, c // 2, 4 * (c % 2) + i, :], ident[:, :])
                elif what == "TB":
                    pe.wait_ge(tail_ready, 2 * XBC * e + 8)
                    for j in range(4):
                        last = turn(b[0:TAIL, j * P:(j + 1) * P], tails[:, j, :], ident[:, :])
                elif what == "TX":
                    pe.wait_ge(tail_ready, 2 * XBC * e + 2 * XBC)
                    for j in range(2):
                        last = turn(b[0:TAIL, j * P:(j + 1) * P], tails[:, 4 + j, :], ident[:, :])
                elif what == "X":
                    pe.wait_ge(xbc_ready, XBC * e + X_AT[-1] + 1)
                    for j in range(4):
                        last = turn(b[0:ROWS[c], j * P:(j + 1) * P], xbc[:, X_AT[j], span[c]], ident[:, :])
                elif what in ("BA", "BB"):
                    pe.wait_ge(acs_lo_ready, e + 1)
                    pe.wait_ge(pick_ready, 1)
                    r = ROWS[c]
                    for i in range(4):
                        h = i + (4 if what == "BB" else 0)
                        pe.matmul(b[0:P, i * r:(i + 1) * r], pick[:, h * P:(h + 1) * P], acs_hi[:, span[c]],
                                  start=True, stop=False)
                        last = pe.matmul(b[0:P, i * r:(i + 1) * r], pick[:, h * P:(h + 1) * P], acs_lo[:, span[c]],
                                         start=False, stop=True)
                elif what == "ST":
                    pe.wait_ge(x_end_ready, TT * e + c + 1)
                    pe.wait_ge(b_rows_ready, 2 * e + 1)
                    last = pe.matmul(b[:, :], b_rows[:, c, :], x_end[:, c % 2, :], start=True, stop=True)
                elif what == "YD":
                    pe.wait_ge(weights_ready, TT * e + c + 1)
                    pe.wait_ge(x_dt_ready, TT * e + c + 1)
                    r = ROWS[c]
                    if r < P:
                        hold(pe)
                    for h in range(HG):
                        last = pe.matmul(b[0:r, h * PD:(h + 1) * PD], decay[0:r, c % 2, h, 0:r],
                                         x_dt[0:r, c % 2, h * PD:(h + 1) * PD], start=True, stop=True)
                elif what == "YO":
                    if c < TT - 1:
                        pe.wait_ge(state_ready, 4 * e + c)
                        last = pe.matmul(b[:, :], xbc[:, C_AT, span[c]], state[:, :], start=True, stop=True)
                    else:
                        pe.wait_ge(off_t_ready, e + 1)
                        for j in range(4):
                            last = turn(b[0:NS, j * P:(j + 1) * P], off_t[:, j * NS:(j + 1) * NS], ident[:, :])
                elif what == "FS":
                    pe.wait_ge(state_ready, 4 * e + 4)
                    for j in range(4):
                        last = turn(b[:, j * P:(j + 1) * P], state[:, j * P:(j + 1) * P], ident[:, :])
                elif what == "HN":
                    pe.wait_ge(x_end_ready, TT * e + TT)
                    pe.wait_ge(b_own_ready, e + 1)
                    j, half = c // 2, c % 2
                    last = pe.matmul(b[:, :], x_end[0:NS, 0, j * P:(j + 1) * P],
                                     b_own[:, 4 * half:4 * half + 4, :].rearrange("p n s -> p (n s)"),
                                     start=True, stop=True)
                elif what == "Z":
                    pe.wait_ge(z_ready, 4 * e + 4)
                    for j in range(4):
                        last = turn(b[0:ROWS[c], j * P:(j + 1) * P], z[:, j, span[c]], ident[:, :])
                elif what == "YT":
                    pe.wait_ge(normed, TT * e + c + 1)
                    r = ROWS[c]
                    if r < P:
                        hold(pe)
                    for j in range(4):
                        last = turn(b[:, j * r:(j + 1) * r], y[0:r, c, j * P:(j + 1) * P], ident[0:r, 0:r])
                last.then_inc(small_ready[n], 1)

            def from_old(e, i):
                pe.wait_ge(h0_t_ready, 8 * e + i + 1)
                if i == 0:
                    pe.wait_ge(off_t_ready, e)
                for n in range(4):
                    seq = 4 * (i % 2) + n
                    at = (i // 2) * NS + NT * seq
                    last = pe.matmul(held[:, at:at + NT], h0_t[:, i % 2, n * P:(n + 1) * P],
                                     xbc[:, C_AT, SEQ + NT * seq:SEQ + NT * seq + NT], start=True, stop=True)
                last.then_inc(off_done, 1)

            def all_dt():
                pe.wait_ge(setup, 2)
                for kk in range(KD):
                    for a, b in ((wdhi, uhi), (wdhi, ulo), (wdlo, uhi)):
                        for h in range(2):
                            last = pe.matmul(small[1 + h][0:NG * HG, 0:HALF], a[:, kk, :], b[:, kk, h * HALF:(h + 1) * HALF],
                                             start=(kk == 0 and a is wdhi and b is uhi),
                                             stop=(kk == KD - 1 and a is wdlo))
                last.then_inc(setup_pe, 1)

            def turn_dt():
                pe.wait_ge(setup_act, 2)
                for c in range(TT):
                    last = turn(held[0:ROWS[c], c * NG * HG:(c + 1) * NG * HG], dt_f[:, span[c]],
                                ident[0:NG * HG, 0:NG * HG])
                last.then_inc(setup_pe, 1)

            def stage(st):
                for t in range(GT):
                    if st.head is not None:
                        project(st.head, t)
                    if st.tail is None and t == 0:
                        all_dt()
                    if st.tail is None and t == 1:
                        turn_dt()
                    for item, e in (st.items(-1) if t == 0 else []) + st.items(t):
                        if item == ("OQ",):
                            from_old(e, 7)
                            continue
                        item_(st, e, item)
                        if item[0] == "HT" and item[1] >= 1:
                            from_old(e, item[1] - 1)

            all_groups(pe, SSD, stage)

        @block.scalar
        def _(act):
            def w_high(e, t):
                act.wait_ge(w_in[t % PAIR], GT // PAIR * 16 * e + 16 * (t // PAIR) + 16)
                act.activation(whi[:, t % PAIR], w[:, t % PAIR], ACT.Copy).then_inc(whi_ready, 1)

            def copied(st, item, dst, src, signal, value):
                filled(act, st, item)
                act.activation(dst, src, ACT.Copy).then_inc(signal, 1)
                act.wait_ge(signal, value)
                free(act, st, item)

            def convolved(e, t):
                x = proj[:, t % PAIR]
                act.wait_ge(raw_free, XBC * e + t)
                act.activation(raw[:, PRE:PRE + HALF], x[:, 0, 0:HALF], ACT.Copy)
                act.activation(raw[:, PRE + HALF:PRE + SEQ], x[:, 1, 0:SEQ - HALF], ACT.Copy)
                new = raw[:, PRE + SEQ:WIDE].rearrange("p (n k) -> p n k", n=NB)[:, :, PRE:PRE + NT]
                act.activation(new, x[:, 1, SEQ - HALF:HALF].rearrange("p (n k) -> p n k", n=NB), ACT.Copy) \
                    .then_inc(raw_ready, 1)
                act.wait_ge(raw_ready, XBC * e + t + 1)
                act.sem_inc(proj_free[t % PAIR], 1)
                act.wait_ge(past_ready, XBC * e + t + 1)
                act.activation(conv[:, 0, 0:COMP], raw[:, 0:COMP], ACT.Identity, scale=par[:, t, NB * PRE:NB * PRE + 1],
                               bias=par[:, t, PAR - 1:PAR]).then_inc(tap0_ready, 1)

            def silu(e, t):
                act.wait_ge(conv_ready, 3 * (XBC * e + t) + 3)
                act.activation(xbc[:, t, 0:SEQ], conv[:, 1, 0:SEQ], ACT.Silu)
                runs = conv[:, 1, SEQ + PRE:WIDE].rearrange("p (n k) -> p n k", n=NB)
                act.activation(xbc[:, t, SEQ:TOK].rearrange("p (n k) -> p n k", n=NB), runs[:, :, 0:NT], ACT.Silu) \
                    .then_inc(xbc_ready, 1)

            def all_dt():
                act.wait_ge(setup_pe, 1)
                for h in range(2):
                    last = act.activation(dt_f[:, h * HALF:(h + 1) * HALF], small[1 + h][0:NG * HG, 0:HALF], ACT.Copy)
                last.then_inc(setup_act, 1)

            def soften():
                act.activation(a_neg[:, :], rows[:, 1, :], ACT.Exp).then_inc(setup_act, 1)
                act.wait_ge(setup, 7)
                act.activation(sp_b[:, :, :], sp_b[:, :, :], ACT.Exp).then_inc(setup_act, 1)
                act.wait_ge(consts_in, 16 * SSD_CONSTS)
                act.activation(pick[:, :], pick_f[:, :], ACT.Copy).then_inc(pick_ready, 1)

            for t in range(PAIR):
                w_high(0, t)
            act.wait_ge(wd_in, 16 * 4)
            act.activation(wdhi[:, :, :], wd[:, :, :], ACT.Copy).then_inc(setup_act, 1)

            def stage(st):
                h = st.head
                for t in range(-1, GT):
                    if t >= 0 and h is not None:
                        act.wait_ge(proj_ready, GT * h + t + 1)
                        nxt = t + PAIR
                        w_high(h + nxt // GT, nxt % GT)
                    if st.tail is None and t == 0:
                        all_dt()
                    if t >= XBC and h is not None:
                        if t == XBC:
                            act.wait_ge(y_stored, 16 * h)
                        act.activation(two(z[:, t - XBC, :]), halves(proj[:, t % PAIR]), ACT.Copy).then_inc(z_ready, 1)
                        act.wait_ge(z_ready, 4 * h + t - XBC + 1)
                        act.sem_inc(proj_free[t % PAIR], 1)
                    for item, e in st.items(t):
                        what = item[0]
                        c = item[1] if len(item) > 1 else None
                        b = bank(st, item) if what != "OQ" else None
                        if what == "PAR":
                            copied(st, item, par[:, :, :].rearrange("p t k -> p (t k)"), b[:, 0:XBC * PAR], par_ready, e + 1)
                        elif what == "AC":
                            filled(act, st, item)
                            act.wait_ge(y_ready, TT * e)
                            act.activation(acs[:, 0:TT - 1, :].rearrange("p c h -> p (c h)"), b[:, 0:(TT - 1) * HG], ACT.Copy)
                            act.activation(acs[0:NS, TT - 1, :], b[0:NS, (TT - 1) * HG:TT * HG], ACT.Copy)
                            act.activation(acs_exp[:, 0:TT - 1, :].rearrange("p c h -> p (c h)"), b[:, 0:(TT - 1) * HG], ACT.Exp)
                            act.activation(acs_exp[0:NS, TT - 1, :], b[0:NS, (TT - 1) * HG:TT * HG], ACT.Exp) \
                                .then_inc(acs_ready, 1)
                            act.wait_ge(acs_ready, e + 1)
                            free(act, st, item)
                        elif what == "AT":
                            act.wait_ge(acs_lo_ready, e)
                            copied(st, item, acs_f[:, 0:SEQ], b[0:HG, :], acs_f_ready, 2 * e + 1)
                        elif what == "AS":
                            filled(act, st, item)
                            act.activation(last_exp[:, :], b[0:HG, 0:NS].rearrange("p (n t) -> p n t", t=NT)[:, :, NT - 1],
                                           ACT.Exp).then_inc(last_exp_ready, 1)
                            copied(st, item, acs_f[:, SEQ:TOK], b[0:HG, 0:NS], acs_f_ready, 2 * e + 2)
                            act.activation(acs_hi[:, :], acs_f[:, :], ACT.Copy).then_inc(acs_hi_ready, 1)
                        elif what == "BT":
                            copied(st, item, b_rows[:, 0:TT - 1, :].rearrange("p c s -> p (c s)"), b[:, :], b_rows_ready, 2 * e + 1)
                        elif what == "BS":
                            copied(st, item, b_rows[0:NS, TT - 1, :], b[0:NS, 0:ST], b_rows_ready, 2 * e + 2)
                        elif what == "CB":
                            copied(st, item, cb[:, 0:TT - 1, :].rearrange("p c i -> p (c i)"), b[:, :], cb_ready, 2 * e + 1)
                        elif what == "CS":
                            copied(st, item, cb[0:NS, TT - 1, 0:NS], b[0:NS, 0:NS], cb_ready, 2 * e + 2)
                        elif what == "DEC":
                            act.wait_ge(h0_scaled, 8 * e)
                            copied(st, item, decay_rows[:, :, :].rearrange("p j n -> p (j n)"), b[:, 0:4 * NB],
                                   decay_rows_ready, e + 1)
                        elif what == "HT":
                            if c >= 2:
                                act.wait_ge(off_done, 8 * e + c - 1)
                            copied(st, item, h0_t[:, c % 2, :], b[:, :], h0_t_ready, 8 * e + c + 1)
                        elif what == "TB":
                            act.wait_ge(tails_stored, 16 * 2 * len(RUNS) * e)
                            copied(st, item, tail_rows[:, 0:4 * P], b[0:TAIL, :], tails_ready, 2 * e + 1)
                        elif what == "TX":
                            copied(st, item, tail_rows[:, 4 * P:], b[0:TAIL, 0:2 * P], tails_ready, 2 * e + 2)
                        elif what == "X":
                            act.wait_ge(x_d_ready, TT * e)
                            copied(st, item, x_rows[0:ROWS[c], c, :], b[0:ROWS[c], :], x_rows_ready, TT * e + c + 1)
                        elif what == "BB":
                            r = ROWS[c]
                            act.wait_ge(seg_ready, TT * e + c + 1)
                            if c < TT - 1:
                                for i, it in enumerate((("BA", c), ("BB", c))):
                                    last = act.activation(chunk_decay[:, c % 2, 4 * i:4 * i + 4],
                                                          bank(st, it)[:, :].rearrange("p (h i) -> p h i", h=4)[:, :, P - 1],
                                                          ACT.Exp)
                                last.then_inc(chunk_decay_ready, 1)
                            act.activation(decay[0:r, c % 2, :, 0:r], decay[0:r, c % 2, :, 0:r], ACT.Exp) \
                                .then_inc(decay_ready, 1)
                        elif what == "OQ":
                            act.wait_ge(off_done, 8 * e + 8)
                            act.activation(off_t[:, :], held[:, 0:4 * NS], ACT.Copy).then_inc(off_t_ready, 1)
                        elif what == "FS":
                            act.wait_ge(final_stored, 16 * e)
                            copied(st, item, state_rows[:, :, :].rearrange("p j s -> p (j s)"), b[:, :], final_ready, e + 1)
                        elif what == "Z":
                            r = ROWS[c]
                            filled(act, st, item)
                            act.wait_ge(gated, TT * e + max(c - 1, 0))
                            act.activation(z_rows[0:r, c % 2, :], b[0:r, :], ACT.Silu).then_inc(z_rows_ready, 1)
                            act.wait_ge(z_rows_ready, TT * e + c + 1)
                            free(act, st, item)
                            act.wait_ge(gated, TT * e + c + 1)
                            act.wait_ge(squares, TT * e + c)
                            act.activation(square[0:r, :], y[0:r, c, :], ACT.Square, accum_out=stats[0:r, 0, c:c + 1]) \
                                .then_inc(squares, 1)
                            if c == TT - 1:
                                act.wait_ge(inv_ready, e + 1)
                                act.activation(stats[:, 2, :], stats[:, 1, :], ACT.Sqrt).then_inc(rstd_ready, 1)
                        elif what == "YT":
                            r = ROWS[c]
                            copied(st, item, z[:, :, span[c]], b[:, 0:4 * r].rearrange("p (j t) -> p j t", j=4),
                                   out_ready, TT * e + c + 1)
                    if 0 <= t < XBC and h is not None:
                        if t == 0:
                            act.wait_ge(x_rows_ready, TT * h)
                            act.wait_ge(off_done, 8 * h)
                        convolved(h, t)
                        if t >= 1:
                            silu(h, t - 1)
                        if st.tail is None and t == 1:
                            soften()
                    if t == XBC and h is not None:
                        if st.tail is not None:
                            filled(act, st, ("YO", 3))
                        silu(h, XBC - 1)

            all_groups(act, SSD, stage)

        @block.vector
        def _(dve):
            steps = 0

            def then(ins):
                nonlocal steps
                ins.then_inc(setup, 1)
                steps += 1
                dve.wait_ge(setup, steps)

            then(dve.memset(raw[:, :], 0.0))
            dve.wait_ge(setup_act, 1)
            then(dve.tensor_tensor(wdlo[:, :, :], wd[:, :, :], wdhi[:, :, :].bitcast(F32), ALU.subtract))

            def soften():
                dve.wait_ge(setup_pe, 2)
                n = NG * HG
                then(dve.memset(sp_a[:, :, :], 0.0))
                bias = rows[:, 0, :].unsqueeze(1).broadcast_to([P, TT - 1, n])
                dve.tensor_tensor(sp_a[:, 0:TT - 1, :], held[:, 0:(TT - 1) * n].rearrange("p (c h) -> p c h", h=n),
                                  bias, ALU.add)
                then(dve.tensor_tensor(sp_a[0:NS, TT - 1, :], held[0:NS, (TT - 1) * n:TT * n], rows[0:NS, 0, :],
                                       ALU.add))
                a_, b_, c_ = (x[:, :, :] for x in (sp_a, sp_b, sp_c))
                then(dve.tensor_scalar(b_, a_, -1.0, None, ALU.mult))
                then(dve.tensor_tensor(b_, a_, b_, ALU.min))
                then(dve.tensor_scalar(a_, a_, 0.0, None, ALU.max))
                dve.wait_ge(setup_act, 4)
                then(dve.tensor_scalar(c_, b_, 2.0, None, ALU.add))
                then(dve.reciprocal(c_, c_))
                then(dve.tensor_tensor(b_, b_, c_, ALU.mult))
                then(dve.tensor_tensor(c_, b_, b_, ALU.mult))
                poly = dt[:, :, :]
                then(dve.tensor_scalar(poly, c_, 1.0 / 19, 1.0 / 17, ALU.mult, ALU.add))
                for k in (15, 13, 11, 9, 7, 5, 3, 1):
                    then(dve.tensor_tensor(poly, poly, c_, ALU.mult))
                    then(dve.tensor_scalar(poly, poly, 1.0 / k, None, ALU.add))
                then(dve.tensor_tensor(poly, poly, b_, ALU.mult))
                then(dve.scalar_tensor_tensor(out=poly, in0=poly, scalar=2.0, in1=a_, op0=ALU.mult, op1=ALU.add))
                dve.wait_ge(setup_act, 3)
                then(dve.tensor_scalar(a_neg[:, :], a_neg[:, :], -1.0, None, ALU.mult))
                then(dve.tensor_tensor(dta[:, :, :], poly, a_neg[:, :].unsqueeze(1).broadcast_to([P, TT, n]), ALU.mult))
                then(dve.memset(stats[:, :, :], 1.0))

            def taps(e, t):
                dve.wait_ge(tap0_ready, XBC * e + t + 1)
                dve.wait_ge(xbc_ready, XBC * e + t)
                at = 3 * (XBC * e + t)
                for k in range(1, TAPS):
                    dve.scalar_tensor_tensor(out=conv[:, k % 2, 0:COMP], in0=raw[:, k:k + COMP],
                                             scalar=par[:, t, NB * PRE + k:NB * PRE + k + 1],
                                             in1=conv[:, (k - 1) % 2, 0:COMP], op0=ALU.mult, op1=ALU.add) \
                        .then_inc(conv_ready, 1)
                    dve.wait_ge(conv_ready, at + k)
                dve.wait_ge(tail_ready, 2 * (XBC * e + t) + 2)
                dve.sem_inc(raw_free, 1)

            def stage(st):
                for t in range(-1, GT):
                    if t == 4 and st.head is not None:
                        e = st.head
                        cols = bass.ds(HG * e, HG)
                        dve.wait_ge(x_d_ready, TT * e)
                        dve.wait_ge(acs_f_ready, 2 * e)
                        dve.tensor_copy(dt_e[:, :, :], dt[:, :, cols]).then_inc(slices_ready, 1)
                        dve.tensor_copy(dta_e[:, :, :], dta[:, :, cols]).then_inc(slices_ready, 1)
                        dve.tensor_copy(d_e[:, :], rows[:, 2, cols]).then_inc(slices_ready, 1)
                    for item, e in st.items(t):
                        what = item[0]
                        c = item[1] if len(item) > 1 else None
                        b = bank(st, item) if what != "OQ" else None
                        if what == "AS":
                            dve.wait_ge(acs_hi_ready, e + 1)
                            dve.tensor_tensor(acs_lo[:, :], acs_f[:, :], acs_hi[:, :].bitcast(F32), ALU.subtract) \
                                .then_inc(acs_lo_ready, 1)
                        elif what == "BS":
                            dve.wait_ge(b_rows_ready, 2 * e + 2)
                            dve.wait_ge(consts_in, 16 * SSD_CONSTS)
                            dve.tensor_tensor(b_own[:, :, :], b_rows[0:NS, TT - 1, :].unsqueeze(1).broadcast_to([NS, NB, ST]),
                                              own[:, :].unsqueeze(2).broadcast_to([NS, NB, ST]), ALU.mult) \
                                .then_inc(b_own_ready, 1)
                        elif what in ("BA", "BB"):
                            r = ROWS[c]
                            filled(dve, st, item)
                            dve.wait_ge(consts_in, 16 * SSD_CONSTS)
                            dve.wait_ge(acs_ready, e + 1)
                            for i in range(4):
                                h = i + (4 if what == "BB" else 0)
                                last = dve.scalar_tensor_tensor(
                                    out=decay[0:r, c % 2, h, 0:r], in0=b[0:r, i * r:(i + 1) * r],
                                    scalar=acs[0:r, c, h:h + 1], in1=(mask if c < TT - 1 else mask_s)[0:r, 0:r],
                                    op0=ALU.subtract, op1=ALU.add)
                            if what == "BB":
                                last.then_inc(seg_ready, 1)
                                dve.wait_ge(seg_ready, TT * e + c + 1)
                                if c < TT - 1:
                                    dve.wait_ge(chunk_decay_ready, 4 * e + c + 1)
                                free(dve, st, ("BA", c))
                                free(dve, st, ("BB", c))
                                dve.wait_ge(decay_ready, TT * e + c + 1)
                                if c < TT - 1:
                                    dve.tensor_copy(to_end[:, c % 2, :], decay[:, c % 2, :, P - 1]) \
                                        .then_inc(to_end_ready, 1)
                                else:
                                    dve.tensor_reduce(to_end[0:NS, c % 2, :],
                                                      decay[0:NS, c % 2, :, NT - 1:NS:NT], AX, ALU.add) \
                                        .then_inc(to_end_ready, 1)
                                dve.wait_ge(to_end_ready, TT * e + c + 1)
                                dve.wait_ge(cb_ready, 2 * e + (1 if c < TT - 1 else 2))
                                dve.tensor_tensor(decay[0:r, c % 2, :, 0:r], decay[0:r, c % 2, :, 0:r],
                                                  cb[0:r, c, 0:r].unsqueeze(1).broadcast_to([r, HG, r]), ALU.mult) \
                                    .then_inc(weights_ready, 1)
                        elif what == "ST":
                            filled(dve, st, item)
                            if c == 0:
                                dve.tensor_copy(state[:, :], b[:, :]).then_inc(state_ready, 1)
                            else:
                                dve.wait_ge(chunk_decay_ready, 4 * e + c + 1)
                                dve.tensor_tensor(heads(state[:, :]), heads(state[:, :]),
                                                  per_head(chunk_decay[:, c % 2, :]), ALU.mult).then_inc(state_step, 1)
                                dve.wait_ge(state_step, 3 * e + c)
                                dve.tensor_tensor(state[:, :], state[:, :], b[:, :], ALU.add).then_inc(state_ready, 1)
                            dve.wait_ge(state_ready, 4 * e + c + 1)
                            free(dve, st, item)
                        elif what == "YO":
                            r = ROWS[c]
                            filled(dve, st, item)
                            dve.tensor_tensor(heads(y[0:r, c, :]), heads(b[0:r, :]), per_head(acs_exp[0:r, c, :]),
                                              ALU.mult).then_inc(y_step, 1)
                            dve.wait_ge(y_step, Y_STEPS * e + 2 * c - 1)
                            free(dve, st, item)
                        elif what == "YD":
                            r = ROWS[c]
                            filled(dve, st, item)
                            dve.wait_ge(x_d_ready, TT * e + c + 1)
                            if c:
                                dve.tensor_tensor(y[0:r, c, :], y[0:r, c, :], b[0:r, :], ALU.add).then_inc(y_step, 1)
                                dve.wait_ge(y_step, Y_STEPS * e + 2 * c)
                                free(dve, st, item)
                                dve.tensor_tensor(y[0:r, c, :], y[0:r, c, :], x_d[0:r, c % 2, :], ALU.add) \
                                    .then_inc(y_ready, 1)
                            else:
                                dve.tensor_tensor(y[0:r, c, :], b[0:r, :], x_d[0:r, c % 2, :], ALU.add) \
                                    .then_inc(y_ready, 1)
                                dve.wait_ge(y_ready, TT * e + 1)
                                free(dve, st, item)
                        elif what == "HN":
                            j, half = c // 2, c % 2
                            filled(dve, st, item)
                            dve.wait_ge(h0_scaled, 8 * e + c + 1)
                            x = h0[:, j, 4 * half:4 * half + 4, :].rearrange("p n s -> p (n s)")
                            dve.tensor_tensor(x, x, b[:, :], ALU.add).then_inc(h0_new, 1)
                            dve.wait_ge(h0_new, 8 * e + c + 1)
                            free(dve, st, item)
                        elif what == "Z":
                            r = ROWS[c]
                            dve.wait_ge(z_rows_ready, TT * e + c + 1)
                            dve.wait_ge(y_ready, TT * e + c + 1)
                            dve.tensor_tensor(y[0:r, c, :], y[0:r, c, :], z_rows[0:r, c % 2, :], ALU.mult) \
                                .then_inc(gated, 1)
                            if c == TT - 1:
                                dve.wait_ge(squares, TT * (e + 1))
                                dve.tensor_scalar(stats[:, 1, :], stats[:, 0, :], 1.0 / GW, EPS, ALU.mult, ALU.add) \
                                    .then_inc(mean_ready, 1)
                                dve.wait_ge(mean_ready, e + 1)
                                dve.reciprocal(stats[:, 1, :], stats[:, 1, :]).then_inc(inv_ready, 1)
                    if t == 4 and st.tail is not None:
                        e = st.tail
                        dve.wait_ge(rstd_ready, e + 1)
                        dve.wait_ge(norm_in, 16 * (e + 1))
                        for c, r in enumerate(ROWS):
                            dve.scalar_tensor_tensor(out=y[0:r, c, :], in0=y[0:r, c, :], scalar=stats[0:r, 2, c:c + 1],
                                                     in1=norm_row[0:r, :], op0=ALU.mult, op1=ALU.mult).then_inc(normed, 1)
                    if 0 <= t < XBC and st.head is not None:
                        taps(st.head, t)
                    if st.tail is None and t == 1:
                        soften()

            all_groups(dve, SSD, stage)

        @block.gpsimd
        def _(pool):
            def w_low(e, t):
                r = t % PAIR
                pool.wait_ge(whi_ready, GT * e + t + 1)
                pool.tensor_tensor(wlo[:, r], w[:, r], whi[:, r].bitcast(F32), ALU.subtract).then_inc(wlo_ready, 1)

            for t in range(PAIR):
                w_low(0, t)
            pool.wait_ge(setup, 1)
            def stage(st):
                for t in range(-1, GT):
                    h = st.head
                    if t >= 0 and h is not None:
                        nxt = t + PAIR
                        w_low(h + nxt // GT, nxt % GT)
                    for item, e in st.items(t):
                        if item[0] == "BA":
                            c = item[1]
                            r = ROWS[c]
                            pool.wait_ge(x_rows_ready, TT * e + c + 1)
                            pool.wait_ge(slices_ready, 3 * e + 3)
                            pool.wait_ge(y_ready, TT * e + max(c - 1, 0))
                            pool.tensor_tensor(heads(x_dt[0:r, c % 2, :]), heads(x_rows[0:r, c, :]), per_head(dt_e[0:r, c, :]),
                                               ALU.mult).then_inc(x_dt_ready, 1)
                            pool.tensor_tensor(heads(x_d[0:r, c % 2, :]), heads(x_rows[0:r, c, :]), per_head(d_e[0:r, :]),
                                               ALU.mult).then_inc(x_d_ready, 1)
                        elif item[0] == "BB":
                            c = item[1]
                            r = ROWS[c]
                            pool.wait_ge(x_dt_ready, TT * e + c + 1)
                            pool.wait_ge(to_end_ready, TT * e + c + 1)
                            if c >= 2:
                                pool.wait_ge(state_ready, 4 * e + c - 1)
                            pool.tensor_tensor(heads(x_end[0:r, c % 2, :]), heads(x_dt[0:r, c % 2, :]),
                                               per_head(to_end[0:r, c % 2, :]), ALU.mult).then_inc(x_end_ready, 1)
                        elif item[0] == "HN":
                            c = item[1]
                            j, half = c // 2, c % 2
                            if c == 0:
                                pool.wait_ge(decay_rows_ready, e + 1)
                                pool.wait_ge(h0_t_ready, 8 * e + 8)
                            x = h0[:, j, 4 * half:4 * half + 4, :]
                            pool.tensor_tensor(x, x, decay_rows[:, j, 4 * half:4 * half + 4].unsqueeze(2)
                                               .broadcast_to([P, 4, ST]), ALU.mult).then_inc(h0_scaled, 1)
                    if 0 <= t < XBC and h is not None:
                        pool.wait_ge(raw_ready, XBC * h + t + 1)
                        if t == 0:
                            pool.wait_ge(par_ready, h + 1)
                            pool.wait_ge(tails_ready, 2 * h)
                        hold(pool)
                        runs = raw[:, PRE + SEQ:WIDE].rearrange("p (n k) -> p n k", n=NB)
                        pool.tensor_copy(runs[:, :, 0:PRE], par[:, t, 0:NB * PRE].rearrange("p (n k) -> p n k", n=NB)) \
                            .then_inc(past_ready, 1)
                        pool.tensor_copy(tails[:, t, 0:PRE], raw[:, SEQ:SEQ + PRE]).then_inc(tail_ready, 1)
                        pool.tensor_copy(tails[:, t, PRE:TAIL].rearrange("p (n k) -> p n k", n=NB), runs[:, :, NT:NT + PRE]) \
                            .then_inc(tail_ready, 1)

            all_groups(pool, SSD, stage)


def load_phase(nc, ident, ident_dram):
    with ExitStack() as ctx:
        m = Mem(nc, ctx, "ld")
        ident_in = m.sem("ident_in")
        block = ctx.enter_context(nc.Block())

        @block.sync
        def _(sp):
            sp.dma_start(ident[:, :], ident_dram).then_inc(ident_in, 16)
            sp.wait_ge(ident_in, 16)


def build(nc, x, t, out, scratch):
    y_dram, h_dram, hs_dram = scratch
    pre, post = x["norm_pre"], x["norm_post"]
    ssd_params = (x["ssd_conv_w"], x["ssd_conv_b"], x["ssd_dt_bias"][0], x["ssd_a_log"][0], x["ssd_d"][0], x["ssd_norm_w"])
    source = (x["x_prompt"][0], x["x_sample"].rearrange("n t d -> (n t) d"))
    target = (out["y_prompt"][0], out["y_sample"].rearrange("n t d -> (n t) d"))
    windows = ("w128", "w512", "w2048")
    with nc.sbuf_tensor("ident", [P, P], F32) as ident, \
            nc.sbuf_tensor("uhi", [P, KD, TOK], F32R) as uhi, nc.sbuf_tensor("ulo", [P, KD, TOK], F32R) as ulo:
        with nc.cleanup_on_exit():
            load_phase(nc, ident, t["ident"])
            with nc.sbuf_tensor("x0", [P, TT, D], F32) as xt:
                norm_phase(nc, "n0", xt, ident, uhi, ulo, None, pre[0], source, None)
        with nc.cleanup_on_exit():
            attention_phase(nc, uhi, ulo, ident, x["attn_w_in"][0], t, [x["cache_kv_" + w] for w in windows], y_dram,
                            [out["p_kv_" + w][0] for w in windows], [out["s_kv_" + w] for w in windows])
        with nc.cleanup_on_exit():
            with nc.sbuf_tensor("x1", [P, TT, D], F32) as xt, nc.sbuf_tensor("yo1", [P, KD, TOK], F32) as yo:
                out_phase(nc, "o1", x["attn_w_out"][0], y_dram, yo, xt, source)
                norm_phase(nc, "n1", xt, ident, uhi, ulo, post[0], pre[1], yo, (h_dram, hs_dram))
        with nc.cleanup_on_exit():
            ssd_phase(nc, uhi, ulo, ident, x["ssd_w_in"][0], t, ssd_params, (x["state_ssm"], x["state_conv"]), y_dram,
                      (out["p_ssm"], out["p_conv"]), (out["s_ssm"], out["s_conv"]))
        with nc.cleanup_on_exit():
            with nc.sbuf_tensor("x2", [P, TT, D], F32) as xt, nc.sbuf_tensor("yo2", [P, KD, TOK], F32) as yo:
                out_phase(nc, "o2", x["ssd_w_out"][0], y_dram, yo, xt, (h_dram, hs_dram))
                norm_phase(nc, "n2", xt, ident, None, None, post[1], None, yo, target)


def tables():
    half = HD // 2
    inv = (np.float32(10000.0) ** (-np.arange(half, dtype=np.float32) / np.float32(half))).astype(np.float32)
    pos = np.concatenate([np.arange(SEQ), np.tile(PAST + np.arange(NT), NB)]).astype(np.float32)
    angle = (pos[None, :] * inv[:, None]).astype(np.float32)
    cos, sin = np.cos(angle), np.sin(angle)

    def z(ok):
        return np.where(ok, 0.0, BIG).astype(np.float32)

    def ones(ok):
        return ok.astype(np.float32)

    i, j = np.arange(P)[:, None], np.arange(P)[None, :]
    masks = np.stack([z(j >= i), z(j <= i), z((j // 32 == i // 32) & (j % 32 <= i % 32))], 1)
    seq, token = i // 32, i % 4
    cached = np.concatenate([j >= token, (np.arange(2 * P)[None, :] % 4) == token,
                             (np.arange(64)[None, :] // 16) == token], 1)
    new, new_token = np.arange(NS)[None, :] // NT, np.arange(NS)[None, :] % NT
    fresh = [(new == 4 * s + seq) & ((new_token <= token) if w == 0 else (new_token == token))
             for s in range(2) for w in range(NW)]
    tri = i <= j
    si, sj = np.arange(NS)[:, None], np.arange(NS)[None, :]
    tri_s = (si <= sj) & (si // NT == sj // NT)
    head = np.arange(HG)[:, None, None]
    return {
        "ident": np.eye(P, dtype=np.float32),
        "cos": np.concatenate([cos, cos]).astype(np.float32),
        "sin": np.concatenate([sin, -sin]).astype(np.float32),
        "masks": masks,
        "mask_s": z(np.concatenate([cached] + fresh, 1)),
        "tri": ones(tri), "tri_s": ones(tri_s), "mask": z(tri), "mask_ss": z(tri_s),
        "own": ones(si // NT == np.arange(NB)[None, :]),
        "pick": ones(np.broadcast_to(head == np.arange(HG)[None, :, None], (HG, HG, P))).reshape(HG, HG * P),
        "spread": ones(head == 2 * np.arange(4)[None, :, None] + np.arange(P)[None, None, :] // PD),
    }


_INS = ["x_prompt", "x_sample", "cache_kv_w128", "cache_kv_w512", "cache_kv_w2048", "state_ssm", "state_conv",
        "norm_pre", "norm_post", "attn_w_in", "attn_w_out", "ssd_w_in", "ssd_conv_w", "ssd_conv_b", "ssd_dt_bias",
        "ssd_a_log", "ssd_d", "ssd_norm_w", "ssd_w_out"]
_OUTS = {
    "y_prompt": (1, SEQ, D), "y_sample": (NB, NT, D),
    "p_kv_w128": (1, 1, 128, 2, NG, HD), "p_kv_w512": (1, 1, SEQ, 2, NG, HD), "p_kv_w2048": (1, 1, SEQ, 2, NG, HD),
    "p_ssm": (1, 1, NG * HG, PD, ST), "p_conv": (1, 1, PRE, INNER + 2 * NG * ST),
    "s_kv_w128": (1, NB, 128, 2, NG, HD), "s_kv_w512": (1, NB, PAST + NT, 2, NG, HD),
    "s_kv_w2048": (1, NB, PAST + NT, 2, NG, HD),
    "s_ssm": (1, NB, NG * HG, PD, ST), "s_conv": (1, NB, PRE, INNER + 2 * NG * ST),
}


def kernel(**inputs):
    import concourse.bacc as bacc
    from concourse.bass_utils import run_bass_kernel_spmd

    nc = bacc.Bacc("TRN2", target_bir_lowering=False, num_devices=1)
    arrays = {}

    def given(name, a):
        arrays[f"in_{name}_dram"] = a
        return nc.dram_tensor(f"in_{name}_dram", a.shape, F32, kind="ExternalInput").ap()

    x = {n: given(n, np.ascontiguousarray(inputs[n])) for n in _INS}
    t = {n: given(n, a) for n, a in tables().items()}
    out = {n: nc.dram_tensor(f"out_{n}_dram", shape, F32, kind="ExternalOutput").ap() for n, shape in _OUTS.items()}
    scratch = [nc.dram_tensor(n, shape, F32, kind="Internal").ap()
               for n, shape in (("mixed", (KI, P, TOK)), ("h_prompt", (SEQ, D)), ("h_sample", (NS, D)))]
    build(nc, x, t, out, scratch)
    r = run_bass_kernel_spmd(nc, [arrays], core_ids=[0])
    return tuple(r.results[0][f"out_{n}_dram"] for n in _OUTS)
```

```python
from contextlib import ExitStack

import numpy as np

import concourse.bass as bass
from concourse import mybir

F32 = mybir.dt.float32
F32R = mybir.dt.float32r
ALU = mybir.AluOpType
ACT = mybir.ActivationFunctionType
AX = mybir.AxisListType.X

P = 128
D = 1024
KD = D // P
SEQ = 512
NB, NT = 8, 4
NS = NB * NT
TOK = SEQ + NS
HALF = TOK // 2
TT = SEQ // P + 1
ROWS = [P] * (TT - 1) + [NS]
PAST = 256
HD = 128
NG = 4
NH = 4
PAIR = 2
WINDOWS = ((128, 1), (512, 4), (2048, 16))
NW = len(WINDOWS)
INNER = 2048
KI = INNER // P
EPS = 1e-6
BIG = -1e30


class Mem:

    def __init__(self, nc, ctx, tag):
        self.nc, self.ctx, self.tag = nc, ctx, tag

    def sb(self, name, shape, dt=F32):
        return self.ctx.enter_context(self.nc.sbuf_tensor(f"{self.tag}_{name}", shape, dt))

    def ps(self, name, shape, dt=F32):
        return self.ctx.enter_context(self.nc.psum_tensor(f"{self.tag}_{name}", shape, dt))

    def sem(self, name):
        return self.nc.alloc_semaphore(name=f"{self.tag}_{name}")


class Plan:

    def __init__(self, ahead, behind, tiles, banks, unbanked):
        self.ahead, self.behind, self.tiles, self.banks, self.unbanked = ahead, behind, tiles, banks, unbanked
        self.once = Stage(self, 0, None, [0] * banks).uses()
        self.each = Stage(self, 1, 0, [0] * banks).uses()

    def first(self):
        return Stage(self, 0, None, [0] * self.banks)

    def middle(self, i):
        return Stage(self, i + 1, i, [a + b * i for a, b in zip(self.once, self.each)])

    def last(self):
        return Stage(self, None, NG - 1, [a + b * (NG - 1) for a, b in zip(self.once, self.each)])


class Stage:

    def __init__(self, plan, head, tail, base):
        self.plan, self.head, self.tail, self.base = plan, head, tail, base
        self.banked = [i for t in range(-1, plan.tiles) for i, _ in self.items(t) if i[0] not in plan.unbanked]

    def items(self, t):
        return ([(i, self.tail) for i in self.plan.behind.get(t, []) if self.tail is not None] +
                [(i, self.head) for i in self.plan.ahead.get(t, []) if self.head is not None])

    def part(self, t, q):
        items = self.items(t)
        return items[len(items) * q // 4:len(items) * (q + 1) // 4]

    def rest(self, t):
        return self.items(t)[len(self.items(t)) // 4:]

    def place(self, item):
        n = self.banked.index(item)
        return n % self.plan.banks, self.base[n % self.plan.banks] + n // self.plan.banks

    def uses(self):
        return [len(self.banked[b::self.plan.banks]) for b in range(self.plan.banks)]


def all_groups(eng, plan, stage):
    stage(plan.first())
    with eng.Fori(0, NG - 1) as i:
        stage(plan.middle(i))
    stage(plan.last())


def halves(ps, rows=P):
    return ps[0:rows, :, 0:HALF]


def two(ap):
    return ap.rearrange("p (b c) -> p b c", b=2)


def bcast_rows(ap):
    return ap.partition_broadcast(P)


def norm_phase(nc, tag, xt, ident, ident_dram, uhi, ulo, pre, src, ring, w_dram, w_at):
    w, whi, wlo = ring
    with ExitStack() as ctx:
        m = Mem(nc, ctx, tag)
        w_pre = m.sb("w_pre", [P, D])
        normed = m.sb("normed", [P, 2, D])
        turned = m.ps("turned", [P, 2, 2, 512])
        square = m.sb("square", [P, 2, D])
        stats = m.sb("stats", [P, TT, 3])
        w_in = m.sem("w_in")
        x_in = [m.sem(f"x_in{i}") for i in range(TT)]
        ident_in, split, parted = m.sem("ident_in"), m.sem("split"), m.sem("parted")
        tile_in = [m.sem(f"tile_in{r}") for r in range(PAIR)]
        squares, mean_ready, inv_ready, rstd_ready = \
            (m.sem(n) for n in ("squares", "mean_ready", "inv_ready", "rstd_ready"))
        normed_ready, turned_ready, hi_ready, lo_ready = \
            (m.sem(n) for n in ("normed_ready", "turned_ready", "hi_ready", "lo_ready"))
        block = ctx.enter_context(nc.Block())
        span = [slice(i * P, i * P + ROWS[i]) for i in range(TT)]

        @block.sync
        def _(sp):
            for i in range(TT):
                rows = src[0][span[i], :] if i < TT - 1 else src[1]
                sp.dma_start(xt[0:ROWS[i], i, :], rows).then_inc(x_in[i], 16)
                if i == 0:
                    sp.dma_start(w_pre[:, :], bcast_rows(pre)).then_inc(w_in, 16)
                    sp.dma_start(ident[:, :], ident_dram).then_inc(ident_in, 16)
            for r in range(PAIR):
                sp.dma_start(w[:, r].rearrange("p (k n) -> p k n", k=KD),
                             w_dram.rearrange("(k p) n -> p k n", p=P)[:, :, w_at[r]:w_at[r] + P]).then_inc(tile_in[r], 16)

        @block.gpsimd
        def _(pool):
            for r in range(PAIR):
                pool.wait_ge(tile_in[r], 16)
                pool.tensor_copy(whi[:, r], w[:, r]).then_inc(split, 1)
                pool.wait_ge(split, r + 1)
                pool.tensor_tensor(wlo[:, r], w[:, r], whi[:, r].bitcast(F32), ALU.subtract).then_inc(parted, 1)

        @block.tensor
        def _(pe):
            pe.wait_ge(ident_in, 16)
            for i, r in enumerate(ROWS):
                pe.wait_ge(normed_ready, i + 1)
                if i >= 2:
                    pe.wait_ge(lo_ready, i - 1)
                for k in range(KD):
                    last = pe.transpose(turned[:, i % 2, k // 4, (k % 4) * r:(k % 4 + 1) * r],
                                        normed[0:r, i % 2, k * P:(k + 1) * P], ident[0:r, 0:r])
                last.then_inc(turned_ready, 1)

        @block.scalar
        def _(act):
            for step in range(TT + 2):
                if step < TT:
                    i, n = step, ROWS[step]
                    act.wait_ge(x_in[i], 16)
                    if i >= 2:
                        act.wait_ge(squares, i - 1)
                    act.activation(square[0:n, i % 2, :], xt[0:n, i, :], ACT.Square, accum_out=stats[0:n, i, 0:1]) \
                        .then_inc(squares, 1)
                if 1 <= step <= TT:
                    i, n = step - 1, ROWS[step - 1]
                    act.wait_ge(inv_ready, i + 1)
                    act.activation(stats[0:n, i, 2:3], stats[0:n, i, 1:2], ACT.Sqrt).then_inc(rstd_ready, 1)
                if step >= 2:
                    i, r = step - 2, ROWS[step - 2]
                    act.wait_ge(turned_ready, i + 1)
                    act.activation(uhi[:, :, span[i]].rearrange("p (a k) c -> p a k c", a=2),
                                   turned[:, i % 2, :, 0:4 * r].rearrange("p a (k c) -> p a k c", k=4),
                                   ACT.Copy).then_inc(hi_ready, 1)

        @block.vector
        def _(dve):
            for step in range(TT + 2):
                if step < TT:
                    i, n = step, ROWS[step]
                    dve.wait_ge(squares, i + 1)
                    dve.tensor_scalar(stats[0:n, i, 1:2], stats[0:n, i, 0:1], 1.0 / D, EPS, ALU.mult, ALU.add) \
                        .then_inc(mean_ready, 1)
                    dve.wait_ge(mean_ready, i + 1)
                    dve.reciprocal(stats[0:n, i, 1:2], stats[0:n, i, 1:2]).then_inc(inv_ready, 1)
                if 1 <= step <= TT:
                    i, n = step - 1, ROWS[step - 1]
                    dve.wait_ge(rstd_ready, i + 1)
                    if i == 0:
                        dve.wait_ge(w_in, 16)
                    if i >= 2:
                        dve.wait_ge(turned_ready, i - 1)
                    dve.scalar_tensor_tensor(out=normed[0:n, i % 2, :], in0=xt[0:n, i, :], scalar=stats[0:n, i, 2:3],
                                             in1=w_pre[0:n, :], op0=ALU.mult, op1=ALU.mult).then_inc(normed_ready, 1)
                if step >= 2:
                    i, r = step - 2, ROWS[step - 2]
                    dve.wait_ge(hi_ready, i + 1)
                    dve.tensor_tensor(ulo[:, :, span[i]].rearrange("p (a k) c -> p a k c", a=2),
                                      turned[:, i % 2, :, 0:4 * r].rearrange("p a (k c) -> p a k c", k=4),
                                      uhi[:, :, span[i]].bitcast(F32).rearrange("p (a k) c -> p a k c", a=2),
                                      ALU.subtract).then_inc(lo_ready, 1)


def mix_phase(nc, tag, w_out, y_dram, xt, x_src, ident, post, dst, pre=None, uhi=None, ulo=None):
    with ExitStack() as ctx:
        m = Mem(nc, ctx, tag)
        CHUNKS = 4
        CK = KI // CHUNKS
        yhi = m.sb("yhi", [P, KI, TOK], F32R)
        ylo = m.sb("ylo", [P, KI, TOK], F32R)
        w = m.sb("w", [P, PAIR, KI * P])
        whi = m.sb("whi", [P, PAIR, KI * P], F32R)
        wlo = m.sb("wlo", [P, PAIR, KI * P], F32R)
        fm = m.sb("fm", [P, PAIR, TOK])
        rows = m.sb("rows", [P, TT, D])
        YS = 8
        y = rows[:, :, :].rearrange("p i d -> p (i d)")[:, 0:YS * TOK].rearrange("p (s t) -> p s t", s=YS)
        w_post = m.sb("w_post", [P, D])
        w_pre = m.sb("w_pre", [P, D])
        squared = m.sb("squared", [P, TT, P])
        sums = m.sb("sums", [P, TT, KD])
        stats = m.sb("stats", [P, 6, TT])
        normed = w[:, 0, :].rearrange("p (s d) -> p s d", s=2)
        square = w[:, 1, 0:D]
        last_rows = w[:, 0, 0:TT * P].rearrange("p (i c) -> p i c", i=TT)
        acc = m.ps("acc", [P, PAIR, 2, 512])
        back = m.ps("back", [P, PAIR, 2, 512])
        w_in = [m.sem(f"w_in{r}") for r in range(PAIR)]
        part_in = [m.sem(f"part_in{c}") for c in range(CHUNKS)]
        y_in = [m.sem(f"y_in{k}") for k in range(YS)]
        x_in, post_in, pre_in = m.sem("x_in"), m.sem("post_in"), m.sem("pre_in")
        whi_ready, wlo_ready, yhi_ready, ylo_ready = (m.sem(n) for n in ("whi_ready", "wlo_ready", "yhi_ready", "ylo_ready"))
        acc_ready, fm_ready, back_ready, rows_ready = (m.sem(n) for n in ("acc_ready", "fm_ready", "back_ready", "rows_ready"))
        cleared, squares = m.sem("cleared"), m.sem("squares")
        weighted, weighted_last = m.sem("weighted"), m.sem("weighted_last")
        stat_step, inv_ready, rstd_ready = m.sem("stat_step"), m.sem("inv_ready"), m.sem("rstd_ready")
        h_ready, h_squares, stored = m.sem("h_ready"), m.sem("h_squares"), m.sem("stored")
        normed_ready, turned_ready, hi_ready, lo_ready = \
            (m.sem(n) for n in ("normed_ready", "turned_ready", "hi_ready", "lo_ready"))
        block = ctx.enter_context(nc.Block())
        span = [slice(i * P, i * P + ROWS[i]) for i in range(TT)]

        def parts_of(o):
            return CHUNKS + o

        @block.sync
        def _(sp):
            tiles = w_out.rearrange("(k p) n -> p k n", p=P)

            def load_y(k):
                sp.dma_start(y[:, k % YS], y_dram[k]).then_inc(y_in[k % YS], 16)

            def load_w(o, r):
                sp.dma_start(w[:, r].rearrange("p (k n) -> p k n", k=KI), tiles[:, :, bass.ts(o, P)]).then_inc(w_in[r], 16)

            for c in range(CHUNKS):
                sp.dma_start(w[:, 0, CK * P * c:CK * P * (c + 1)].rearrange("p (k n) -> p k n", k=CK),
                             tiles[:, CK * c:CK * (c + 1), 0:P]).then_inc(part_in[c], 16)
                for k in range(YS // CHUNKS * c, YS // CHUNKS * (c + 1)):
                    load_y(k)
            for k in range(YS, KI):
                sp.wait_ge(ylo_ready, k - YS + 1)
                load_y(k)
                if k == KI - 3:
                    load_w(1, 1)
            sp.dma_start(w_post[:, :], bcast_rows(post)).then_inc(post_in, 16)
            for i in range(TT):
                x_rows = x_src[0][span[i], :] if i < TT - 1 else x_src[1]
                sp.dma_start(xt[0:ROWS[i], i, :], x_rows).then_inc(x_in, 16)
            if pre is not None:
                sp.dma_start(w_pre[:, :], bcast_rows(pre)).then_inc(pre_in, 16)
            sp.wait_ge(wlo_ready, parts_of(0))
            load_w(2, 0)
            with sp.Fori(0, KD // 2 - 2) as i:
                for r in (1, 0):
                    o = 2 * i + 2 - r
                    sp.wait_ge(wlo_ready, parts_of(o))
                    load_w(o + 2, r)
            sp.wait_ge(wlo_ready, parts_of(KD - 3))
            load_w(KD - 1, 1)
            for i in range(TT):
                sp.wait_ge(h_ready, i + 1)
                out = dst[0][span[i], :] if i < TT - 1 else dst[1]
                sp.dma_start(out, xt[0:ROWS[i], i, :]).then_inc(stored, 16)
            sp.wait_ge(stored, 16 * TT)
            sp.wait_ge(x_in, 16 * TT)

        @block.tensor
        def _(pe):
            def products(o, r, k0, k1):
                for k in range(k0, k1):
                    if isinstance(o, int) and o == 0:
                        pe.wait_ge(ylo_ready, k + 1)
                        if k % CK == 0:
                            pe.wait_ge(wlo_ready, k // CK + 1)
                    for a, b in ((whi, yhi), (whi, ylo), (wlo, yhi)):
                        for h in range(2):
                            last = pe.matmul(acc[:, r, h, 0:HALF], a[:, r, k * P:(k + 1) * P],
                                             b[:, k, h * HALF:(h + 1) * HALF],
                                             start=(k == 0 and a is whi and b is yhi),
                                             stop=(k == KI - 1 and a is wlo))
                if k1 == KI:
                    last.then_inc(acc_ready, 1)

            def turn(o, r):
                pe.wait_ge(fm_ready, o + 1)
                if not isinstance(o, int) or o >= 2:
                    pe.wait_ge(rows_ready, o - 1)
                for i in range(TT):
                    last = pe.transpose(back[0:ROWS[i], r, i // (TT - 1), (i % (TT - 1)) * P:(i % (TT - 1) + 1) * P],
                                        fm[:, r, span[i]], ident[:, :])
                last.then_inc(back_ready, 1)

            def tile(o, r):
                first = isinstance(o, int) and o == 0
                if not first:
                    pe.wait_ge(wlo_ready, parts_of(o))
                    if not isinstance(o, int) or o >= 2:
                        pe.wait_ge(fm_ready, o - 1)
                products(o, r, 0, KI // 2)
                if not first:
                    turn(o - 1, 1 - r)
                products(o, r, KI // 2, KI)

            tile(0, 0)
            tile(1, 1)
            with pe.Fori(0, KD // 2 - 1) as i:
                tile(2 * i + 2, 0)
                tile(2 * i + 3, 1)
            turn(KD - 1, 1)
            if pre is not None:
                for i in range(TT):
                    pe.wait_ge(normed_ready, i + 1)
                    if i >= 2:
                        pe.wait_ge(lo_ready, i - 1)
                    r = ROWS[i]
                    for k in range(KD):
                        last = pe.transpose(acc[:, i % 2, k // 4, (k % 4) * r:(k % 4 + 1) * r],
                                            normed[0:r, i % 2, k * P:(k + 1) * P], ident[0:r, 0:r])
                    last.then_inc(turned_ready, 1)

        @block.scalar
        def _(act):
            def evacuate(o, r):
                act.wait_ge(acc_ready, o + 1)
                if not isinstance(o, int) or o >= 2:
                    act.wait_ge(back_ready, o - 1)
                act.activation(two(fm[:, r]), halves(acc[:, r]), ACT.Copy).then_inc(fm_ready, 1)

            def square_rows(o, r):
                act.wait_ge(rows_ready, o + 1)
                act.wait_ge(squares, o)
                for i, n in enumerate(ROWS):
                    x = last_rows[0:n, i, :] if isinstance(o, int) and o == KD - 1 else rows[0:n, i, bass.ds(o * P, P)]
                    last = act.activation(squared[0:n, i, :], x, ACT.Square,
                                          accum_out=sums[0:n, i, bass.ds(o, 1)])
                last.then_inc(squares, 1)

            for k in range(KI):
                if k % CK == 0:
                    act.wait_ge(part_in[k // CK], 16)
                    at = slice(k * P, (k + CK) * P)
                    act.activation(whi[:, 0, at], w[:, 0, at], ACT.Copy).then_inc(whi_ready, 1)
                act.wait_ge(y_in[k % YS], 16 * (k // YS) + 16)
                act.activation(yhi[:, k, :], y[:, k % YS], ACT.Copy).then_inc(yhi_ready, 1)
            act.wait_ge(w_in[1], 16)
            act.activation(whi[:, 1], w[:, 1], ACT.Copy).then_inc(whi_ready, 1)
            act.wait_ge(acc_ready, 1)
            evacuate(0, 0)
            act.wait_ge(w_in[0], 16)
            act.activation(whi[:, 0], w[:, 0], ACT.Copy).then_inc(whi_ready, 1)
            act.wait_ge(cleared, 1)
            with act.Fori(0, KD // 2 - 2) as i:
                for o, r in ((2 * i + 1, 1), (2 * i + 2, 0)):
                    evacuate(o, r)
                    act.wait_ge(w_in[r], 16 * (i + 2))
                    act.activation(whi[:, r], w[:, r], ACT.Copy).then_inc(whi_ready, 1)
                    square_rows(o - 1, 1 - r)
            for o in range(KD - 3, KD):
                evacuate(o, o % 2)
                if o == KD - 3:
                    act.wait_ge(w_in[1], 16 * (KD // 2))
                    act.activation(whi[:, 1], w[:, 1], ACT.Copy).then_inc(whi_ready, 1)
                square_rows(o - 1, (o - 1) % 2)
            square_rows(KD - 1, 1)

            act.wait_ge(inv_ready, 1)
            act.activation(stats[:, 2, :], stats[:, 1, :], ACT.Sqrt).then_inc(rstd_ready, 1)
            for step in range(TT + 3 if pre is not None else 0):
                if step < TT:
                    i, n = step, ROWS[step]
                    act.wait_ge(h_ready, i + 1)
                    if i:
                        act.wait_ge(h_squares, i)
                    act.activation(square[0:n, :], xt[0:n, i, :], ACT.Square, accum_out=stats[0:n, 3, i:i + 1]) \
                        .then_inc(h_squares, 1)
                if 1 <= step <= TT:
                    i, n = step - 1, ROWS[step - 1]
                    act.wait_ge(inv_ready, i + 2)
                    act.activation(stats[0:n, 5, i:i + 1], stats[0:n, 4, i:i + 1], ACT.Sqrt).then_inc(rstd_ready, 1)
                if step >= 3:
                    i, r = step - 3, ROWS[step - 3]
                    act.wait_ge(turned_ready, i + 1)
                    act.activation(uhi[:, :, span[i]].rearrange("p (a k) c -> p a k c", a=2),
                                   acc[:, i % 2, :, 0:4 * r].rearrange("p a (k c) -> p a k c", k=4),
                                   ACT.Copy).then_inc(hi_ready, 1)

        @block.vector
        def _(dve):
            def get_rows(o, r):
                dve.wait_ge(back_ready, o + 1)
                at = bass.ds(o * P, P)
                dve.tensor_copy(rows[:, 0:TT - 1, at], back[:, r, 0, :].rearrange("p (i c) -> p i c", c=P))
                dve.tensor_copy(rows[0:NS, TT - 1, at], back[0:NS, r, 1, 0:P]).then_inc(rows_ready, 1)

            def w_low(n, r, at=slice(0, KI * P)):
                dve.wait_ge(whi_ready, n)
                dve.tensor_tensor(wlo[:, r, at], w[:, r, at], whi[:, r, at].bitcast(F32), ALU.subtract) \
                    .then_inc(wlo_ready, 1)

            dve.memset(sums[:, :, :], 1.0).then_inc(cleared, 1)
            dve.memset(stats[:, :, :], 1.0).then_inc(cleared, 1)
            for k in range(KI):
                if k % CK == 0:
                    w_low(k // CK + 1, 0, slice(k * P, (k + CK) * P))
                dve.wait_ge(yhi_ready, k + 1)
                dve.tensor_tensor(ylo[:, k, :], y[:, k % YS], yhi[:, k, :].bitcast(F32), ALU.subtract).then_inc(ylo_ready, 1)
            w_low(parts_of(1), 1)
            w_low(parts_of(2), 0)
            with dve.Fori(0, KD // 2 - 2) as i:
                for o, r in ((2 * i + 1, 1), (2 * i + 2, 0)):
                    w_low(parts_of(o + 2), r)
                    get_rows(o - 1, 1 - r)
            w_low(parts_of(KD - 1), 1)
            for o in range(KD - 4, KD - 1):
                get_rows(o, o % 2)
            dve.wait_ge(back_ready, KD)
            at = slice((KD - 1) * P, D)
            turned = back[:, 1, 0, :].rearrange("p (i c) -> p i c", c=P)
            dve.tensor_copy(last_rows[:, 0:TT - 1, :], turned)
            dve.tensor_copy(last_rows[0:NS, TT - 1, :], back[0:NS, 1, 1, 0:P]).then_inc(rows_ready, 1)
            dve.wait_ge(post_in, 16)
            dve.tensor_tensor(rows[:, 0:TT - 1, at], turned, w_post[:, at].unsqueeze(1).broadcast_to([P, TT - 1, P]),
                              ALU.mult)
            dve.tensor_tensor(rows[0:NS, TT - 1, at], back[0:NS, 1, 1, 0:P], w_post[0:NS, at], ALU.mult) \
                .then_inc(weighted_last, 1)

            steps = 0

            def then(ins):
                nonlocal steps
                steps += 1
                ins.then_inc(stat_step, 1)
                dve.wait_ge(stat_step, steps)

            dve.wait_ge(squares, KD)
            then(dve.tensor_reduce(stats[:, 0, :], sums[:, :, :], AX, ALU.add))
            then(dve.tensor_scalar(stats[:, 1, :], stats[:, 0, :], 1.0 / D, EPS, ALU.mult, ALU.add))
            dve.reciprocal(stats[:, 1, :], stats[:, 1, :]).then_inc(inv_ready, 1)
            dve.wait_ge(rstd_ready, 1)
            dve.wait_ge(weighted, KD - 1)
            dve.wait_ge(weighted_last, 1)
            dve.wait_ge(x_in, 16 * TT)
            for step in range(TT + 3 if pre is not None else TT):
                if step < TT:
                    i, n = step, ROWS[step]
                    dve.scalar_tensor_tensor(out=xt[0:n, i, :], in0=rows[0:n, i, :], scalar=stats[0:n, 2, i:i + 1],
                                             in1=xt[0:n, i, :], op0=ALU.mult, op1=ALU.add).then_inc(h_ready, 1)
                if pre is None:
                    continue
                if 1 <= step <= TT:
                    i, n = step - 1, ROWS[step - 1]
                    dve.wait_ge(h_squares, i + 1)
                    then(dve.tensor_scalar(stats[0:n, 4, i:i + 1], stats[0:n, 3, i:i + 1], 1.0 / D, EPS, ALU.mult, ALU.add))
                    dve.reciprocal(stats[0:n, 4, i:i + 1], stats[0:n, 4, i:i + 1]).then_inc(inv_ready, 1)
                if 2 <= step <= TT + 1:
                    i, n = step - 2, ROWS[step - 2]
                    dve.wait_ge(rstd_ready, i + 2)
                    if i == 0:
                        dve.wait_ge(pre_in, 16)
                    if i >= 2:
                        dve.wait_ge(turned_ready, i - 1)
                    dve.scalar_tensor_tensor(out=normed[0:n, i % 2, :], in0=xt[0:n, i, :], scalar=stats[0:n, 5, i:i + 1],
                                             in1=w_pre[0:n, :], op0=ALU.mult, op1=ALU.mult).then_inc(normed_ready, 1)
                if step >= 3:
                    i, r = step - 3, ROWS[step - 3]
                    dve.wait_ge(hi_ready, i + 1)
                    dve.tensor_tensor(ulo[:, :, span[i]].rearrange("p (a k) c -> p a k c", a=2),
                                      acc[:, i % 2, :, 0:4 * r].rearrange("p a (k c) -> p a k c", k=4),
                                      uhi[:, :, span[i]].bitcast(F32).rearrange("p (a k) c -> p a k c", a=2),
                                      ALU.subtract).then_inc(lo_ready, 1)

        @block.gpsimd
        def _(pool):
            pool.wait_ge(post_in, 16)
            with pool.Fori(0, KD - 1) as o:
                pool.wait_ge(squares, o + 1)
                at = bass.ds(o * P, P)
                x = rows[:, 0:TT - 1, at]
                pool.tensor_tensor(x, x, w_post[:, at].unsqueeze(1).broadcast_to([P, TT - 1, P]), ALU.mult)
                x = rows[0:NS, TT - 1, at]
                pool.tensor_tensor(x, x, w_post[0:NS, at], ALU.mult).then_inc(weighted, 1)


TILES = NW * (2 + NH) + NH
CH = (P, P, P, 64)
CW = sum(CH)
SW = CW + NW * NS
SCALE = float(HD) ** -0.5
MERGE = 9


def attn_columns(t, g):
    if t >= NW * (2 + NH):
        return 3 * INNER + 6 * NG * HD + g * (NH * HD) + (t - NW * (2 + NH)) * HD
    w, j = divmod(t, 2 + NH)
    if j == 0:
        return 3 * INNER + w * NG * HD + g * HD
    if j == 1:
        return 3 * INNER + (NW + w) * NG * HD + g * HD
    return w * INNER + g * (NH * HD) + (j - 2) * HD


def attn_kind(t):
    if t >= NW * (2 + NH):
        return "G", t - NW * (2 + NH)
    w, j = divmod(t, 2 + NH)
    return ("K", w) if j == 0 else ("V", w) if j == 1 else ("Q", w, j - 2)


ROPED = [t for t in range(TILES) if attn_kind(t)[0] in "KQ"]
UNITS = {0: [[(1, 0), (1, 1), (2, 1), (2, 2)], [(3, 2), (3, 3), (0, 0)]],
         1: [[(i, i) for i in range(4)]], 2: [[(i, i) for i in range(4)]]}
SLOT = {(0, 0): 0, (0, 1): 1, (1, 0): 2, (2, 0): 3}

ATTN_AHEAD = {
    0: [],
    1: [],
    2: [],
    3: [("V", 0), ("K", 0), ("X", 0), ("S", 0, 0, 0), ("S", 0, 0, 1)],
    4: [("S", 0, 1, 0), ("S", 0, 1, 1)],
    5: [("S", 0, 2, 1)],
    6: [("S", 0, 2, 0), ("S", 0, 3, 0), ("S", 0, 3, 1)],
    7: [],
    8: [],
    9: [("V", 1), ("K", 1), ("X", 1), ("S", 1, 0, 0)],
    10: [("S", 1, 1, 0), ("KT", 0, 0)],
    11: [("KT", 0, 1), ("S", 1, 2, 0)],
    12: [("S", 1, 3, 0)],
    13: [("KT", 0, 2)],
    14: [("KT", 0, 3)],
    15: [("V", 2), ("K", 2), ("X", 2), ("S", 2, 0, 0)],
    16: [("S", 2, 1, 0)],
    17: [("S", 2, 2, 0)],
    18: [("S", 2, 3, 0), ("SC", 0)],
    19: [("SN", 0), ("KT", 1, 0), ("KT", 1, 1), ("KT", 1, 2), ("KT", 1, 3), ("M", 0), ("M", 1), ("M", 2)],
    20: [("D", 0), ("D", 1), ("D", 2), ("PC", 0), ("PN", 0), ("SC", 1), ("SN", 1)],
    21: [("OS", 0)],
}
HEADS = [("PT", h, w, u) for h in range(NH) for w, u in SLOT]
ATTN_BEHIND = {
    0: [("PC", 1), ("PN", 1), ("F",)],
    1: [("OS", 1), ("PT", 0, 0, 0), ("PT", 0, 0, 1), ("PT", 0, 1, 0), ("PT", 0, 2, 0)],
    2: [("PT", 1, 0, 0), ("PT", 1, 0, 1), ("PT", 1, 1, 0), ("PT", 1, 2, 0), ("PT", 2, 0, 0), ("PT", 2, 0, 1),
        ("PT", 2, 1, 0)],
    3: [("PT", 2, 2, 0), ("PT", 3, 0, 0), ("PT", 3, 0, 1), ("PT", 3, 1, 0), ("PT", 3, 2, 0)],
}
SCORES = [item for t in range(TILES) for item in ATTN_AHEAD[t] if item[0] == "S"]
ATTN = Plan(ATTN_AHEAD, ATTN_BEHIND, TILES, 2, ("OS",))


def attention_phase(nc, uhi, ulo, ident, ring, w_in_dram, tables, caches, y_dram, p_kv, s_kv):
    w, whi, wlo = ring
    plan = ATTN
    with ExitStack() as ctx:
        m = Mem(nc, ctx, "at")
        cos = m.sb("cos", [P, TOK])
        sin = m.sb("sin", [P, TOK])
        masks = m.sb("masks", [P, 3, P])
        mask_s = m.sb("mask_s", [P, 2 * SW - CW])
        q = m.sb("q", [P, NH, SEQ])
        qs = m.sb("qs", [P, NW, 4, NH, 8])
        k = m.sb("k", [P, SEQ])
        ks = m.sb("ks", [P, NW, NS])
        v = m.sb("v", [P, TOK])
        v_rows = m.sb("v_rows", [P, NW, 4, HD])
        k_rows = m.sb("k_rows", [P, 4, HD])
        new_rows = m.sb("new_rows", [NS, NW, 2, HD])
        straight = m.sb("straight", [P, TOK])
        crossed = m.sb("crossed", [P, TOK])
        probs = m.sb("probs", [P, NH, 4, 512])
        top = m.sb("top", [P, NW, 4, NH])
        neg_top = m.sb("neg_top", [P, NW, 4, NH])
        den = m.sb("den", [P, NW, 4, NH])
        factor = m.sb("factor", [P, NW, 4, NH])
        row_top = m.sb("row_top", [NH, NW, SEQ])
        row_den = m.sb("row_den", [NH, NW, SEQ])
        row_all = m.sb("row_all", [NH, SEQ])
        probs_t = m.sb("probs_t", [P, 2, 512])
        k_cache = m.sb("k_cache", [P, 4, 4, HD])
        v_cache = m.sb("v_cache", [P, 4, 4, HD])
        keys_t = m.sb("keys_t", [P, 4, CW])
        probs_s = m.sb("probs_s", [P, SW])
        stat_s = m.sb("stat_s", [P, 4])
        cached_t = m.sb("cached_t", [P, 4, P])
        new_t = m.sb("new_t", [NS, NW, P])
        yg = m.sb("yg", [P, NH, TOK])
        proj = m.ps("proj", [P, PAIR, 2, 512])
        small = [m.ps(f"small{b}", [P, 512]) for b in range(2)]
        out_t = [m.ps(f"out_t{b}", [P, 512]) for b in range(2)]

        held_back = m.sem("held_back")
        consts_in = m.sem("consts_in")
        w_in = [m.sem(f"w_in{r}") for r in range(PAIR)]
        whi_ready = m.sem("whi_ready")
        wlo_ready = m.sem("wlo_ready")
        proj_ready = m.sem("proj_ready")
        proj_free = [m.sem(f"proj_free{r}") for r in range(PAIR)]
        turned_ready = m.sem("turned_ready")
        qk_ready = m.sem("qk_ready")
        v_ready = m.sem("v_ready")
        small_ready = [m.sem(f"small_ready{b}") for b in range(2)]
        small_free = [m.sem(f"small_free{b}") for b in range(2)]
        masked_ready = m.sem("masked_ready")
        top_ready = m.sem("top_ready")
        neg_ready = m.sem("neg_ready")
        probs_ready = m.sem("probs_ready")
        kv_rows_ready = m.sem("kv_rows_ready")
        kv_stored = m.sem("kv_stored")
        k_cache_in = m.sem("k_cache_in")
        v_cache_in = m.sem("v_cache_in")
        keys_ready = m.sem("keys_ready")
        s_masked = m.sem("s_masked")
        s_top = m.sem("s_top")
        s_neg = m.sem("s_neg")
        s_exp = m.sem("s_exp")
        s_inv = m.sem("s_inv")
        s_probs = m.sem("s_probs")
        s_turned = m.sem("s_turned")
        s_out = m.sem("s_out")
        rows_ready = m.sem("rows_ready")
        merge = m.sem("merge")
        shift_exp = m.sem("shift_exp")
        factor_ready = m.sem("factor_ready")
        scaled_ready = m.sem("scaled_ready")
        probs_t_ready = m.sem("probs_t_ready")
        head_done = m.sem("head_done")
        gates_ready = m.sem("gates_ready")
        silu_ready = m.sem("silu_ready")
        keys_odd_ready = m.sem("keys_odd_ready")
        out_free = [m.sem(f"out_free{b}") for b in range(2)]
        yg_ready = m.sem("yg_ready")
        y_stored = m.sem("y_stored")
        caches_copied = m.sem("caches_copied")
        block = ctx.enter_context(nc.Block())

        def bank(st, item):
            return small[st.place(item)[0]]

        def filled(eng, st, item):
            b, ahead = st.place(item)
            eng.wait_ge(small_ready[b], ahead + 1)

        def free(eng, st, item):
            eng.sem_inc(small_free[st.place(item)[0]], 1)

        def strided(ap, w_, i):
            d = WINDOWS[w_][1]
            if d == 1:
                return ap[:, i * P:(i + 1) * P]
            if d == 4:
                return ap.rearrange("p (m r) -> p r m", r=4)[:, i, :]
            return ap.rearrange("p (m r) -> p r m", r=16)[:, 4 * i:4 * i + 4, :]

        def square(ap, w_):
            return ap.rearrange("p (r m) -> p r m", r=4) if WINDOWS[w_][1] == 16 else ap

        STORES = (6, 6, 12)

        @block.sync
        def _(sp):
            def load_w(g, t, slot):
                src = w_in_dram.rearrange("(k p) n -> p k n", p=P)[:, :, bass.ds(attn_columns(t, g), P)]
                sp.dma_start(w[:, slot].rearrange("p (k n) -> p k n", k=KD), src).then_inc(w_in[slot], 16)

            def load_cache(g, s, kv, dst, signal):
                for c, (cache, rows) in enumerate(((0, slice(0, P)), (1, slice(0, P)), (1, slice(P, 2 * P)))):
                    src = caches[cache][0, 4 * s:4 * s + 4, rows, kv, bass.ds(g, 1), :]
                    sp.dma_start(dst[:, :, c, :], src.rearrange("n p g d -> p n (g d)")).then_inc(signal, 16)
                for t in range(NT):
                    src = caches[2][0, 4 * s:4 * s + 4, :, kv, bass.ds(g, 1), :] \
                        .rearrange("n (m r) g d -> r m n (g d)", r=16)[t]
                    sp.dma_start(dst[16 * t:16 * t + 16, :, 3, :], src).then_inc(signal, 16)

            def store_rows(w_, g, kv, rows):
                out = p_kv[w_][0, :, kv, bass.ds(g, 1), :]
                if w_ == 0:
                    sp.dma_start(out.rearrange("p g d -> p (g d)"), rows[:, 3, :]).then_inc(kv_stored, 16)
                elif w_ == 1:
                    sp.dma_start(out.rearrange("(p r) g d -> p r (g d)", r=4), rows).then_inc(kv_stored, 16)
                else:
                    for r in range(4):
                        sp.dma_start(out.rearrange("(m i r) g d -> r m i (g d)", i=4, r=4)[r],
                                     rows[32 * r:32 * r + 32]).then_inc(kv_stored, 16)

            def store_new(w_, g):
                keep = s_kv[w_].shape[2]
                out = s_kv[w_][0, :, keep - NT:keep, :, bass.ds(g, 1), :]
                for t in range(NT):
                    sp.dma_start(out[:, t].rearrange("n k g d -> n k (g d)"), new_rows[t:NS:NT, w_]) \
                        .then_inc(kv_stored, 16)

            for t in range(PAIR):
                load_w(0, PAIR + t, t)
            sp.dma_start(cos[:, :], tables["cos"]).then_inc(consts_in, 16)
            sp.dma_start(sin[:, :], tables["sin"]).then_inc(consts_in, 16)
            sp.dma_start(masks[:, :, :], tables["masks"]).then_inc(consts_in, 16)
            sp.dma_start(mask_s[:, :], tables["mask_s"]).then_inc(consts_in, 16)

            def stage(st):
                g = st.head
                for t in range(TILES):
                    if t == 4 and st.tail is not None:
                        sp.wait_ge(yg_ready, (NH + 4) * (st.tail + 1))
                        sp.dma_start(y_dram[bass.ds(NH * st.tail, NH)].rearrange("h p t -> p h t"), yg[:, :, :]) \
                            .then_inc(y_stored, 16)
                    if g is None:
                        continue
                    sp.wait_ge(wlo_ready, TILES * g + t + PAIR + 1)
                    nxt = t + 2 * PAIR
                    load_w(g + nxt // TILES, nxt % TILES, t % PAIR)
                    if t == 0:
                        sp.wait_ge(keys_ready, 4 * g)
                        sp.wait_ge(keys_odd_ready, 4 * g)
                        load_cache(g, 0, 0, k_cache, k_cache_in)
                    if t == 5:
                        sp.wait_ge(s_out, 2 * g)
                        load_cache(g, 0, 1, v_cache, v_cache_in)
                    if t in (1, 2, 4, 5, 7, 8):
                        i, j = divmod((1, 2, 4, 5, 7, 8).index(t), 2)
                        c_rows, keep = caches[i].shape[2], s_kv[i].shape[2]
                        skip = c_rows - (keep - NT)
                        sp.dma_start(s_kv[i][0, bass.ds(2 * g + j, 1), 0:keep - NT].rearrange("n s k h d -> (n s) (k h d)"),
                                     caches[i][0, bass.ds(2 * g + j, 1), skip:].rearrange("n s k h d -> (n s) (k h d)")) \
                            .then_inc(caches_copied, 16)
                    for w_ in range(NW):
                        if t == 6 * w_ + 4:
                            sp.wait_ge(kv_rows_ready, 3 * (NW * g + w_) + 3)
                            store_rows(w_, g, 1, v_rows[:, w_])
                            store_rows(w_, g, 0, k_rows[:, :, :])
                            store_new(w_, g)
                    if t == 16:
                        sp.wait_ge(keys_ready, 4 * g + 2)
                        sp.wait_ge(keys_odd_ready, 4 * g + 2)
                        load_cache(g, 1, 0, k_cache, k_cache_in)
                if g is not None:
                    sp.wait_ge(s_out, 2 * g + 1)
                    load_cache(g, 1, 1, v_cache, v_cache_in)

            all_groups(sp, ATTN, stage)
            sp.wait_ge(y_stored, 16 * NG)
            sp.wait_ge(kv_stored, 16 * sum(STORES) * NG)
            sp.wait_ge(caches_copied, 16 * 2 * NW * NG)
            for r in range(PAIR):
                sp.wait_ge(w_in[r], 16 * (TILES * NG // PAIR + 1))

        @block.tensor
        def _(pe):
            def project(g, t, q):
                r = t % PAIR
                if q == 0:
                    pe.wait_ge(wlo_ready, TILES * g + t + 1)
                    pe.wait_ge(proj_free[r], TILES // PAIR * g + t // PAIR)
                for kk in range(KD // 4 * q, KD // 4 * (q + 1)):
                    for a, b in ((whi, uhi), (whi, ulo), (wlo, uhi)):
                        for h in range(2):
                            last = pe.matmul(proj[:, r, h, 0:HALF], a[:, r, kk * P:(kk + 1) * P],
                                             b[:, kk, h * HALF:(h + 1) * HALF],
                                             start=(kk == 0 and a is whi and b is uhi),
                                             stop=(kk == KD - 1 and a is wlo))
                if q == 3:
                    last.then_inc(proj_ready, 1)

            def turn(out, ins, one):
                return pe.matmul(out, ins, one, is_transpose=True, start=True, stop=True)

            def roped(g, t):
                pe.wait_ge(qk_ready, 2 * len(ROPED) * g + 2 * ROPED.index(t) + 2)

            def small_item(st, g, item):
                n, ahead = st.place(item)
                b = small[n]
                pe.wait_ge(small_free[n], ahead)
                what = item[0]
                if what == "V":
                    pe.wait_ge(v_ready, NW * g + item[1] + 1)
                    for i in range(4):
                        last = turn(b[:, i * HD:(i + 1) * HD], v[:, i * P:(i + 1) * P], ident[:, :])
                elif what == "K":
                    roped(g, 6 * item[1])
                    for i in range(3 if item[1] == 0 else 0, 4):
                        last = turn(b[:, i * HD:(i + 1) * HD], k[:, i * P:(i + 1) * P], ident[:, :])
                elif what == "X":
                    turn(b[0:NS, 0:HD], ks[:, item[1], :], ident[:, :])
                    last = turn(b[0:NS, HD:2 * HD], v[:, SEQ:TOK], ident[:, :])
                elif what == "S":
                    _, w_, h, u = item
                    roped(g, 6 * w_ + 2 + h)
                    for j, (qt, kt) in enumerate(UNITS[w_][u]):
                        last = pe.matmul(b[:, j * P:(j + 1) * P], q[:, h, qt * P:(qt + 1) * P],
                                         k[:, kt * P:(kt + 1) * P], start=True, stop=True)
                elif what == "KT":
                    _, s, ni = item
                    pe.wait_ge(k_cache_in, 16 * 7 * (2 * g + s + 1))
                    for c, rows in enumerate(CH):
                        last = turn(b[:, c * P:c * P + rows], k_cache[0:rows, ni, c, :],
                                            ident[0:rows, 0:rows])
                elif what in ("SC", "SN"):
                    s = item[1]
                    roped(g, ROPED[-1])
                    pe.wait_ge(keys_ready, 4 * g + 2 * s + 2)
                    pe.wait_ge(keys_odd_ready, 4 * g + 2 * s + 2)
                    for ni in range(4):
                        pair = (4 * s + ni) // 2
                        for w_ in range(NW):
                            if what == "SC":
                                at = (0, P, 3 * P)[w_]
                                cols = (P, 2 * P, 64)[w_]
                                rhs, o = keys_t[:, ni, at:at + cols], b[32 * ni:32 * ni + 32, at:at + cols]
                            else:
                                rhs, o = ks[:, w_, :], b[32 * ni:32 * ni + 32, w_ * NS:(w_ + 1) * NS]
                            last = pe.matmul(o, qs[:, w_, pair].rearrange("p h t -> p (h t)"), rhs, start=True, stop=True)
                elif what == "M":
                    pe.wait_ge(top_ready, len(SCORES) * (g + 1))
                    for i in range(4):
                        last = turn(strided(b[0:NH, :], item[1], i), top[:, item[1], i, :], square(ident[:, :], item[1]))
                elif what == "D":
                    pe.wait_ge(probs_ready, len(SCORES) * (g + 1))
                    for i in range(4):
                        last = turn(strided(b[0:NH, :], item[1], i), den[:, item[1], i, :], square(ident[:, :], item[1]))
                elif what == "PC":
                    pe.wait_ge(s_probs, 2 * g + item[1] + 1)
                    for c, rows in enumerate(CH):
                        last = turn(b[0:rows, c * P:(c + 1) * P], probs_s[:, c * P:c * P + rows], ident[:, :])
                elif what == "PN":
                    for w_ in range(NW):
                        last = turn(b[0:NS, w_ * P:(w_ + 1) * P],
                                            probs_s[:, CW + w_ * NS:CW + (w_ + 1) * NS], ident[:, :])
                elif what == "F":
                    pe.wait_ge(merge, MERGE * g + MERGE)
                    pe.sem_inc(held_back, 1)
                    for w_ in range(NW):
                        for i in range(4):
                            at = (w_ * 4 + i) * NH
                            row = row_den[:, 2, i * P:(i + 1) * P] if w_ == 2 else strided(row_top[:, w_, :], w_, i)
                            last = turn(b[:, at:at + NH], row, ident[0:NH, 0:NH])
                elif what == "PT":
                    _, h, w_, u = item
                    pe.wait_ge(scaled_ready, len(HEADS) * g + HEADS.index(item) + 1)
                    for j in range(len(UNITS[w_][u])):
                        last = turn(b[:, j * P:(j + 1) * P], probs[:, h, SLOT[w_, u], j * P:(j + 1) * P],
                                            ident[:, :])
                last.then_inc(small_ready[n], 1)

            def sample_out(g, s):
                pe.wait_ge(s_turned, 4 * g + 2 * s + 2)
                pe.wait_ge(v_cache_in, 16 * 7 * (2 * g + s + 1))
                pe.wait_ge(kv_rows_ready, 3 * NW * (g + 1))
                pe.wait_ge(out_free[s], 3 * g)
                for w_ in range(NW):
                    pe.matmul(out_t[s][:, 0:P], new_rows[:, w_, 1, :], new_t[:, w_, :], start=(w_ == 0), stop=False,
                              skip_group_check=True)
                for ni in range(4):
                    for c, rows in enumerate(CH):
                        last = pe.matmul(out_t[s][:, 32 * ni:32 * ni + 32], v_cache[0:rows, ni, c, :],
                                         cached_t[0:rows, c, 32 * ni:32 * ni + 32], start=False,
                                         stop=(c == len(CH) - 1), skip_group_check=True)
                last.then_inc(s_out, 1)

            def weigh(g, n):
                _, h, w_, u = HEADS[n]
                pe.wait_ge(probs_t_ready, len(HEADS) * g + n + 1)
                if SLOT[w_, u] == 0:
                    pe.wait_ge(out_free[h % 2], 3 * g + 1 + h // 2)
                for j, (qt, kt) in enumerate(UNITS[w_][u]):
                    last = pe.matmul(strided(out_t[h % 2][:, :], w_, qt), v_rows[:, w_, kt, :],
                                     square(probs_t[:, n % 2, j * P:(j + 1) * P], w_),
                                     start=(SLOT[w_, u] == 0 and j == 0), stop=(SLOT[w_, u] == 3 and j == 3),
                                     skip_group_check=True)
                last.then_inc(head_done, 1)

            def run(st, items):
                for item, g in items:
                    if item[0] == "OS":
                        sample_out(g, item[1])
                        continue
                    small_item(st, g, item)
                    if item[0] == "PT" and item != HEADS[0]:
                        weigh(g, HEADS.index(item) - 1)
                    if item == HEADS[-1]:
                        weigh(g, len(HEADS) - 1)

            def stage(st):
                for t in range(TILES):
                    for q in range(4):
                        if st.head is not None:
                            project(st.head, t, q)
                        if q < 3:
                            run(st, st.part(t - 1, q + 1))
                    run(st, st.part(t, 0))
                run(st, st.rest(TILES - 1))

            all_groups(pe, ATTN, stage)

        @block.scalar
        def _(act):
            def w_high(g, t):
                act.wait_ge(w_in[t % PAIR], TILES // PAIR * 16 * g + 16 * (t // PAIR))
                act.activation(whi[:, t % PAIR], w[:, t % PAIR], ACT.Copy).then_inc(whi_ready, 1)

            def exps(g, item):
                _, w_, h, u = item
                n = SCORES.index(item)
                act.wait_ge(neg_ready, len(SCORES) * g + n + 1)
                blocks = UNITS[w_][u]
                for qt in dict.fromkeys(b[0] for b in blocks):
                    js = [j for j, b in enumerate(blocks) if b[0] == qt]
                    x = probs[:, h, SLOT[w_, u], js[0] * P:(js[-1] + 1) * P]
                    last = act.activation(x, x, ACT.Exp, bias=neg_top[:, w_, qt, h:h + 1], scale=SCALE,
                                          accum_out=den[:, w_, qt, h:h + 1])
                last.then_inc(probs_ready, 1)

            def copied(st, item, dst, src, signal, value):
                filled(act, st, item)
                act.activation(dst, src, ACT.Copy).then_inc(signal, 1)
                act.wait_ge(signal, value)
                free(act, st, item)

            act.sem_inc(whi_ready, PAIR)
            def projected(g, t):
                act.wait_ge(proj_ready, TILES * g + t + 1)
                nxt = t + PAIR
                w_high(g + nxt // TILES, nxt % TILES)
                what = attn_kind(t)
                if what[0] == "V":
                    if what[1] == 0:
                        act.wait_ge(kv_rows_ready, 3 * NW * g)
                    d = WINDOWS[what[1]][1]
                    order = v[:, 0:SEQ].rearrange("p (r m) -> p m r", r=d)
                    for h, (a, z) in enumerate(((0, HALF), (HALF, SEQ))):
                        act.activation(order[:, a // d:z // d, :],
                                       proj[:, t % PAIR, h, 0:z - a].rearrange("p (m r) -> p m r", r=d), ACT.Copy)
                    act.activation(v[:, SEQ:TOK], proj[:, t % PAIR, 1, SEQ - HALF:HALF], ACT.Copy).then_inc(v_ready, 1)
                    act.wait_ge(v_ready, NW * g + what[1] + 1)
                    act.sem_inc(proj_free[t % PAIR], 1)
                if what[0] == "G":
                    if what[1] == 0:
                        act.wait_ge(y_stored, 16 * g)
                    act.activation(two(yg[:, what[1], :]), halves(proj[:, t % PAIR]), ACT.Copy).then_inc(gates_ready, 1)
                    act.wait_ge(gates_ready, NH * g + what[1] + 1)
                    act.sem_inc(proj_free[t % PAIR], 1)

            def stage(st):
                for t in range(TILES):
                    if st.head is not None:
                        projected(st.head, t)
                    if t == 0 and st.tail is not None:
                        act.activation(yg[:, :, :], yg[:, :, :], ACT.Silu).then_inc(silu_ready, 1)
                    for item, g in st.items(t):
                        if item[0] == "V":
                            w_ = item[1]
                            act.wait_ge(kv_stored, 16 * (sum(STORES) * g + sum(STORES[:w_])))
                            act.wait_ge(head_done, len(HEADS) * g)
                            copied(st, item, v_rows[:, w_], bank(st, item)[:, :].rearrange("p (i d) -> p i d", i=4),
                                   kv_rows_ready, 3 * (NW * g + w_) + 1)
                        elif item[0] == "K":
                            w_ = item[1]
                            lo = 3 if w_ == 0 else 0
                            copied(st, item, k_rows[:, lo:4],
                                   bank(st, item)[:, lo * HD:4 * HD].rearrange("p (i d) -> p i d", d=HD),
                                   kv_rows_ready, 3 * (NW * g + w_) + 2)
                        elif item[0] == "X":
                            w_ = item[1]
                            act.wait_ge(s_out, 2 * g)
                            copied(st, item, new_rows[:, w_],
                                   bank(st, item)[0:NS, 0:2 * HD].rearrange("p (i d) -> p i d", d=HD),
                                   kv_rows_ready, 3 * (NW * g + w_) + 3)
                        elif item[0] == "KT":
                            _, s, ni = item
                            if ni % 2 == 0:
                                if s == 1:
                                    filled(act, st, ("SC", 0))
                                copied(st, item, keys_t[:, ni, :], bank(st, item)[:, 0:CW], keys_ready,
                                       4 * g + 2 * s + ni // 2 + 1)
                        elif item[0] == "SN":
                            act.wait_ge(s_neg, 2 * g + item[1] + 1)
                            act.activation(probs_s[:, :], probs_s[:, :], ACT.Exp, bias=stat_s[:, 1:2], scale=SCALE,
                                           accum_out=stat_s[:, 2:3]).then_inc(s_exp, 1)
                        elif item[0] in ("M", "D"):
                            dst = row_top if item[0] == "M" else row_den
                            copied(st, item, dst[:, item[1], :], bank(st, item)[0:NH, :], rows_ready,
                                   2 * NW * g + (0 if item[0] == "M" else NW) + item[1] + 1)
                        elif item[0] == "PC":
                            s = item[1]
                            b = bank(st, item)
                            filled(act, st, item)
                            act.wait_ge(s_out, 2 * g + s)
                            act.activation(cached_t[:, 0:3, :], b[:, 0:3 * P].rearrange("p (c q) -> p c q", c=3), ACT.Copy)
                            act.activation(cached_t[0:64, 3, :], b[0:64, 3 * P:4 * P], ACT.Copy).then_inc(s_turned, 1)
                            act.wait_ge(s_turned, 4 * g + 2 * s + 1)
                            free(act, st, item)
                        elif item[0] == "PN":
                            copied(st, item, new_t[:, :, :],
                                   bank(st, item)[0:NS, 0:NW * P].rearrange("p (w q) -> p w q", w=NW),
                                   s_turned, 4 * g + 2 * item[1] + 2)
                        elif item[0] == "PT":
                            n = HEADS.index(item)
                            act.wait_ge(head_done, len(HEADS) * g + max(n - 1, 0))
                            cols = len(UNITS[item[2]][item[3]]) * P
                            copied(st, item, probs_t[:, n % 2, 0:cols], bank(st, item)[:, 0:cols], probs_t_ready,
                                   len(HEADS) * g + n + 1)
                    if st.head is not None:
                        for item in ATTN_AHEAD.get(t - 1, []):
                            if item[0] == "S":
                                exps(st.head, item)
                    if t == 20 and st.head is not None:
                        g = st.head
                        act.wait_ge(merge, MERGE * g + 3)
                        act.activation(row_top[:, :, :], row_top[:, :, :], ACT.Exp, scale=SCALE).then_inc(shift_exp, 1)

            all_groups(act, ATTN, stage)

        @block.vector
        def _(dve):
            dve.wait_ge(consts_in, 64)

            def rotate(g, t):
                n = ROPED.index(t)
                r = t % PAIR
                x = proj[:, r]
                dve.wait_ge(qk_ready, 2 * len(ROPED) * g + 2 * n)
                dve.tensor_tensor(two(straight[:, :]), halves(x), two(cos[:, :]), ALU.mult).then_inc(turned_ready, 1)
                dve.tensor_tensor(two(crossed[0:64, :]), x[64:P, :, 0:HALF], two(sin[64:P, :]), ALU.mult) \
                    .then_inc(turned_ready, 1)
                dve.tensor_tensor(two(crossed[64:P, :]), x[0:64, :, 0:HALF], two(sin[0:64, :]), ALU.mult) \
                    .then_inc(turned_ready, 1)
                dve.wait_ge(turned_ready, 3 * len(ROPED) * g + 3 * n + 3)
                dve.sem_inc(proj_free[r], 1)

            def blocks(ap, n):
                return ap.rearrange("p (j c) -> p j c", j=n)

            def mask_and_top(st, g, item):
                _, w_, h, u = item
                n = len(SCORES) * g + SCORES.index(item)
                b = bank(st, item)
                filled(dve, st, item)
                dst = probs[:, h, SLOT[w_, u], :]
                if w_ == 0:
                    c = 2 if u == 0 else 1
                    band = masks[:, 0:2, :].rearrange("p a c -> p (a c)")
                    last = dve.tensor_tensor(blocks(dst[:, 0:256 * c], c), blocks(b[:, 0:256 * c], c),
                                             band.unsqueeze(1).broadcast_to([P, c, 256]), ALU.add)
                    if u == 1:
                        last = dve.tensor_tensor(dst[:, 256:384], b[:, 256:384], masks[:, 1, :], ALU.add)
                else:
                    last = dve.tensor_tensor(blocks(dst, 4), blocks(b[:, :], 4),
                                             masks[:, w_, :].unsqueeze(1).broadcast_to([P, 4, P]), ALU.add)
                last.then_inc(masked_ready, 1)
                dve.wait_ge(masked_ready, n + 1)
                free(dve, st, item)
                if w_ == 0:
                    tops = [(1, 3, 0, 512)] if u == 0 else [(3, 4, 0, 256), (0, 1, 256, 384)]
                else:
                    tops = [(0, 4, 0, 512)]
                for a, z, lo, hi in tops:
                    last = dve.tensor_reduce(top[:, w_, a:z, h], blocks(dst[:, lo:hi], z - a), AX, ALU.max)
                last.then_inc(top_ready, 1)
                dve.wait_ge(top_ready, n + 1)
                for a, z, _, _ in tops:
                    last = dve.tensor_scalar(neg_top[:, w_, a:z, h], top[:, w_, a:z, h], -SCALE, None, ALU.mult)
                last.then_inc(neg_ready, 1)

            def sample_top(st, g, s):
                filled(dve, st, ("SC", s))
                dve.tensor_tensor(probs_s[:, 0:CW], bank(st, ("SC", s))[:, 0:CW], mask_s[:, 0:CW], ALU.add) \
                    .then_inc(s_masked, 1)
                filled(dve, st, ("SN", s))
                dve.tensor_tensor(probs_s[:, CW:SW], bank(st, ("SN", s))[:, 0:SW - CW],
                                  mask_s[:, CW + (SW - CW) * s:CW + (SW - CW) * (s + 1)], ALU.add) \
                    .then_inc(s_masked, 1)
                dve.wait_ge(s_masked, 4 * g + 2 * s + 2)
                free(dve, st, ("SC", s))
                free(dve, st, ("SN", s))
                dve.tensor_reduce(stat_s[:, 0:1], probs_s[:, :], AX, ALU.max).then_inc(s_top, 1)
                dve.wait_ge(s_top, 2 * g + s + 1)
                dve.tensor_scalar(stat_s[:, 1:2], stat_s[:, 0:1], -SCALE, None, ALU.mult).then_inc(s_neg, 1)

            def sample_normalise(g, s):
                dve.wait_ge(s_exp, 2 * g + s + 1)
                dve.reciprocal(stat_s[:, 3:4], stat_s[:, 2:3]).then_inc(s_inv, 1)
                dve.wait_ge(s_inv, 2 * g + s + 1)
                dve.tensor_scalar(probs_s[:, :], probs_s[:, :], stat_s[:, 3:4], None, ALU.mult).then_inc(s_probs, 1)

            def sample_gate(g, s):
                dve.wait_ge(s_out, 2 * g + s + 1)
                dve.wait_ge(silu_ready, g + 1)
                for j in range(2):
                    o = out_t[s][:, 0:P].rearrange("p (i j h k t) -> p j k h i t", i=2, j=2, h=NH, k=2)[:, j, j]
                    dst = yg[:, :, SEQ + 16 * s:SEQ + 16 * s + 16].rearrange("p h (i j t) -> p j h i t", i=2, j=2)[:, j]
                    dve.tensor_tensor(dst, o, dst, ALU.mult).then_inc(yg_ready, 1)
                dve.wait_ge(yg_ready, (NH + 4) * g + 2 * s + 2)
                dve.sem_inc(out_free[s], 1)

            def merge_windows(g):
                steps = MERGE * g

                def then(ins, n):
                    ins.then_inc(merge, 1)
                    dve.wait_ge(merge, steps + n)

                dve.wait_ge(rows_ready, 2 * NW * (g + 1))
                t = row_all[:, :]
                then(dve.tensor_tensor(t, row_top[:, 0, :], row_top[:, 1, :], ALU.max), 1)
                then(dve.tensor_tensor(t, t, row_top[:, 2, :], ALU.max), 2)
                wide = row_all[:, :].unsqueeze(1).broadcast_to([NH, NW, SEQ])
                then(dve.tensor_tensor(row_top[:, :, :], row_top[:, :, :], wide, ALU.subtract), 3)
                dve.wait_ge(shift_exp, g + 1)
                then(dve.tensor_tensor(row_den[:, :, :], row_den[:, :, :], row_top[:, :, :], ALU.mult), 4)
                then(dve.tensor_tensor(t, row_den[:, 0, :], row_den[:, 1, :], ALU.add), 5)
                then(dve.tensor_tensor(t, t, row_den[:, 2, :], ALU.add), 6)
                then(dve.reciprocal(t, t), 7)
                then(dve.tensor_tensor(row_top[:, 0:2, :], row_top[:, 0:2, :], wide[:, 0:2, :], ALU.mult), 8)
                then(dve.tensor_tensor(row_den[:, 2, :].rearrange("p (r m) -> p m r", r=16),
                                       row_top[:, 2, :].rearrange("p (m r) -> p m r", r=16),
                                       t.rearrange("p (m r) -> p m r", r=16), ALU.mult), 9)

            def get_factors(st, g):
                filled(dve, st, ("F",))
                dve.tensor_copy(factor[:, :, :, :].rearrange("p w i h -> p (w i h)"),
                                bank(st, ("F",))[:, 0:NW * 4 * NH]).then_inc(factor_ready, 1)
                dve.wait_ge(factor_ready, g + 1)
                free(dve, st, ("F",))

            def scale(n):
                _, h, w_, u = HEADS[n]
                dst = probs[:, h, SLOT[w_, u], :]
                if w_ == 0:
                    parts = [(1, 3, 0, 512)] if u == 0 else [(3, 4, 0, 256), (0, 1, 256, 384)]
                else:
                    parts = [(0, 4, 0, 512)]
                for a, z, lo, hi in parts:
                    x = blocks(dst[:, lo:hi], z - a)
                    f = factor[:, w_, a:z, h].unsqueeze(2).broadcast_to([P, z - a, (hi - lo) // (z - a)])
                    last = dve.tensor_tensor(x, x, f, ALU.mult)
                last.then_inc(scaled_ready, 1)

            def gate(g, h):
                dve.wait_ge(head_done, len(HEADS) * g + 4 * h + 4)
                dve.tensor_tensor(yg[:, h, 0:SEQ], yg[:, h, 0:SEQ], out_t[h % 2][:, :], ALU.mult).then_inc(yg_ready, 1)
                dve.wait_ge(yg_ready, (NH + 4) * g + 4 + h + 1)
                dve.sem_inc(out_free[h % 2], 1)

            def stage(st):
                h = st.head
                for t in range(TILES):
                    if h is not None and attn_kind(t)[0] in "KQ":
                        dve.wait_ge(proj_ready, TILES * h + t + 1)
                        rotate(h, t)
                    for item, g in st.items(t):
                        if item[0] == "S":
                            mask_and_top(st, g, item)
                        elif item[0] == "KT" and item[2] % 2 == 1:
                            _, s, ni = item
                            filled(dve, st, item)
                            if s == 1:
                                filled(dve, st, ("SC", 0))
                            dve.tensor_copy(keys_t[:, ni, :], bank(st, item)[:, 0:CW]).then_inc(keys_odd_ready, 1)
                            dve.wait_ge(keys_odd_ready, 4 * g + 2 * s + ni // 2 + 1)
                            free(dve, st, item)
                        elif item[0] == "SN":
                            dve.wait_ge(s_turned, 4 * g + 2 * item[1])
                            sample_top(st, g, item[1])
                        elif item[0] == "F":
                            sample_gate(g, 0)
                            get_factors(st, g)
                            for n in range(6):
                                scale(n)
                        elif item[0] == "OS" and item[1] == 1:
                            sample_gate(g, 1)
                        elif item[0] == "PT":
                            n = HEADS.index(item)
                            if n + 5 >= 6 and n + 5 < len(HEADS):
                                scale(n + 5)
                            if n % 4 == 1 and n > 4:
                                gate(g, n // 4 - 1)
                            if n == len(HEADS) - 1:
                                gate(g, NH - 1)
                    if t == 19 and h is not None:
                        sample_normalise(h, 0)
                    if t == 20 and h is not None:
                        sample_normalise(h, 1)
                        merge_windows(h)

            all_groups(dve, ATTN, stage)

        @block.gpsimd
        def _(pool):
            def w_low(g, t):
                r = t % PAIR
                pool.wait_ge(whi_ready, TILES * g + t + 1)
                pool.tensor_tensor(wlo[:, r], w[:, r], whi[:, r].bitcast(F32), ALU.subtract).then_inc(wlo_ready, 1)

            pool.sem_inc(wlo_ready, PAIR)
            def stage(st):
                g = st.head
                for t in range(TILES if g is not None else 0):
                    nxt = t + PAIR
                    w_low(g + nxt // TILES, nxt % TILES)
                    what = attn_kind(t)
                    if what[0] not in "KQ":
                        continue
                    n = ROPED.index(t)
                    w_ = what[1]
                    pool.wait_ge(turned_ready, 3 * len(ROPED) * g + 3 * n + 3)
                    if t == 0:
                        pool.wait_ge(masked_ready, len(SCORES) * g)
                        pool.wait_ge(s_masked, 4 * g)
                        pool.wait_ge(kv_rows_ready, 3 * NW * g)
                    elif what[0] == "K":
                        filled(pool, st, ("S", w_ - 1, NH - 1, len(UNITS[w_ - 1]) - 1))
                    elif w_:
                        filled(pool, st, ("S", w_ - 1, what[2], len(UNITS[w_ - 1]) - 1))
                    dst, new = (k[:, :], ks[:, w_, :]) if what[0] == "K" else (q[:, what[2], :], qs[:, w_, :, what[2], :])
                    d = WINDOWS[w_][1]
                    a, b = straight[:, 0:SEQ], crossed[:, 0:SEQ]
                    if d > 1:
                        dst = dst.rearrange("p (r m) -> p m r", r=d)
                        a, b = (x.rearrange("p (m r) -> p m r", r=d) for x in (a, b))
                    pool.tensor_tensor(dst, a, b, ALU.add).then_inc(qk_ready, 1)
                    a, b = straight[:, SEQ:TOK], crossed[:, SEQ:TOK]
                    if what[0] == "Q":
                        a, b = (x.rearrange("p (i t) -> p i t", i=4) for x in (a, b))
                    pool.tensor_tensor(new, a, b, ALU.add).then_inc(qk_ready, 1)

            all_groups(pool, ATTN, stage)


GT = 10
XBC = 6
HG = 8
PD = 64
GW = HG * PD
ST = 128
TAPS = 4
PRE = TAPS - 1
WIDE = SEQ + PRE + NB * (NT + PRE)
COMP = WIDE - PRE
PAR = NB * PRE + TAPS + 1
TAIL = PRE + NB * PRE


B_AT, C_AT, X_AT = 0, 5, (1, 2, 3, 4)
RUNS = ((B_AT, 1), (X_AT[0], 4), (C_AT, 1))


def ssd_columns(t, e):
    if t == B_AT:
        return 2 * INNER + e * ST
    if t == C_AT:
        return 2 * INNER + NG * ST + e * ST
    if t < XBC:
        return INNER + e * GW + X_AT.index(t) * P
    return e * GW + (t - XBC) * P


def channel(t, e):
    return ssd_columns(t, e) - INNER


SSD_AHEAD = {
    -1: [("PAR",)],
    6: [("BT",), ("AC",), ("AT",), ("AS",), ("X", 0), ("BS",), ("X", 1)],
    7: [("CB",), ("CS",), ("HT", 0), ("DEC",), ("HT", 1), ("X", 2), ("BA", 0)],
    8: [("BB", 0), ("HT", 2), ("YD", 0), ("HT", 3), ("ST", 0), ("HT", 4), ("HT", 5), ("TB",), ("BA", 1), ("BB", 1),
        ("YO", 1)],
    9: [("HT", 6), ("ST", 1), ("HT", 7), ("YD", 1), ("TX",), ("X", 3), ("X", 4), ("OQ",), ("BA", 2), ("BB", 2)],
}
SSD_BEHIND = {
    0: [("YO", 2), ("ST", 2), ("YD", 2), ("BA", 3), ("BB", 3), ("BA", 4), ("BB", 4), ("YO", 3)],
    1: [("ST", 3), ("YD", 3), ("YO", 4), ("YD", 4)],
    2: [("FS",), ("Z", 0), ("HN", 0), ("Z", 1), ("HN", 1)],
    3: [("Z", 2), ("HN", 2), ("Z", 3), ("HN", 3), ("Z", 4), ("HN", 4)],
    4: [("HN", 5), ("HN", 6), ("HN", 7)],
    5: [("YT", c) for c in range(TT)],
}
BANKS = 3
SSD = Plan(SSD_AHEAD, SSD_BEHIND, GT, BANKS, ("OQ",))
SSD_CONSTS = 7
Y_STEPS = 2 * (TT - 1)


def ssd_phase(nc, uhi, ulo, ident, w_in_dram, tables, params, states, y_dram, p_out, s_out_dram):
    conv_w, conv_b, dt_bias, a_log, d_skip, norm_w = params
    state_ssm, state_conv = states
    p_ssm, p_conv = p_out
    s_ssm, s_conv = s_out_dram
    with ExitStack() as ctx:
        m = Mem(nc, ctx, "sd")
        tri = m.sb("tri", [P, P])
        tri_s = m.sb("tri_s", [NS, NS])
        mask = m.sb("mask", [P, P])
        mask_s = m.sb("mask_s", [NS, NS])
        own = m.sb("own", [NS, NB])
        pick_f = m.sb("pick_f", [HG, HG * P])
        pick = m.sb("pick", [HG, HG * P], F32R)
        spread = m.sb("spread", [HG, 4, P])
        zero = m.sb("zero", [P, 1])
        rows = m.sb("rows", [P, 3, NG * HG])
        a_neg = m.sb("a_neg", [P, NG * HG])
        w = m.sb("w", [P, PAIR, KD * P])
        whi = m.sb("whi", [P, PAIR, KD * P], F32R)
        wlo = m.sb("wlo", [P, PAIR, KD * P], F32R)
        wd = m.sb("wd", [P, KD, NG * HG])
        wdhi = m.sb("wdhi", [P, KD, NG * HG], F32R)
        wdlo = m.sb("wdlo", [P, KD, NG * HG], F32R)
        dt_f = m.sb("dt_f", [NG * HG, TOK])
        dt = m.sb("dt", [P, TT, NG * HG])
        dta = m.sb("dta", [P, TT, NG * HG])
        sp_a = m.sb("sp_a", [P, TT, NG * HG])
        sp_b = m.sb("sp_b", [P, TT, NG * HG])
        sp_c = m.sb("sp_c", [P, TT, NG * HG])
        dt_e = m.sb("dt_e", [P, TT, HG])
        dta_e = m.sb("dta_e", [P, TT, HG])
        d_e = m.sb("d_e", [P, HG])
        acs = m.sb("acs", [P, TT, HG])
        acs_exp = m.sb("acs_exp", [P, TT, HG])
        acs_f = m.sb("acs_f", [HG, TOK])
        acs_hi = m.sb("acs_hi", [HG, TOK], F32R)
        acs_lo = m.sb("acs_lo", [HG, TOK], F32R)
        last_exp = m.sb("last_exp", [HG, NB])
        decay_rows = m.sb("decay_rows", [P, 4, NB])
        par_rows = m.sb("par_rows", [PAR, XBC * P])
        par = m.sb("par", [P, XBC, PAR])
        raw = m.sb("raw", [P, WIDE])
        conv = m.sb("conv", [P, 2, WIDE])
        tails = m.sb("tails", [P, XBC, TAIL])
        tail_rows = m.sb("tail_rows", [TAIL, XBC * P])
        xbc = m.sb("xbc", [P, XBC, TOK])
        z = m.sb("z", [P, 4, TOK])
        b_rows = m.sb("b_rows", [P, TT, ST])
        b_own = m.sb("b_own", [NS, NB, ST])
        cb = m.sb("cb", [P, TT, P])
        norm_row = m.sb("norm_row", [P, GW])
        x_rows = m.sb("x_rows", [P, TT, GW])
        x_dt = m.sb("x_dt", [P, 2, GW])
        x_end = m.sb("x_end", [P, 2, GW])
        x_d = m.sb("x_d", [P, 2, GW])
        decay = m.sb("decay", [P, 2, HG, P])
        to_end = m.sb("to_end", [P, 2, HG])
        chunk_decay = m.sb("chunk_decay", [P, 2, HG])
        state = m.sb("state", [P, GW])
        state_rows = m.sb("state_rows", [P, 4, ST])
        h0 = m.sb("h0", [P, 4, NB, ST])
        h0_t = m.sb("h0_t", [P, 2, 4 * P])
        off_t = m.sb("off_t", [P, 4 * NS])
        y = m.sb("y", [P, TT, GW])
        square = m.sb("square", [P, GW])
        stats = m.sb("stats", [P, 3, TT])
        proj = m.ps("proj", [P, PAIR, 2, 512])
        small = [m.ps(f"small{b}", [P, 512]) for b in range(BANKS)]
        held = m.ps("held", [P, 512])

        s = m.sem
        held_back = s("held_back")
        wd_in, consts_in, w_in, = s("wd_in"), s("consts_in"), [s(f"w_in{r}") for r in range(PAIR)]
        whi_ready, wlo_ready, proj_ready = s("whi_ready"), s("wlo_ready"), s("proj_ready")
        proj_free = [s(f"proj_free{r}") for r in range(PAIR)]
        small_ready = [s(f"small_ready{b}") for b in range(BANKS)]
        small_free = [s(f"small_free{b}") for b in range(BANKS)]
        setup = s("setup")
        setup_act = s("setup_act")
        setup_pe = s("setup_pe")
        pick_ready = s("pick_ready")
        par_in, h0_in, norm_in = s("par_in"), s("h0_in"), s("norm_in")
        slices_ready = s("slices_ready")
        par_ready, acs_ready, acs_exp_ready = s("par_ready"), s("acs_ready"), s("acs_exp_ready")
        acs_f_ready, acs_hi_ready, acs_lo_ready = s("acs_f_ready"), s("acs_hi_ready"), s("acs_lo_ready")
        last_exp_ready, decay_rows_ready = s("last_exp_ready"), s("decay_rows_ready")
        raw_ready, past_ready, tail_ready, raw_free = s("raw_ready"), s("past_ready"), s("tail_ready"), s("raw_free")
        tap0_ready, conv_ready, xbc_ready, z_ready = s("tap0_ready"), s("conv_ready"), s("xbc_ready"), s("z_ready")
        b_rows_ready, b_own_ready, cb_ready = s("b_rows_ready"), s("b_own_ready"), s("cb_ready")
        h0_t_ready, off_done, off_t_ready = s("h0_t_ready"), s("off_done"), s("off_t_ready")
        x_rows_ready, x_dt_ready, x_d_ready, x_end_ready = s("x_rows_ready"), s("x_dt_ready"), s("x_d_ready"), s("x_end_ready")
        seg_ready, decay_ready, chunk_decay_ready = s("seg_ready"), s("decay_ready"), s("chunk_decay_ready")
        to_end_ready, weights_ready = s("to_end_ready"), s("weights_ready")
        state_step, state_ready = s("state_step"), s("state_ready")
        y_step, y_ready = s("y_step"), s("y_ready")
        tails_ready, tails_stored = s("tails_ready"), s("tails_stored")
        final_ready, final_stored = s("final_ready"), s("final_stored")
        h0_scaled, h0_new, h0_stored = s("h0_scaled"), s("h0_new"), s("h0_stored")
        z_silu, gated, squares, mean_ready, inv_ready, rstd_ready = \
            s("z_silu"), s("gated"), s("squares"), s("mean_ready"), s("inv_ready"), s("rstd_ready")
        normed, out_ready, y_stored = s("normed"), s("out_ready"), s("y_stored")
        block = ctx.enter_context(nc.Block())
        span = [slice(c * P, c * P + ROWS[c]) for c in range(TT)]

        def bank(st, item):
            return small[st.place(item)[0]]

        def filled(eng, st, item):
            b, ahead = st.place(item)
            eng.wait_ge(small_ready[b], ahead + 1)

        def hold(eng):
            eng.sem_inc(held_back, 1)

        def free(eng, st, item):
            eng.sem_inc(small_free[st.place(item)[0]], 1)

        def heads(ap):
            return ap.rearrange("p (h d) -> p h d", h=HG)

        def per_head(ap):
            return ap.unsqueeze(2).broadcast_to([ap.shape[0], HG, PD])

        @block.sync
        def _(sp):
            def load_w(e, t, slot):
                src = w_in_dram.rearrange("(k p) n -> p k n", p=P)[:, :, bass.ds(ssd_columns(t, e), P)]
                sp.dma_start(w[:, slot].rearrange("p (k n) -> p k n", k=KD), src).then_inc(w_in[slot], 16)

            consts = ((tri[:, :], tables["tri"]), (tri_s[:, :], tables["tri_s"]), (mask[:, :], tables["mask"]),
                      (mask_s[:, :], tables["mask_ss"]), (own[:, :], tables["own"]), (pick_f[:, :], tables["pick"]),
                      (spread[:, :, :], tables["spread"]))
            assert len(consts) == SSD_CONSTS

            def stage(st):
                e, g = st.head, st.tail
                for t in range(GT):
                    if t == 0 and e is not None:
                        sp.wait_ge(par_ready, e)
                        for k, n in RUNS:
                            lo, hi, at = k * P, (k + n) * P, bass.ds(channel(k, e), n * P)
                            past = state_conv[0].rearrange("n k c -> (n k) c")[:, at]
                            sp.dma_start(par_rows[0:NB * PRE, lo:hi], past).then_inc(par_in, 16)
                            sp.dma_start(par_rows[NB * PRE:NB * PRE + TAPS, lo:hi], conv_w[0][:, at]).then_inc(par_in, 16)
                            sp.dma_start(par_rows[NB * PRE + TAPS:PAR, lo:hi], conv_b[:, at]).then_inc(par_in, 16)
                    if e is not None:
                        if st.tail is None and t == 1:
                            for dst, src in consts:
                                sp.dma_start(dst, src).then_inc(consts_in, 16)
                        sp.wait_ge(wlo_ready, GT * e + t + PAIR + 1)
                        nxt = t + 2 * PAIR
                        hold(sp)
                        load_w(e + nxt // GT, nxt % GT, t % PAIR)
                    if t == 4 and g is not None:
                        sp.wait_ge(final_ready, g + 1)
                        sp.dma_start(p_ssm[0, 0].rearrange("h p s -> (h p) s")[bass.ds(GW * g, GW)]
                                     .rearrange("(j q) s -> q j s", q=P), state_rows[:, :, :]).then_inc(final_stored, 16)
                        for j in range(4):
                            sp.wait_ge(h0_new, 8 * g + 2 * j + 2)
                            sp.dma_start(s_ssm[0].rearrange("n h p s -> (h p) n s")[bass.ds(GW * g + P * j, P)], h0[:, j]) \
                                .then_inc(h0_stored, 16)
                        sp.wait_ge(out_ready, TT * g + TT)
                        sp.dma_start(y_dram[bass.ds(4 * g, 4)].rearrange("k p t -> p k t"), z[:, :, :]).then_inc(y_stored, 16)
                    if t == 4 and e is not None:
                        sp.wait_ge(normed, TT * e)
                        sp.dma_start(norm_row[:, :], norm_w[0, bass.ds(GW * e, GW)].partition_broadcast(P)) \
                            .then_inc(norm_in, 16)
                        sp.wait_ge(h0_stored, 16 * 4 * e)
                        for j in range(4):
                            src = state_ssm[0].rearrange("n h p s -> (h p) n s")[bass.ds(GW * e + P * j, P)]
                            sp.dma_start(h0[:, j], src).then_inc(h0_in, 16)
                if e is not None:
                    sp.wait_ge(tails_ready, 2 * e + 2)
                    hold(sp)
                    for k, n in RUNS:
                        lo, hi, at = k * P, (k + n) * P, bass.ds(channel(k, e), n * P)
                        sp.dma_start(p_conv[0, 0][:, at], tail_rows[0:PRE, lo:hi]).then_inc(tails_stored, 16)
                        sp.dma_start(s_conv[0].rearrange("n k c -> (n k) c")[:, at], tail_rows[PRE:TAIL, lo:hi]) \
                            .then_inc(tails_stored, 16)

            for t in range(PAIR):
                load_w(0, t, t)
            dt_in = ((wd[:, :, :], w_in_dram.rearrange("(k p) n -> p k n", p=P)[:, :, 2 * INNER + 2 * NG * ST:]),
                     (rows[:, 0, :], bcast_rows(dt_bias)), (rows[:, 1, :], bcast_rows(a_log)),
                     (rows[:, 2, :], bcast_rows(d_skip)))
            for dst, src in dt_in:
                sp.dma_start(dst, src).then_inc(wd_in, 16)
            for t in range(PAIR):
                sp.wait_ge(wlo_ready, t + 1)
                load_w(0, PAIR + t, t)
            all_groups(sp, SSD, stage)
            sp.wait_ge(y_stored, 16 * NG)
            sp.wait_ge(h0_stored, 16 * 4 * NG)
            sp.wait_ge(final_stored, 16 * NG)
            sp.wait_ge(tails_stored, 16 * 2 * len(RUNS) * NG)
            for r in range(PAIR):
                sp.wait_ge(w_in[r], 16 * (GT * NG // PAIR + 2))

        @block.tensor
        def _(pe):
            def turn(out, ins, one):
                return pe.matmul(out, ins, one, is_transpose=True, start=True, stop=True)

            def project(e, t, q):
                r = t % PAIR
                if q == 0:
                    pe.wait_ge(wlo_ready, GT * e + t + 1)
                    pe.wait_ge(proj_free[r], GT // PAIR * e + t // PAIR)
                for kk in range(KD // 4 * q, KD // 4 * (q + 1)):
                    for a, b in ((whi, uhi), (whi, ulo), (wlo, uhi)):
                        for h in range(2):
                            last = pe.matmul(proj[:, r, h, 0:HALF], a[:, r, kk * P:(kk + 1) * P],
                                             b[:, kk, h * HALF:(h + 1) * HALF],
                                             start=(kk == 0 and a is whi and b is uhi),
                                             stop=(kk == KD - 1 and a is wlo))
                if q == 3:
                    last.then_inc(proj_ready, 1)

            def item_(st, e, item):
                n, ahead = st.place(item)
                b = small[n]
                pe.wait_ge(small_free[n], ahead)
                what = item[0]
                c = item[1] if len(item) > 1 else None
                if what == "PAR":
                    pe.wait_ge(par_in, 16 * 3 * len(RUNS) * (e + 1))
                    hold(pe)
                    for j in range(XBC):
                        last = turn(b[:, j * PAR:(j + 1) * PAR], par_rows[:, j * P:(j + 1) * P], ident[0:PAR, 0:PAR])
                elif what == "AC":
                    pe.wait_ge(slices_ready, 3 * e + 3)
                    pe.wait_ge(consts_in, 16 * SSD_CONSTS)
                    for i in range(TT - 1):
                        last = pe.matmul(b[:, i * HG:(i + 1) * HG], tri[:, :], dta_e[:, i, :], start=True, stop=True)
                    last = pe.matmul(b[0:NS, (TT - 1) * HG:TT * HG], tri_s[:, :], dta_e[0:NS, TT - 1, :],
                                     start=True, stop=True)
                elif what == "AT":
                    for i in range(TT - 1):
                        last = pe.matmul(b[0:HG, span[i]], dta_e[:, i, :], tri[:, :], start=True, stop=True)
                elif what == "AS":
                    hold(pe)
                    last = pe.matmul(b[0:HG, 0:NS], dta_e[0:NS, TT - 1, :], tri_s[:, :], start=True, stop=True)
                elif what == "BT":
                    pe.wait_ge(xbc_ready, XBC * e + B_AT + 1)
                    for i in range(TT - 1):
                        last = turn(b[:, i * ST:(i + 1) * ST], xbc[:, B_AT, span[i]], ident[:, :])
                elif what == "BS":
                    last = turn(b[0:NS, 0:ST], xbc[:, B_AT, span[TT - 1]], ident[:, :])
                elif what == "CB":
                    pe.wait_ge(xbc_ready, XBC * e + C_AT + 1)
                    for i in range(TT - 1):
                        last = pe.matmul(b[:, i * P:(i + 1) * P], xbc[:, B_AT, span[i]], xbc[:, C_AT, span[i]],
                                         start=True, stop=True)
                elif what == "CS":
                    hold(pe)
                    last = pe.matmul(b[0:NS, 0:NS], xbc[:, B_AT, span[TT - 1]], xbc[:, C_AT, span[TT - 1]],
                                     start=True, stop=True)
                elif what == "DEC":
                    pe.wait_ge(last_exp_ready, e + 1)
                    for j in range(4):
                        last = pe.matmul(b[:, j * NB:(j + 1) * NB], spread[:, j, :], last_exp[:, :],
                                         start=True, stop=True)
                elif what == "HT":
                    pe.wait_ge(h0_in, 16 * 4 * (e + 1))
                    for i in range(4):
                        last = turn(b[:, i * P:(i + 1) * P], h0[:, c // 2, 4 * (c % 2) + i, :], ident[:, :])
                elif what == "TB":
                    pe.wait_ge(tail_ready, 2 * XBC * e + 8)
                    for j in range(4):
                        last = turn(b[0:TAIL, j * P:(j + 1) * P], tails[:, j, :], ident[:, :])
                elif what == "TX":
                    pe.wait_ge(tail_ready, 2 * XBC * e + 2 * XBC)
                    for j in range(2):
                        last = turn(b[0:TAIL, j * P:(j + 1) * P], tails[:, 4 + j, :], ident[:, :])
                elif what == "X":
                    pe.wait_ge(xbc_ready, XBC * e + X_AT[-1] + 1)
                    for j in range(4):
                        last = turn(b[0:ROWS[c], j * P:(j + 1) * P], xbc[:, X_AT[j], span[c]], ident[:, :])
                elif what in ("BA", "BB"):
                    pe.wait_ge(acs_lo_ready, e + 1)
                    pe.wait_ge(pick_ready, 1)
                    r = ROWS[c]
                    for i in range(4):
                        h = i + (4 if what == "BB" else 0)
                        pe.matmul(b[0:P, i * r:(i + 1) * r], pick[:, h * P:(h + 1) * P], acs_hi[:, span[c]],
                                  start=True, stop=False)
                        last = pe.matmul(b[0:P, i * r:(i + 1) * r], pick[:, h * P:(h + 1) * P], acs_lo[:, span[c]],
                                         start=False, stop=True)
                elif what == "ST":
                    pe.wait_ge(x_end_ready, TT * e + c + 1)
                    pe.wait_ge(b_rows_ready, 2 * e + 1)
                    last = pe.matmul(b[:, :], b_rows[:, c, :], x_end[:, c % 2, :], start=True, stop=True)
                elif what == "YD":
                    pe.wait_ge(weights_ready, TT * e + c + 1)
                    pe.wait_ge(x_dt_ready, TT * e + c + 1)
                    r = ROWS[c]
                    if r < P:
                        hold(pe)
                    for h in range(HG):
                        last = pe.matmul(b[0:r, h * PD:(h + 1) * PD], decay[0:r, c % 2, h, 0:r],
                                         x_dt[0:r, c % 2, h * PD:(h + 1) * PD], start=True, stop=True)
                elif what == "YO":
                    if c < TT - 1:
                        pe.wait_ge(state_ready, 4 * e + c)
                        last = pe.matmul(b[:, :], xbc[:, C_AT, span[c]], state[:, :], start=True, stop=True)
                    else:
                        pe.wait_ge(off_t_ready, e + 1)
                        for j in range(4):
                            last = turn(b[0:NS, j * P:(j + 1) * P], off_t[:, j * NS:(j + 1) * NS], ident[:, :])
                elif what == "FS":
                    pe.wait_ge(state_ready, 4 * e + 4)
                    for j in range(4):
                        last = turn(b[:, j * P:(j + 1) * P], state[:, j * P:(j + 1) * P], ident[:, :])
                elif what == "HN":
                    pe.wait_ge(x_end_ready, TT * e + TT)
                    pe.wait_ge(b_own_ready, e + 1)
                    j, half = c // 2, c % 2
                    last = pe.matmul(b[:, :], x_end[0:NS, 0, j * P:(j + 1) * P],
                                     b_own[:, 4 * half:4 * half + 4, :].rearrange("p n s -> p (n s)"),
                                     start=True, stop=True)
                elif what == "Z":
                    pe.wait_ge(z_silu, e + 1)
                    for j in range(4):
                        last = turn(b[0:ROWS[c], j * P:(j + 1) * P], z[:, j, span[c]], ident[:, :])
                elif what == "YT":
                    pe.wait_ge(normed, TT * e + c + 1)
                    r = ROWS[c]
                    if r < P:
                        hold(pe)
                    for j in range(4):
                        last = turn(b[:, j * r:(j + 1) * r], y[0:r, c, j * P:(j + 1) * P], ident[0:r, 0:r])
                last.then_inc(small_ready[n], 1)

            def from_old(e, i):
                pe.wait_ge(h0_t_ready, 8 * e + i + 1)
                if i == 0:
                    pe.wait_ge(off_t_ready, e)
                for n in range(4):
                    seq = 4 * (i % 2) + n
                    at = (i // 2) * NS + NT * seq
                    last = pe.matmul(held[:, at:at + NT], h0_t[:, i % 2, n * P:(n + 1) * P],
                                     xbc[:, C_AT, SEQ + NT * seq:SEQ + NT * seq + NT], start=True, stop=True)
                last.then_inc(off_done, 1)

            def all_dt():
                pe.wait_ge(setup, 2)
                for kk in range(KD):
                    for a, b in ((wdhi, uhi), (wdhi, ulo), (wdlo, uhi)):
                        for h in range(2):
                            last = pe.matmul(small[1 + h][0:NG * HG, 0:HALF], a[:, kk, :], b[:, kk, h * HALF:(h + 1) * HALF],
                                             start=(kk == 0 and a is wdhi and b is uhi),
                                             stop=(kk == KD - 1 and a is wdlo))
                last.then_inc(setup_pe, 1)

            def turn_dt():
                pe.wait_ge(setup_act, 2)
                for c in range(TT):
                    last = turn(held[0:ROWS[c], c * NG * HG:(c + 1) * NG * HG], dt_f[:, span[c]],
                                ident[0:NG * HG, 0:NG * HG])
                last.then_inc(setup_pe, 1)

            def run(st, items):
                for item, e in items:
                    if item == ("OQ",):
                        from_old(e, 7)
                        continue
                    item_(st, e, item)
                    if item[0] == "HT" and item[1] >= 1:
                        from_old(e, item[1] - 1)

            def stage(st):
                for t in range(GT):
                    for q in range(4):
                        if st.head is not None:
                            project(st.head, t, q)
                        if q < 3 and t > 0:
                            run(st, st.part(t - 1, q + 1))
                    if t == 0:
                        run(st, st.items(-1))
                    if st.tail is None and t == 0:
                        all_dt()
                    if st.tail is None and t == 1:
                        turn_dt()
                    run(st, st.part(t, 0))
                run(st, st.rest(GT - 1))

            all_groups(pe, SSD, stage)

        @block.scalar
        def _(act):
            def w_high(e, t):
                act.wait_ge(w_in[t % PAIR], GT // PAIR * 16 * e + 16 * (t // PAIR) + 16)
                act.activation(whi[:, t % PAIR], w[:, t % PAIR], ACT.Copy).then_inc(whi_ready, 1)

            def copied(st, item, dst, src, signal, value):
                filled(act, st, item)
                act.activation(dst, src, ACT.Copy).then_inc(signal, 1)
                act.wait_ge(signal, value)
                free(act, st, item)

            def raw_out(e, t):
                act.wait_ge(setup, 1)
                x = proj[:, t % PAIR]
                act.wait_ge(raw_free, XBC * e + t)
                act.activation(raw[:, PRE:PRE + HALF], x[:, 0, 0:HALF], ACT.Copy)
                act.activation(raw[:, PRE + HALF:PRE + SEQ], x[:, 1, 0:SEQ - HALF], ACT.Copy)
                new = raw[:, PRE + SEQ:WIDE].rearrange("p (n k) -> p n k", n=NB)[:, :, PRE:PRE + NT]
                act.activation(new, x[:, 1, SEQ - HALF:HALF].rearrange("p (n k) -> p n k", n=NB), ACT.Copy) \
                    .then_inc(raw_ready, 1)
                act.wait_ge(raw_ready, XBC * e + t + 1)
                act.sem_inc(proj_free[t % PAIR], 1)

            def first_tap(e, t):
                act.wait_ge(past_ready, XBC * e + t + 1)
                act.activation(conv[:, 0, 0:COMP], raw[:, 0:COMP], ACT.Identity, scale=par[:, t, NB * PRE:NB * PRE + 1],
                               bias=par[:, t, PAR - 1:PAR]).then_inc(tap0_ready, 1)

            def silu(e, t):
                act.wait_ge(conv_ready, 3 * (XBC * e + t) + 3)
                act.activation(xbc[:, t, 0:SEQ], conv[:, 1, 0:SEQ], ACT.Silu)
                runs = conv[:, 1, SEQ + PRE:WIDE].rearrange("p (n k) -> p n k", n=NB)
                act.activation(xbc[:, t, SEQ:TOK].rearrange("p (n k) -> p n k", n=NB), runs[:, :, 0:NT], ACT.Silu) \
                    .then_inc(xbc_ready, 1)

            def all_dt():
                act.wait_ge(setup_pe, 1)
                for h in range(2):
                    last = act.activation(dt_f[:, h * HALF:(h + 1) * HALF], small[1 + h][0:NG * HG, 0:HALF], ACT.Copy)
                last.then_inc(setup_act, 1)

            def soften():
                act.activation(a_neg[:, :], rows[:, 1, :], ACT.Exp).then_inc(setup_act, 1)
                act.wait_ge(setup, 7)
                act.activation(sp_b[:, :, :], sp_b[:, :, :], ACT.Exp).then_inc(setup_act, 1)
                act.wait_ge(consts_in, 16 * SSD_CONSTS)
                act.activation(pick[:, :], pick_f[:, :], ACT.Copy).then_inc(pick_ready, 1)

            for t in range(PAIR):
                w_high(0, t)
            act.wait_ge(wd_in, 16 * 4)
            act.activation(wdhi[:, :, :], wd[:, :, :], ACT.Copy).then_inc(setup_act, 1)

            def run(st, items):
                for item, e in items:
                    what = item[0]
                    c = item[1] if len(item) > 1 else None
                    b = bank(st, item) if what != "OQ" else None
                    if what == "PAR":
                        copied(st, item, par[:, :, :].rearrange("p t k -> p (t k)"), b[:, 0:XBC * PAR], par_ready, e + 1)
                    elif what == "AC":
                        filled(act, st, item)
                        act.wait_ge(y_ready, TT * e)
                        act.activation(acs[:, 0:TT - 1, :].rearrange("p c h -> p (c h)"), b[:, 0:(TT - 1) * HG], ACT.Copy)
                        act.activation(acs[0:NS, TT - 1, :], b[0:NS, (TT - 1) * HG:TT * HG], ACT.Copy)
                        act.activation(acs_exp[:, 0:TT - 1, :].rearrange("p c h -> p (c h)"), b[:, 0:(TT - 1) * HG], ACT.Exp)
                        act.activation(acs_exp[0:NS, TT - 1, :], b[0:NS, (TT - 1) * HG:TT * HG], ACT.Exp) \
                            .then_inc(acs_ready, 1)
                        act.wait_ge(acs_ready, e + 1)
                        free(act, st, item)
                    elif what == "AT":
                        act.wait_ge(acs_lo_ready, e)
                        copied(st, item, acs_f[:, 0:SEQ], b[0:HG, :], acs_f_ready, 2 * e + 1)
                    elif what == "AS":
                        filled(act, st, item)
                        act.activation(last_exp[:, :], b[0:HG, 0:NS].rearrange("p (n t) -> p n t", t=NT)[:, :, NT - 1],
                                       ACT.Exp).then_inc(last_exp_ready, 1)
                        copied(st, item, acs_f[:, SEQ:TOK], b[0:HG, 0:NS], acs_f_ready, 2 * e + 2)
                        act.activation(acs_hi[:, :], acs_f[:, :], ACT.Copy).then_inc(acs_hi_ready, 1)
                    elif what == "BT":
                        copied(st, item, b_rows[:, 0:TT - 1, :].rearrange("p c s -> p (c s)"), b[:, :], b_rows_ready, 2 * e + 1)
                    elif what == "BS":
                        copied(st, item, b_rows[0:NS, TT - 1, :], b[0:NS, 0:ST], b_rows_ready, 2 * e + 2)
                    elif what == "CB":
                        copied(st, item, cb[:, 0:TT - 1, :].rearrange("p c i -> p (c i)"), b[:, :], cb_ready, 2 * e + 1)
                    elif what == "CS":
                        copied(st, item, cb[0:NS, TT - 1, 0:NS], b[0:NS, 0:NS], cb_ready, 2 * e + 2)
                    elif what == "DEC":
                        act.wait_ge(h0_scaled, 8 * e)
                        copied(st, item, decay_rows[:, :, :].rearrange("p j n -> p (j n)"), b[:, 0:4 * NB],
                               decay_rows_ready, e + 1)
                    elif what == "TB":
                        act.wait_ge(tails_stored, 16 * 2 * len(RUNS) * e)
                        copied(st, item, tail_rows[:, 0:4 * P], b[0:TAIL, :], tails_ready, 2 * e + 1)
                    elif what == "TX":
                        copied(st, item, tail_rows[:, 4 * P:], b[0:TAIL, 0:2 * P], tails_ready, 2 * e + 2)
                    elif what == "X":
                        act.wait_ge(x_d_ready, TT * e)
                        copied(st, item, x_rows[0:ROWS[c], c, :], b[0:ROWS[c], :], x_rows_ready, TT * e + c + 1)
                    elif what == "BB":
                        r = ROWS[c]
                        act.wait_ge(seg_ready, TT * e + c + 1)
                        if c < TT - 1:
                            for i, it in enumerate((("BA", c), ("BB", c))):
                                last = act.activation(chunk_decay[:, c % 2, 4 * i:4 * i + 4],
                                                      bank(st, it)[:, :].rearrange("p (h i) -> p h i", h=4)[:, :, P - 1],
                                                      ACT.Exp)
                            last.then_inc(chunk_decay_ready, 1)
                        act.activation(decay[0:r, c % 2, :, 0:r], decay[0:r, c % 2, :, 0:r], ACT.Exp) \
                            .then_inc(decay_ready, 1)
                    elif what == "OQ":
                        act.wait_ge(off_done, 8 * e + 8)
                        act.activation(off_t[:, :], held[:, 0:4 * NS], ACT.Copy).then_inc(off_t_ready, 1)
                    elif what == "FS":
                        act.wait_ge(final_stored, 16 * e)
                        copied(st, item, state_rows[:, :, :].rearrange("p j s -> p (j s)"), b[:, :], final_ready, e + 1)
                    elif what == "Z":
                        r = ROWS[c]
                        act.wait_ge(gated, TT * e + c + 1)
                        act.wait_ge(squares, TT * e + c)
                        act.activation(square[0:r, :], y[0:r, c, :], ACT.Square, accum_out=stats[0:r, 0, c:c + 1]) \
                            .then_inc(squares, 1)
                        if c == TT - 1:
                            act.wait_ge(inv_ready, e + 1)
                            act.activation(stats[:, 2, :], stats[:, 1, :], ACT.Sqrt).then_inc(rstd_ready, 1)
                    elif what == "YT":
                        r = ROWS[c]
                        copied(st, item, z[:, :, span[c]], b[:, 0:4 * r].rearrange("p (j t) -> p j t", j=4),
                               out_ready, TT * e + c + 1)

            def stage(st):
                h = st.head
                for t in range(-1, GT):
                    if t >= 0 and h is not None:
                        if t == 1:
                            act.wait_ge(x_rows_ready, TT * h)
                            act.wait_ge(off_done, 8 * h)
                        if t == XBC and st.tail is not None:
                            filled(act, st, ("YO", 3))
                        if 1 <= t <= XBC:
                            silu(h, t - 1)
                        act.wait_ge(proj_ready, GT * h + t + 1)
                        if t < XBC:
                            raw_out(h, t)
                        nxt = t + PAIR
                        w_high(h + nxt // GT, nxt % GT)
                        if t < XBC:
                            first_tap(h, t)
                        else:
                            if t == XBC:
                                act.wait_ge(y_stored, 16 * h)
                            act.activation(two(z[:, t - XBC, :]), halves(proj[:, t % PAIR]), ACT.Copy).then_inc(z_ready, 1)
                            act.wait_ge(z_ready, 4 * h + t - XBC + 1)
                            act.sem_inc(proj_free[t % PAIR], 1)
                    if st.tail is None and t == 0:
                        all_dt()
                    if st.tail is None and t == 1:
                        soften()
                    if t == 1 and st.tail is not None:
                        act.activation(z[:, :, :], z[:, :, :], ACT.Silu).then_inc(z_silu, 1)
                    run(st, st.items(t))

            all_groups(act, SSD, stage)

        @block.vector
        def _(dve):
            steps = 0

            def then(ins):
                nonlocal steps
                ins.then_inc(setup, 1)
                steps += 1
                dve.wait_ge(setup, steps)

            then(dve.memset(raw[:, :], 0.0))
            dve.wait_ge(setup_act, 1)
            then(dve.tensor_tensor(wdlo[:, :, :], wd[:, :, :], wdhi[:, :, :].bitcast(F32), ALU.subtract))

            def soften():
                dve.wait_ge(setup_pe, 2)
                n = NG * HG
                then(dve.memset(sp_a[:, :, :], 0.0))
                bias = rows[:, 0, :].unsqueeze(1).broadcast_to([P, TT - 1, n])
                dve.tensor_tensor(sp_a[:, 0:TT - 1, :], held[:, 0:(TT - 1) * n].rearrange("p (c h) -> p c h", h=n),
                                  bias, ALU.add)
                then(dve.tensor_tensor(sp_a[0:NS, TT - 1, :], held[0:NS, (TT - 1) * n:TT * n], rows[0:NS, 0, :],
                                       ALU.add))
                a_, b_, c_ = (x[:, :, :] for x in (sp_a, sp_b, sp_c))
                then(dve.tensor_scalar(b_, a_, -1.0, None, ALU.mult))
                then(dve.tensor_tensor(b_, a_, b_, ALU.min))
                then(dve.tensor_scalar(a_, a_, 0.0, None, ALU.max))
                dve.wait_ge(setup_act, 4)
                then(dve.tensor_scalar(c_, b_, 2.0, None, ALU.add))
                then(dve.reciprocal(c_, c_))
                then(dve.tensor_tensor(b_, b_, c_, ALU.mult))
                then(dve.tensor_tensor(c_, b_, b_, ALU.mult))
                poly = dt[:, :, :]
                then(dve.tensor_scalar(poly, c_, 1.0 / 19, 1.0 / 17, ALU.mult, ALU.add))
                for k in (15, 13, 11, 9, 7, 5, 3, 1):
                    then(dve.tensor_tensor(poly, poly, c_, ALU.mult))
                    then(dve.tensor_scalar(poly, poly, 1.0 / k, None, ALU.add))
                then(dve.tensor_tensor(poly, poly, b_, ALU.mult))
                then(dve.scalar_tensor_tensor(out=poly, in0=poly, scalar=2.0, in1=a_, op0=ALU.mult, op1=ALU.add))
                dve.wait_ge(setup_act, 3)
                then(dve.tensor_scalar(a_neg[:, :], a_neg[:, :], -1.0, None, ALU.mult))
                then(dve.tensor_tensor(dta[:, :, :], poly, a_neg[:, :].unsqueeze(1).broadcast_to([P, TT, n]), ALU.mult))
                then(dve.memset(stats[:, :, :], 1.0))

            def taps(e, t):
                dve.wait_ge(tap0_ready, XBC * e + t + 1)
                dve.wait_ge(xbc_ready, XBC * e + t)
                at = 3 * (XBC * e + t)
                for k in range(1, TAPS):
                    dve.scalar_tensor_tensor(out=conv[:, k % 2, 0:COMP], in0=raw[:, k:k + COMP],
                                             scalar=par[:, t, NB * PRE + k:NB * PRE + k + 1],
                                             in1=conv[:, (k - 1) % 2, 0:COMP], op0=ALU.mult, op1=ALU.add) \
                        .then_inc(conv_ready, 1)
                    dve.wait_ge(conv_ready, at + k)
                dve.wait_ge(tail_ready, 2 * (XBC * e + t) + 2)
                dve.sem_inc(raw_free, 1)

            def run(st, items):
                for item, e in items:
                    what = item[0]
                    c = item[1] if len(item) > 1 else None
                    b = bank(st, item) if what != "OQ" else None
                    if what == "AS":
                        dve.wait_ge(acs_hi_ready, e + 1)
                        dve.tensor_tensor(acs_lo[:, :], acs_f[:, :], acs_hi[:, :].bitcast(F32), ALU.subtract) \
                            .then_inc(acs_lo_ready, 1)
                    elif what == "BS":
                        dve.wait_ge(b_rows_ready, 2 * e + 2)
                        dve.wait_ge(consts_in, 16 * SSD_CONSTS)
                        dve.tensor_tensor(b_own[:, :, :], b_rows[0:NS, TT - 1, :].unsqueeze(1).broadcast_to([NS, NB, ST]),
                                          own[:, :].unsqueeze(2).broadcast_to([NS, NB, ST]), ALU.mult) \
                            .then_inc(b_own_ready, 1)
                    elif what in ("BA", "BB"):
                        r = ROWS[c]
                        filled(dve, st, item)
                        dve.wait_ge(consts_in, 16 * SSD_CONSTS)
                        dve.wait_ge(acs_ready, e + 1)
                        for i in range(4):
                            h = i + (4 if what == "BB" else 0)
                            last = dve.scalar_tensor_tensor(
                                out=decay[0:r, c % 2, h, 0:r], in0=b[0:r, i * r:(i + 1) * r],
                                scalar=acs[0:r, c, h:h + 1], in1=(mask if c < TT - 1 else mask_s)[0:r, 0:r],
                                op0=ALU.subtract, op1=ALU.add)
                        if what == "BB":
                            last.then_inc(seg_ready, 1)
                            dve.wait_ge(seg_ready, TT * e + c + 1)
                            if c < TT - 1:
                                dve.wait_ge(chunk_decay_ready, 4 * e + c + 1)
                            free(dve, st, ("BA", c))
                            free(dve, st, ("BB", c))
                            dve.wait_ge(decay_ready, TT * e + c + 1)
                            if c < TT - 1:
                                dve.tensor_copy(to_end[:, c % 2, :], decay[:, c % 2, :, P - 1]) \
                                    .then_inc(to_end_ready, 1)
                            else:
                                dve.tensor_reduce(to_end[0:NS, c % 2, :],
                                                  decay[0:NS, c % 2, :, NT - 1:NS:NT], AX, ALU.add) \
                                    .then_inc(to_end_ready, 1)
                            dve.wait_ge(to_end_ready, TT * e + c + 1)
                            dve.wait_ge(cb_ready, 2 * e + (1 if c < TT - 1 else 2))
                            dve.tensor_tensor(decay[0:r, c % 2, :, 0:r], decay[0:r, c % 2, :, 0:r],
                                              cb[0:r, c, 0:r].unsqueeze(1).broadcast_to([r, HG, r]), ALU.mult) \
                                .then_inc(weights_ready, 1)
                    elif what == "ST":
                        filled(dve, st, item)
                        if c == 0:
                            dve.tensor_copy(state[:, :], b[:, :]).then_inc(state_ready, 1)
                        else:
                            dve.wait_ge(chunk_decay_ready, 4 * e + c + 1)
                            dve.tensor_tensor(heads(state[:, :]), heads(state[:, :]),
                                              per_head(chunk_decay[:, c % 2, :]), ALU.mult).then_inc(state_step, 1)
                            dve.wait_ge(state_step, 3 * e + c)
                            dve.tensor_tensor(state[:, :], state[:, :], b[:, :], ALU.add).then_inc(state_ready, 1)
                        dve.wait_ge(state_ready, 4 * e + c + 1)
                        free(dve, st, item)
                    elif what == "YO":
                        r = ROWS[c]
                        filled(dve, st, item)
                        dve.tensor_tensor(heads(y[0:r, c, :]), heads(b[0:r, :]), per_head(acs_exp[0:r, c, :]),
                                          ALU.mult).then_inc(y_step, 1)
                        dve.wait_ge(y_step, Y_STEPS * e + 2 * c - 1)
                        free(dve, st, item)
                    elif what == "YD":
                        r = ROWS[c]
                        filled(dve, st, item)
                        dve.wait_ge(x_d_ready, TT * e + c + 1)
                        if c:
                            dve.tensor_tensor(y[0:r, c, :], y[0:r, c, :], b[0:r, :], ALU.add).then_inc(y_step, 1)
                            dve.wait_ge(y_step, Y_STEPS * e + 2 * c)
                            free(dve, st, item)
                            dve.tensor_tensor(y[0:r, c, :], y[0:r, c, :], x_d[0:r, c % 2, :], ALU.add) \
                                .then_inc(y_ready, 1)
                        else:
                            dve.tensor_tensor(y[0:r, c, :], b[0:r, :], x_d[0:r, c % 2, :], ALU.add) \
                                .then_inc(y_ready, 1)
                            dve.wait_ge(y_ready, TT * e + 1)
                            free(dve, st, item)
                    elif what == "HT":
                        filled(dve, st, item)
                        if c >= 2:
                            dve.wait_ge(off_done, 8 * e + c - 1)
                        dve.tensor_copy(h0_t[:, c % 2, :], b[:, :]).then_inc(h0_t_ready, 1)
                        dve.wait_ge(h0_t_ready, 8 * e + c + 1)
                        free(dve, st, item)
                    elif what == "HN":
                        j, half = c // 2, c % 2
                        filled(dve, st, item)
                        dve.wait_ge(h0_scaled, 8 * e + c + 1)
                        x = h0[:, j, 4 * half:4 * half + 4, :].rearrange("p n s -> p (n s)")
                        dve.tensor_tensor(x, x, b[:, :], ALU.add).then_inc(h0_new, 1)
                        dve.wait_ge(h0_new, 8 * e + c + 1)
                        free(dve, st, item)
                    elif what == "Z":
                        r = ROWS[c]
                        filled(dve, st, item)
                        dve.wait_ge(y_ready, TT * e + c + 1)
                        dve.tensor_tensor(y[0:r, c, :], y[0:r, c, :], b[0:r, :], ALU.mult).then_inc(gated, 1)
                        dve.wait_ge(gated, TT * e + c + 1)
                        free(dve, st, item)
                        if c == TT - 1:
                            dve.wait_ge(squares, TT * (e + 1))
                            dve.tensor_scalar(stats[:, 1, :], stats[:, 0, :], 1.0 / GW, EPS, ALU.mult, ALU.add) \
                                .then_inc(mean_ready, 1)
                            dve.wait_ge(mean_ready, e + 1)
                            dve.reciprocal(stats[:, 1, :], stats[:, 1, :]).then_inc(inv_ready, 1)

            def stage(st):
                for t in range(-1, GT):
                    if t == 4 and st.head is not None:
                        e = st.head
                        cols = bass.ds(HG * e, HG)
                        dve.wait_ge(x_d_ready, TT * e)
                        dve.wait_ge(acs_f_ready, 2 * e)
                        dve.tensor_copy(dt_e[:, :, :], dt[:, :, cols]).then_inc(slices_ready, 1)
                        dve.tensor_copy(dta_e[:, :, :], dta[:, :, cols]).then_inc(slices_ready, 1)
                        dve.tensor_copy(d_e[:, :], rows[:, 2, cols]).then_inc(slices_ready, 1)
                    if t == 4 and st.tail is not None:
                        e = st.tail
                        dve.wait_ge(rstd_ready, e + 1)
                        dve.wait_ge(norm_in, 16 * (e + 1))
                        for c, r in enumerate(ROWS):
                            dve.scalar_tensor_tensor(out=y[0:r, c, :], in0=y[0:r, c, :], scalar=stats[0:r, 2, c:c + 1],
                                                     in1=norm_row[0:r, :], op0=ALU.mult, op1=ALU.mult).then_inc(normed, 1)
                    run(st, st.part(t, 0))
                    if 0 <= t < XBC and st.head is not None:
                        taps(st.head, t)
                    if st.tail is None and t == 1:
                        soften()
                    run(st, st.rest(t))

            all_groups(dve, SSD, stage)

        @block.gpsimd
        def _(pool):
            def w_low(e, t):
                r = t % PAIR
                pool.wait_ge(whi_ready, GT * e + t + 1)
                pool.tensor_tensor(wlo[:, r], w[:, r], whi[:, r].bitcast(F32), ALU.subtract).then_inc(wlo_ready, 1)

            for t in range(PAIR):
                w_low(0, t)
            pool.wait_ge(setup, 1)
            def run(st, items):
                for item, e in items:
                    if item[0] == "BA":
                        c = item[1]
                        r = ROWS[c]
                        pool.wait_ge(x_rows_ready, TT * e + c + 1)
                        pool.wait_ge(slices_ready, 3 * e + 3)
                        pool.wait_ge(y_ready, TT * e + max(c - 1, 0))
                        pool.tensor_tensor(heads(x_dt[0:r, c % 2, :]), heads(x_rows[0:r, c, :]), per_head(dt_e[0:r, c, :]),
                                           ALU.mult).then_inc(x_dt_ready, 1)
                        pool.tensor_tensor(heads(x_d[0:r, c % 2, :]), heads(x_rows[0:r, c, :]), per_head(d_e[0:r, :]),
                                           ALU.mult).then_inc(x_d_ready, 1)
                    elif item[0] == "BB":
                        c = item[1]
                        r = ROWS[c]
                        pool.wait_ge(x_dt_ready, TT * e + c + 1)
                        pool.wait_ge(to_end_ready, TT * e + c + 1)
                        if c >= 2:
                            pool.wait_ge(state_ready, 4 * e + c - 1)
                        pool.tensor_tensor(heads(x_end[0:r, c % 2, :]), heads(x_dt[0:r, c % 2, :]),
                                           per_head(to_end[0:r, c % 2, :]), ALU.mult).then_inc(x_end_ready, 1)
                    elif item[0] == "HN":
                        c = item[1]
                        j, half = c // 2, c % 2
                        if c == 0:
                            pool.wait_ge(decay_rows_ready, e + 1)
                            pool.wait_ge(h0_t_ready, 8 * e + 8)
                        x = h0[:, j, 4 * half:4 * half + 4, :]
                        pool.tensor_tensor(x, x, decay_rows[:, j, 4 * half:4 * half + 4].unsqueeze(2)
                                           .broadcast_to([P, 4, ST]), ALU.mult).then_inc(h0_scaled, 1)

            def stage(st):
                h = st.head
                for t in range(-1, GT):
                    if 0 <= t < XBC and h is not None:
                        pool.wait_ge(raw_ready, XBC * h + t + 1)
                        if t == 0:
                            pool.wait_ge(par_ready, h + 1)
                        hold(pool)
                        runs = raw[:, PRE + SEQ:WIDE].rearrange("p (n k) -> p n k", n=NB)
                        pool.tensor_copy(runs[:, :, 0:PRE], par[:, t, 0:NB * PRE].rearrange("p (n k) -> p n k", n=NB)) \
                            .then_inc(past_ready, 1)
                    if t >= 0 and h is not None:
                        nxt = t + PAIR
                        w_low(h + nxt // GT, nxt % GT)
                    if 0 <= t < XBC and h is not None:
                        if t == 0:
                            pool.wait_ge(tails_ready, 2 * h)
                            hold(pool)
                        pool.tensor_copy(tails[:, t, 0:PRE], raw[:, SEQ:SEQ + PRE]).then_inc(tail_ready, 1)
                        pool.tensor_copy(tails[:, t, PRE:TAIL].rearrange("p (n k) -> p n k", n=NB), runs[:, :, NT:NT + PRE]) \
                            .then_inc(tail_ready, 1)
                    run(st, st.items(t))

            all_groups(pool, SSD, stage)


def build(nc, x, t, out, scratch):
    y_dram, h_dram, hs_dram = scratch
    pre, post = x["norm_pre"], x["norm_post"]
    ssd_params = (x["ssd_conv_w"], x["ssd_conv_b"], x["ssd_dt_bias"][0], x["ssd_a_log"][0], x["ssd_d"][0], x["ssd_norm_w"])
    source = (x["x_prompt"][0], x["x_sample"].rearrange("n t d -> (n t) d"))
    target = (out["y_prompt"][0], out["y_sample"].rearrange("n t d -> (n t) d"))
    windows = ("w128", "w512", "w2048")
    with nc.sbuf_tensor("ident", [P, P], F32) as ident, \
            nc.sbuf_tensor("uhi", [P, KD, TOK], F32R) as uhi, nc.sbuf_tensor("ulo", [P, KD, TOK], F32R) as ulo:
        with nc.sbuf_tensor("w", [P, PAIR, KD * P], F32) as w, nc.sbuf_tensor("whi", [P, PAIR, KD * P], F32R) as whi, \
                nc.sbuf_tensor("wlo", [P, PAIR, KD * P], F32R) as wlo:
            ring = (w, whi, wlo)
            with nc.cleanup_on_exit():
                with nc.sbuf_tensor("x0", [P, TT, D], F32) as xt:
                    norm_phase(nc, "n0", xt, ident, t["ident"], uhi, ulo, pre[0], source, ring, x["attn_w_in"][0],
                               [attn_columns(r, 0) for r in range(PAIR)])
            with nc.cleanup_on_exit():
                attention_phase(nc, uhi, ulo, ident, ring, x["attn_w_in"][0], t, [x["cache_kv_" + w] for w in windows],
                                y_dram, [out["p_kv_" + w][0] for w in windows], [out["s_kv_" + w] for w in windows])
        with nc.cleanup_on_exit():
            with nc.sbuf_tensor("x1", [P, TT, D], F32) as xt:
                mix_phase(nc, "m1", x["attn_w_out"][0], y_dram, xt, source, ident, post[0], (h_dram, hs_dram),
                          pre[1], uhi, ulo)
        with nc.cleanup_on_exit():
            ssd_phase(nc, uhi, ulo, ident, x["ssd_w_in"][0], t, ssd_params, (x["state_ssm"], x["state_conv"]), y_dram,
                      (out["p_ssm"], out["p_conv"]), (out["s_ssm"], out["s_conv"]))
        with nc.cleanup_on_exit():
            with nc.sbuf_tensor("x2", [P, TT, D], F32) as xt:
                mix_phase(nc, "m2", x["ssd_w_out"][0], y_dram, xt, (h_dram, hs_dram), ident, post[1], target)


def tables():
    half = HD // 2
    inv = (np.float32(10000.0) ** (-np.arange(half, dtype=np.float32) / np.float32(half))).astype(np.float32)
    pos = np.concatenate([np.arange(SEQ), np.tile(PAST + np.arange(NT), NB)]).astype(np.float32)
    angle = (pos[None, :] * inv[:, None]).astype(np.float32)
    cos, sin = np.cos(angle), np.sin(angle)

    def z(ok):
        return np.where(ok, 0.0, BIG).astype(np.float32)

    def ones(ok):
        return ok.astype(np.float32)

    i, j = np.arange(P)[:, None], np.arange(P)[None, :]
    masks = np.stack([z(j >= i), z(j <= i), z((j // 32 == i // 32) & (j % 32 <= i % 32))], 1)
    seq, token = i // 32, i % 4
    cached = np.concatenate([j >= token, (np.arange(2 * P)[None, :] % 4) == token,
                             (np.arange(64)[None, :] // 16) == token], 1)
    new, new_token = np.arange(NS)[None, :] // NT, np.arange(NS)[None, :] % NT
    fresh = [(new == 4 * s + seq) & ((new_token <= token) if w == 0 else (new_token == token))
             for s in range(2) for w in range(NW)]
    tri = i <= j
    si, sj = np.arange(NS)[:, None], np.arange(NS)[None, :]
    tri_s = (si <= sj) & (si // NT == sj // NT)
    head = np.arange(HG)[:, None, None]
    return {
        "ident": np.eye(P, dtype=np.float32),
        "cos": np.concatenate([cos, cos]).astype(np.float32),
        "sin": np.concatenate([sin, -sin]).astype(np.float32),
        "masks": masks,
        "mask_s": z(np.concatenate([cached] + fresh, 1)),
        "tri": ones(tri), "tri_s": ones(tri_s), "mask": z(tri), "mask_ss": z(tri_s),
        "own": ones(si // NT == np.arange(NB)[None, :]),
        "pick": ones(np.broadcast_to(head == np.arange(HG)[None, :, None], (HG, HG, P))).reshape(HG, HG * P),
        "spread": ones(head == 2 * np.arange(4)[None, :, None] + np.arange(P)[None, None, :] // PD),
    }


_INS = ["x_prompt", "x_sample", "cache_kv_w128", "cache_kv_w512", "cache_kv_w2048", "state_ssm", "state_conv",
        "norm_pre", "norm_post", "attn_w_in", "attn_w_out", "ssd_w_in", "ssd_conv_w", "ssd_conv_b", "ssd_dt_bias",
        "ssd_a_log", "ssd_d", "ssd_norm_w", "ssd_w_out"]
_OUTS = {
    "y_prompt": (1, SEQ, D), "y_sample": (NB, NT, D),
    "p_kv_w128": (1, 1, 128, 2, NG, HD), "p_kv_w512": (1, 1, SEQ, 2, NG, HD), "p_kv_w2048": (1, 1, SEQ, 2, NG, HD),
    "p_ssm": (1, 1, NG * HG, PD, ST), "p_conv": (1, 1, PRE, INNER + 2 * NG * ST),
    "s_kv_w128": (1, NB, 128, 2, NG, HD), "s_kv_w512": (1, NB, PAST + NT, 2, NG, HD),
    "s_kv_w2048": (1, NB, PAST + NT, 2, NG, HD),
    "s_ssm": (1, NB, NG * HG, PD, ST), "s_conv": (1, NB, PRE, INNER + 2 * NG * ST),
}


def kernel(**inputs):
    import concourse.bacc as bacc
    from concourse.bass_utils import run_bass_kernel_spmd

    nc = bacc.Bacc("TRN2", target_bir_lowering=False, num_devices=1)
    arrays = {}

    def given(name, a):
        arrays[f"in_{name}_dram"] = a
        return nc.dram_tensor(f"in_{name}_dram", a.shape, F32, kind="ExternalInput").ap()

    x = {n: given(n, np.ascontiguousarray(inputs[n])) for n in _INS}
    t = {n: given(n, a) for n, a in tables().items()}
    out = {n: nc.dram_tensor(f"out_{n}_dram", shape, F32, kind="ExternalOutput").ap() for n, shape in _OUTS.items()}
    scratch = [nc.dram_tensor(n, shape, F32, kind="Internal").ap()
               for n, shape in (("mixed", (KI, P, TOK)), ("h_prompt", (SEQ, D)), ("h_sample", (NS, D)))]
    build(nc, x, t, out, scratch)
    r = run_bass_kernel_spmd(nc, [arrays], core_ids=[0])
    return tuple(r.results[0][f"out_{n}_dram"] for n in _OUTS)
```
